# Optimizing a Trainium2 kernel written in Bass

```python
import math
import jax
import jax.numpy as jnp
from jax import lax
import numpy as np
import jax, jax.numpy as jnp

D_MODEL = 1024
BATCH = 1
SEQ = 512
DEPTH = 1

HEAD_DIM = 64
MIX_WIDTH = D_MODEL
A_WIDTH = MIX_WIDTH // 2
B_WIDTH = MIX_WIDTH - A_WIDTH
A_HEADS = A_WIDTH // HEAD_DIM
B_HEADS = B_WIDTH // (2 * HEAD_DIM)
DIL_PATTERNS = ((128, 1), (512, 4), (2048, 16))
BAND_BLOCK = 128
Q_BLOCK = 128
N_EXPERTS = 32
TOP_K = 4
D_FF = D_MODEL
SWIGLU_LIMIT = 7.0
SWIGLU_ALPHA = 1.702
MOE_BLOCK = 128
RMS_EPS = 1e-6
ATTN_SCALE = HEAD_DIM ** -0.5
IN_SIZES = (A_WIDTH, A_WIDTH, A_WIDTH, B_WIDTH, B_WIDTH, B_WIDTH)
IN_WIDTH = sum(IN_SIZES)
IN_SPLITS = tuple(int(v) for v in np.cumsum(IN_SIZES)[:-1])


def rms_norm(x, g):
    xf = x.astype(jnp.float32)
    y = xf * lax.rsqrt(jnp.mean(xf * xf, axis=-1, keepdims=True) + RMS_EPS)
    return (y * g.astype(jnp.float32)).astype(x.dtype)

def alibi_slopes(n):
    return 2.0 ** (-8.0 * jnp.arange(1, n + 1, dtype=jnp.float32) / n)

def dilated_band_attention(q, k, v, slopes, window, dil):
    bsz, nh, n_tok, hd = q.shape
    L = n_tok // dil
    w_sub = window // dil
    nb = -(-L // BAND_BLOCK)
    Lp = nb * BAND_BLOCK

    def to_sub(t):
        t = jnp.swapaxes(t.reshape(bsz, nh, L, dil, hd), 2, 3)
        return jnp.pad(t, ((0, 0), (0, 0), (0, 0), (0, Lp - L), (0, 0)))

    def key_band(t):
        t = jnp.pad(to_sub(t), ((0, 0), (0, 0), (0, 0), (BAND_BLOCK, 0), (0, 0)))
        t = t.reshape(bsz, nh, dil, nb + 1, BAND_BLOCK, hd)
        return jnp.concatenate([t[:, :, :, :-1], t[:, :, :, 1:]], axis=4)

    qs = to_sub(q).reshape(bsz, nh, dil, nb, BAND_BLOCK, hd)
    ks, vs = key_band(k), key_band(v)
    iq = jnp.arange(BAND_BLOCK)[:, None]
    ik = jnp.arange(2 * BAND_BLOCK)[None, :]
    delta = iq - ik + BAND_BLOCK
    k_sub = (jnp.arange(nb)[:, None] * BAND_BLOCK - BAND_BLOCK
             + jnp.arange(2 * BAND_BLOCK)[None, :])
    valid = ((delta >= 0) & (delta <= w_sub))[None] & (k_sub >= 0)[:, None, :]
    bias = -slopes[:, None, None] * (delta * dil).astype(jnp.float32)[None]
    s = jnp.einsum('bhrnqd,bhrnkd->bhrnqk', qs, ks).astype(jnp.float32) * ATTN_SCALE
    s = s + bias[None, :, None, None]
    s = jnp.where(valid[None, None, None], s, -jnp.inf)
    m = jnp.max(s, axis=-1, keepdims=True)
    e = jnp.exp(s - m)
    den = jnp.sum(e, axis=-1, keepdims=True)
    o = jnp.einsum('bhrnqk,bhrnkd->bhrnqd', (e / den).astype(v.dtype), vs)
    lse = (m + jnp.log(den))[..., 0]

    def from_sub(t):
        tail = t.shape[5:]
        t = t.reshape((bsz, nh, dil, Lp) + tail)[:, :, :, :L]
        t = jnp.swapaxes(t, 2, 3)
        return t.reshape((bsz, nh, n_tok) + tail)

    return from_sub(o), from_sub(lse)

def dilated_mixture_attention(q, k, v, slopes):
    outs, lses = [], []
    for window, dil in DIL_PATTERNS:
        o, lse = dilated_band_attention(q, k, v, slopes, window, dil)
        outs.append(o)
        lses.append(lse)
    w = jax.nn.softmax(jnp.stack(lses, axis=0), axis=0)
    return jnp.einsum('pbhs,pbhsd->bhsd', w.astype(q.dtype), jnp.stack(outs, axis=0))

def differential_attention(q, k, v, slopes, lam):
    bsz, nh, n_tok, _, hd = q.shape
    nqb = n_tok // Q_BLOCK
    qb = jnp.moveaxis(q.reshape(bsz, nh, nqb, Q_BLOCK, 2, hd), 2, 0)
    k_pos = jnp.arange(n_tok)

    def block(args):
        q_blk, start = args
        dist = (start + jnp.arange(Q_BLOCK))[:, None] - k_pos[None, :]
        sc = jnp.einsum('bhqcd,bhkcd->bhcqk', q_blk, k).astype(jnp.float32) * ATTN_SCALE
        sc = sc - slopes[None, :, None, None, None] * dist.astype(jnp.float32)
        sc = jnp.where(dist >= 0, sc, -jnp.inf)
        p = jax.nn.softmax(sc, axis=-1)
        a = p[:, :, 0] - lam * p[:, :, 1]
        return jnp.einsum('bhqk,bhkd->bhqd', a.astype(v.dtype), v)

    o = lax.map(block, (qb, jnp.arange(nqb) * Q_BLOCK))
    return jnp.moveaxis(o, 0, 2).reshape(bsz, nh, n_tok, 2 * hd)

def moe_ffn(h, w_router, b_router, w_gate_up, b_gate_up, w_down, b_down):
    n, d = h.shape
    logits = (h @ w_router).astype(jnp.float32) + b_router.astype(jnp.float32)
    top_val, top_idx = lax.top_k(logits, TOP_K)
    gates = jax.nn.softmax(top_val, axis=-1)
    n_assign = n * TOP_K
    flat_e = top_idx.reshape(-1)
    order = jnp.argsort(flat_e)
    e_sorted = flat_e[order]
    tok_sorted = order // TOP_K
    gate_sorted = gates.reshape(-1)[order]
    counts = jnp.zeros((N_EXPERTS,), jnp.int32).at[flat_e].add(1)
    padded = (counts + MOE_BLOCK - 1) // MOE_BLOCK * MOE_BLOCK
    pad_end = jnp.cumsum(padded)
    pad_start = pad_end - padded
    grp_start = jnp.cumsum(counts) - counts
    dest = pad_start[e_sorted] + jnp.arange(n_assign) - grp_start[e_sorted]
    n_blocks = -(-(n_assign + N_EXPERTS * (MOE_BLOCK - 1)) // MOE_BLOCK)
    buf_tok = jnp.zeros((n_blocks * MOE_BLOCK,), jnp.int32).at[dest].set(tok_sorted)
    block_e = jnp.minimum(jnp.searchsorted(pad_end, jnp.arange(n_blocks) * MOE_BLOCK, side='right'),
                          N_EXPERTS - 1)
    xb = h[buf_tok].reshape(n_blocks, MOE_BLOCK, d)

    def expert_block(args):
        xe, e = args
        gu = xe @ w_gate_up[e] + b_gate_up[e]
        g = jnp.minimum(gu[:, :D_FF], SWIGLU_LIMIT)
        u = jnp.clip(gu[:, D_FF:], -SWIGLU_LIMIT, SWIGLU_LIMIT)
        act = (u + 1.0) * (g * jax.nn.sigmoid(SWIGLU_ALPHA * g))
        return act @ w_down[e] + b_down[e]

    yb = lax.map(expert_block, (xb, block_e)).reshape(-1, d)
    y = yb[dest] * gate_sorted[:, None].astype(yb.dtype)
    return jax.ops.segment_sum(y, tok_sorted, num_segments=n)

def hybrid_layer(x, c, w_ada, b_ada, norm1_g, w_in, a_q_norm_g, a_k_norm_g, b_q_norm_g,
                 b_k_norm_g, lambda_q1, lambda_k1, lambda_q2, lambda_k2, diff_norm_g, w_out,
                 norm2_g, w_router, b_router, w_gate_up, b_gate_up, w_down, b_down, lambda_init):
    bsz, n_tok, d = x.shape
    mod = jax.nn.silu(c) @ w_ada + b_ada
    shift1, scale1, gate1, shift2, scale2, gate2 = jnp.split(mod[:, None, :], 6, axis=-1)

    h = rms_norm(x, norm1_g) * (1.0 + scale1) + shift1
    proj = h @ w_in
    aq, ak, av, bq, bk, bv = jnp.split(proj, IN_SPLITS, axis=-1)

    def heads_a(t):
        return jnp.swapaxes(t.reshape(bsz, n_tok, A_HEADS, HEAD_DIM), 1, 2)

    aq = rms_norm(heads_a(aq), a_q_norm_g)
    ak = rms_norm(heads_a(ak), a_k_norm_g)
    o_a = dilated_mixture_attention(aq, ak, heads_a(av), alibi_slopes(A_HEADS))
    o_a = jnp.swapaxes(o_a, 1, 2).reshape(bsz, n_tok, A_WIDTH)

    def heads_b(t):
        return jnp.swapaxes(t.reshape(bsz, n_tok, B_HEADS, 2, HEAD_DIM), 1, 2)

    bq = rms_norm(heads_b(bq), b_q_norm_g)
    bk = rms_norm(heads_b(bk), b_k_norm_g)
    bv = jnp.swapaxes(bv.reshape(bsz, n_tok, B_HEADS, 2 * HEAD_DIM), 1, 2)
    lam = (jnp.exp(jnp.sum(lambda_q1.astype(jnp.float32) * lambda_k1.astype(jnp.float32)))
           - jnp.exp(jnp.sum(lambda_q2.astype(jnp.float32) * lambda_k2.astype(jnp.float32)))
           + lambda_init)
    o_b = differential_attention(bq, bk, bv, alibi_slopes(B_HEADS), lam)
    o_b = rms_norm(o_b, diff_norm_g) * (1.0 - lambda_init)
    o_b = jnp.swapaxes(o_b, 1, 2).reshape(bsz, n_tok, B_WIDTH)

    mixed = jnp.concatenate([o_a, o_b], axis=-1) @ w_out
    x = x + gate1 * mixed

    h2 = rms_norm(x, norm2_g) * (1.0 + scale2) + shift2
    y = moe_ffn(h2.reshape(bsz * n_tok, d), w_router, b_router, w_gate_up, b_gate_up,
                w_down, b_down).reshape(bsz, n_tok, d)
    return x + gate2 * y

def first_inputs(seed: int = 0) -> dict:
    key = jax.random.key(seed)
    ks = jax.random.split(key, 24)

    def nrm(k, shape, scale):
        return jax.random.normal(k, shape, jnp.float32) * scale

    def gain(k, shape):
        return 1.0 + nrm(k, shape, 0.05)

    L = DEPTH
    return {
        'x': nrm(ks[0], (BATCH, SEQ, D_MODEL), 1.0),
        'c': nrm(ks[1], (BATCH, D_MODEL), 1.0),
        'w_ada': nrm(ks[2], (L, D_MODEL, 6 * D_MODEL), 0.5 * D_MODEL ** -0.5),
        'b_ada': nrm(ks[3], (L, 6 * D_MODEL), 0.02),
        'norm1_g': gain(ks[4], (L, D_MODEL)),
        'w_in': nrm(ks[5], (L, D_MODEL, IN_WIDTH), D_MODEL ** -0.5),
        'a_q_norm_g': gain(ks[6], (L, HEAD_DIM)),
        'a_k_norm_g': gain(ks[7], (L, HEAD_DIM)),
        'b_q_norm_g': gain(ks[8], (L, HEAD_DIM)),
        'b_k_norm_g': gain(ks[9], (L, HEAD_DIM)),
        'lambda_q1': nrm(ks[10], (L, HEAD_DIM), 0.1),
        'lambda_k1': nrm(ks[11], (L, HEAD_DIM), 0.1),
        'lambda_q2': nrm(ks[12], (L, HEAD_DIM), 0.1),
        'lambda_k2': nrm(ks[13], (L, HEAD_DIM), 0.1),
        'diff_norm_g': gain(ks[14], (L, 2 * HEAD_DIM)),
        'w_out': nrm(ks[15], (L, MIX_WIDTH, D_MODEL), MIX_WIDTH ** -0.5),
        'norm2_g': gain(ks[16], (L, D_MODEL)),
        'w_router': nrm(ks[17], (L, D_MODEL, N_EXPERTS), D_MODEL ** -0.5),
        'b_router': nrm(ks[18], (L, N_EXPERTS), 0.01),
        'w_gate_up': nrm(ks[19], (L, N_EXPERTS, D_MODEL, 2 * D_FF), D_MODEL ** -0.5),
        'b_gate_up': nrm(ks[20], (L, N_EXPERTS, 2 * D_FF), 0.01),
        'w_down': nrm(ks[21], (L, N_EXPERTS, D_FF, D_MODEL), D_FF ** -0.5),
        'b_down': nrm(ks[22], (L, N_EXPERTS, D_MODEL), 0.01),
    }

def first_block(x, c, w_ada, b_ada, norm1_g, w_in, a_q_norm_g, a_k_norm_g, b_q_norm_g, b_k_norm_g,
              lambda_q1, lambda_k1, lambda_q2, lambda_k2, diff_norm_g, w_out, norm2_g, w_router,
              b_router, w_gate_up, b_gate_up, w_down, b_down):
    for l in range(DEPTH):
        lambda_init = 0.8 - 0.6 * math.exp(-0.3 * l)
        x = hybrid_layer(x, c, w_ada[l], b_ada[l], norm1_g[l], w_in[l], a_q_norm_g[l],
                         a_k_norm_g[l], b_q_norm_g[l], b_k_norm_g[l], lambda_q1[l], lambda_k1[l],
                         lambda_q2[l], lambda_k2[l], diff_norm_g[l], w_out[l], norm2_g[l],
                         w_router[l], b_router[l], w_gate_up[l], b_gate_up[l], w_down[l],
                         b_down[l], lambda_init)
    return x


CHUNK = 64
EPS = 1e-6

SSM_WIDTH = 512
SSM_GROUP = 16
SSM_GROUPS = SSM_WIDTH // SSM_GROUP
SSM_STATE = 64
DT_MIN = 1e-3
DT_MAX = 1e-1

ATT_HEADS = 8
HEAD_DIM_2 = 128
ATT_WIDTH = ATT_HEADS * HEAD_DIM_2

N_BRANCHES = 2
IN_SPLITS_2 = (
    SSM_WIDTH,
    SSM_WIDTH + ATT_WIDTH,
    SSM_WIDTH + 2 * ATT_WIDTH,
    SSM_WIDTH + 3 * ATT_WIDTH,
    SSM_WIDTH + 3 * ATT_WIDTH + ATT_HEADS,
    SSM_WIDTH + 3 * ATT_WIDTH + ATT_HEADS + D_MODEL,
)
IN_COLS = SSM_WIDTH + 3 * ATT_WIDTH + ATT_HEADS + N_BRANCHES * D_MODEL

PEER_HEADS = 8
PEER_KEYS = 128
PEER_EXPERTS = PEER_KEYS * PEER_KEYS
PEER_QUERY = 256
PEER_HALF = PEER_QUERY // 2
PEER_TOPK = 16
TOKEN_BLOCK = 128


def rms_norm_2(x, g):
    x32 = x.astype(jnp.float32)
    y = x32 * lax.rsqrt(jnp.mean(x32 * x32, axis=-1, keepdims=True) + EPS)
    return (y * g.astype(jnp.float32)).astype(x.dtype)

def _complex_affine_combine(earlier, later):
    ar1, ai1, br1, bi1 = earlier
    ar2, ai2, br2, bi2 = later
    return (ar2 * ar1 - ai2 * ai1,
            ar2 * ai1 + ai2 * ar1,
            ar2 * br1 - ai2 * bi1 + br2,
            ar2 * bi1 + ai2 * br1 + bi2)

def s5_branch(u, a_re, a_im, log_step, b_re, b_im, c_re, c_im, d_skip, w_glu):
    bsz, seq = u.shape[0], u.shape[1]
    f32 = jnp.float32
    u32 = u.astype(f32)
    ug = u32.reshape(bsz, seq, SSM_GROUPS, SSM_GROUP)
    step = jnp.exp(log_step.astype(f32))[:, None]
    ar = a_re.astype(f32)
    ai = a_im.astype(f32)
    mag = jnp.exp(ar * step)
    lam_re = mag * jnp.cos(ai * step)
    lam_im = mag * jnp.sin(ai * step)
    nr = lam_re - 1.0
    ni = lam_im
    den = ar * ar + ai * ai
    coef_re = (nr * ar + ni * ai) / den
    coef_im = (ni * ar - nr * ai) / den
    br = coef_re[..., None] * b_re.astype(f32) - coef_im[..., None] * b_im.astype(f32)
    bi = coef_re[..., None] * b_im.astype(f32) + coef_im[..., None] * b_re.astype(f32)
    xr = jnp.einsum('blgh,gph->blgp', ug, br)
    xi = jnp.einsum('blgh,gph->blgp', ug, bi)
    lr = jnp.broadcast_to(lam_re[None, None], (1, seq, SSM_GROUPS, SSM_STATE))
    li = jnp.broadcast_to(lam_im[None, None], (1, seq, SSM_GROUPS, SSM_STATE))
    _, _, sr, si = lax.associative_scan(_complex_affine_combine, (lr, li, xr, xi), axis=1)
    y = (jnp.einsum('blgp,ghp->blgh', sr, c_re.astype(f32))
         - jnp.einsum('blgp,ghp->blgh', si, c_im.astype(f32)))
    y = y.reshape(bsz, seq, SSM_WIDTH) + d_skip.astype(f32) * u32
    y = jax.nn.gelu(y).astype(u.dtype)
    z = y @ w_glu
    val, gate = jnp.split(z, 2, axis=-1)
    return val * jax.nn.sigmoid(gate)

def head_rms_norm(x, g):
    x32 = x.astype(jnp.float32)
    y = x32 * lax.rsqrt(jnp.mean(x32 * x32, axis=-1, keepdims=True) + EPS)
    return (y * g.astype(jnp.float32)).astype(x.dtype)

def forgetting_attention(q, k, v, f_logit, f_bias, q_g, k_g):
    bsz, seq = q.shape[0], q.shape[1]
    q = head_rms_norm(q.reshape(bsz, seq, ATT_HEADS, HEAD_DIM_2), q_g).transpose(0, 2, 1, 3)
    k = head_rms_norm(k.reshape(bsz, seq, ATT_HEADS, HEAD_DIM_2), k_g).transpose(0, 2, 1, 3)
    v = v.reshape(bsz, seq, ATT_HEADS, HEAD_DIM_2).transpose(0, 2, 1, 3)
    log_f = jax.nn.log_sigmoid((f_logit + f_bias).astype(jnp.float32)).transpose(0, 2, 1)
    cum = jnp.cumsum(log_f, axis=-1)
    n_blk = seq // Q_BLOCK
    q_blocks = q.reshape(bsz, ATT_HEADS, n_blk, Q_BLOCK, HEAD_DIM_2).transpose(2, 0, 1, 3, 4)
    c_blocks = cum.reshape(bsz, ATT_HEADS, n_blk, Q_BLOCK).transpose(2, 0, 1, 3)
    key_pos = jnp.arange(seq)
    scale = HEAD_DIM_2 ** -0.5

    def one_block(args):
        blk, q_blk, c_blk = args
        s = jnp.einsum('bhqd,bhkd->bhqk', q_blk, k).astype(jnp.float32) * scale
        s = s + c_blk[..., None] - cum[:, :, None, :]
        q_pos = blk * Q_BLOCK + jnp.arange(Q_BLOCK)
        s = jnp.where(key_pos[None, :] <= q_pos[:, None], s, -jnp.inf)
        p = jax.nn.softmax(s, axis=-1)
        return jnp.einsum('bhqk,bhkd->bhqd', p.astype(v.dtype), v)

    o = lax.map(one_block, (jnp.arange(n_blk), q_blocks, c_blocks))
    return o.transpose(1, 0, 3, 2, 4).reshape(bsz, seq, ATT_WIDTH)

def peer_ffn(h, w_query, sub_keys, u_tab, v_tab):
    bsz, seq, d = h.shape
    q = (h @ w_query).reshape(bsz, seq, PEER_HEADS, 2, PEER_HALF).astype(jnp.float32)
    scores = jnp.einsum('blhcd,hckd->blhck', q, sub_keys.astype(jnp.float32))
    s_top, i_top = lax.top_k(scores, PEER_TOPK)
    cand_s = (s_top[..., 0, :, None] + s_top[..., 1, None, :]).reshape(bsz, seq, PEER_HEADS, PEER_TOPK * PEER_TOPK)
    cand_i = (i_top[..., 0, :, None] * PEER_KEYS + i_top[..., 1, None, :]).reshape(bsz, seq, PEER_HEADS, PEER_TOPK * PEER_TOPK)
    best_s, pos = lax.top_k(cand_s, PEER_TOPK)
    expert_idx = jnp.take_along_axis(cand_i, pos, axis=-1)
    gates = jax.nn.softmax(best_s, axis=-1)
    n_tok = bsz * seq
    n_tb = n_tok // TOKEN_BLOCK
    h_blocks = h.reshape(n_tb, TOKEN_BLOCK, d)
    i_blocks = expert_idx.reshape(n_tb, TOKEN_BLOCK, PEER_HEADS, PEER_TOPK)
    g_blocks = gates.reshape(n_tb, TOKEN_BLOCK, PEER_HEADS, PEER_TOPK)

    def one_block(args):
        h_blk, i_blk, g_blk = args
        u_sel = u_tab[i_blk]
        act = jax.nn.gelu(jnp.einsum('td,thkd->thk', h_blk, u_sel).astype(jnp.float32))
        w = (g_blk * act).astype(h.dtype)
        return jnp.einsum('thk,thkd->td', w, v_tab[i_blk])

    out = lax.map(one_block, (h_blocks, i_blocks, g_blocks))
    return out.reshape(bsz, seq, d)

def second_inputs(seed: int = 0) -> dict:
    key = jax.random.key(seed)
    ks = jax.random.split(key, 21)
    f32 = jnp.float32
    nrm = lambda k, shape: jax.random.normal(k, shape, dtype=f32)
    x = nrm(ks[0], (BATCH, SEQ, D_MODEL))
    mix_norm_g = 1.0 + 0.02 * nrm(ks[1], (DEPTH, D_MODEL))
    w_in = nrm(ks[2], (DEPTH, D_MODEL, IN_COLS)) * D_MODEL ** -0.5
    ssm_a_re = -0.5 + 0.01 * nrm(ks[3], (DEPTH, SSM_GROUPS, SSM_STATE))
    ssm_a_im = math.pi * jnp.arange(SSM_STATE, dtype=f32) + 0.01 * nrm(ks[4], (DEPTH, SSM_GROUPS, SSM_STATE))
    ssm_log_step = jax.random.uniform(ks[5], (DEPTH, SSM_GROUPS), dtype=f32, minval=math.log(DT_MIN), maxval=math.log(DT_MAX))
    ssm_b_re = nrm(ks[6], (DEPTH, SSM_GROUPS, SSM_STATE, SSM_GROUP)) * (2.0 * SSM_GROUP) ** -0.5
    ssm_b_im = nrm(ks[7], (DEPTH, SSM_GROUPS, SSM_STATE, SSM_GROUP)) * (2.0 * SSM_GROUP) ** -0.5
    ssm_c_re = nrm(ks[8], (DEPTH, SSM_GROUPS, SSM_GROUP, SSM_STATE)) * (2.0 * SSM_STATE) ** -0.5
    ssm_c_im = nrm(ks[9], (DEPTH, SSM_GROUPS, SSM_GROUP, SSM_STATE)) * (2.0 * SSM_STATE) ** -0.5
    ssm_d = nrm(ks[10], (DEPTH, SSM_WIDTH))
    ssm_w_glu = nrm(ks[11], (DEPTH, SSM_WIDTH, 2 * D_MODEL)) * SSM_WIDTH ** -0.5
    fox_forget_bias = 2.0 + 0.5 * nrm(ks[12], (DEPTH, ATT_HEADS))
    q_norm_g = 1.0 + 0.02 * nrm(ks[13], (DEPTH, HEAD_DIM_2))
    k_norm_g = 1.0 + 0.02 * nrm(ks[14], (DEPTH, HEAD_DIM_2))
    w_out = nrm(ks[15], (DEPTH, D_MODEL, D_MODEL)) * D_MODEL ** -0.5
    ffn_norm_g = 1.0 + 0.02 * nrm(ks[16], (DEPTH, D_MODEL))
    peer_w_query = nrm(ks[17], (DEPTH, D_MODEL, PEER_HEADS * PEER_QUERY)) * D_MODEL ** -0.5
    peer_sub_keys = nrm(ks[18], (DEPTH, PEER_HEADS, 2, PEER_KEYS, PEER_HALF)) * PEER_HALF ** -0.5
    peer_u = nrm(ks[19], (DEPTH, PEER_EXPERTS, D_MODEL)) * D_MODEL ** -0.5
    peer_v = nrm(ks[20], (DEPTH, PEER_EXPERTS, D_MODEL)) * 0.1
    return {"x": x, "mix_norm_g": mix_norm_g, "w_in": w_in,
            "ssm_a_re": ssm_a_re, "ssm_a_im": ssm_a_im, "ssm_log_step": ssm_log_step,
            "ssm_b_re": ssm_b_re, "ssm_b_im": ssm_b_im, "ssm_c_re": ssm_c_re, "ssm_c_im": ssm_c_im,
            "ssm_d": ssm_d, "ssm_w_glu": ssm_w_glu, "fox_forget_bias": fox_forget_bias,
            "q_norm_g": q_norm_g, "k_norm_g": k_norm_g, "w_out": w_out, "ffn_norm_g": ffn_norm_g,
            "peer_w_query": peer_w_query, "peer_sub_keys": peer_sub_keys,
            "peer_u": peer_u, "peer_v": peer_v}

def second_block(x, mix_norm_g, w_in, ssm_a_re, ssm_a_im, ssm_log_step, ssm_b_re, ssm_b_im,
              ssm_c_re, ssm_c_im, ssm_d, ssm_w_glu, fox_forget_bias, q_norm_g, k_norm_g,
              w_out, ffn_norm_g, peer_w_query, peer_sub_keys, peer_u, peer_v):
    for layer in range(DEPTH):
        h = rms_norm_2(x, mix_norm_g[layer])
        proj = h @ w_in[layer]
        u, q, k, v, f_logit, g_ssm, g_att = jnp.split(proj, IN_SPLITS_2, axis=-1)
        y_ssm = s5_branch(u, ssm_a_re[layer], ssm_a_im[layer], ssm_log_step[layer],
                          ssm_b_re[layer], ssm_b_im[layer], ssm_c_re[layer], ssm_c_im[layer],
                          ssm_d[layer], ssm_w_glu[layer])
        y_att = forgetting_attention(q, k, v, f_logit, fox_forget_bias[layer],
                                     q_norm_g[layer], k_norm_g[layer])
        merged = jax.nn.sigmoid(g_ssm) * y_ssm + jax.nn.sigmoid(g_att) * y_att
        x = x + (merged @ w_out[layer]).astype(x.dtype)
        h2 = rms_norm_2(x, ffn_norm_g[layer])
        x = x + peer_ffn(h2, peer_w_query[layer], peer_sub_keys[layer],
                         peer_u[layer], peer_v[layer]).astype(x.dtype)
    return x


def setup_inputs(seed=0):
    out = dict(first_inputs(seed))
    for name, value in second_inputs(seed + 1).items():
        if name != "x":
            out[name + "_2"] = value
    return out


def reference(
    x, c, w_ada, b_ada, norm1_g, w_in, a_q_norm_g, a_k_norm_g, b_q_norm_g, b_k_norm_g,
    lambda_q1, lambda_k1, lambda_q2, lambda_k2, diff_norm_g, w_out, norm2_g, w_router, b_router,
    w_gate_up, b_gate_up, w_down, b_down, mix_norm_g_2, w_in_2, ssm_a_re_2, ssm_a_im_2,
    ssm_log_step_2, ssm_b_re_2, ssm_b_im_2, ssm_c_re_2, ssm_c_im_2, ssm_d_2, ssm_w_glu_2,
    fox_forget_bias_2, q_norm_g_2, k_norm_g_2, w_out_2, ffn_norm_g_2, peer_w_query_2,
    peer_sub_keys_2, peer_u_2, peer_v_2,
):
    x = first_block(
        x, c, w_ada, b_ada, norm1_g, w_in, a_q_norm_g, a_k_norm_g, b_q_norm_g, b_k_norm_g,
        lambda_q1, lambda_k1, lambda_q2, lambda_k2, diff_norm_g, w_out, norm2_g, w_router,
        b_router, w_gate_up, b_gate_up, w_down, b_down,
    )
    return second_block(
        x, mix_norm_g_2, w_in_2, ssm_a_re_2, ssm_a_im_2, ssm_log_step_2, ssm_b_re_2, ssm_b_im_2,
        ssm_c_re_2, ssm_c_im_2, ssm_d_2, ssm_w_glu_2, fox_forget_bias_2, q_norm_g_2, k_norm_g_2,
        w_out_2, ffn_norm_g_2, peer_w_query_2, peer_sub_keys_2, peer_u_2, peer_v_2,
    )


_drawn_inputs = setup_inputs


def setup_inputs(seed=0):
    import zlib

    import numpy as np

    out = dict(_drawn_inputs(seed))
    spreads = {}
    factors = {'norm1_g': 2.876,
     'a_q_norm_g': 8.0,
     'a_k_norm_g': 8.0,
     'b_q_norm_g': 5.492,
     'b_k_norm_g': 4.921,
     'lambda_q1': 8.0,
     'lambda_q2': 3.049,
     'diff_norm_g': 4.054,
     'b_router': 4.961,
     'b_gate_up': 8.0,
     'b_down': 8.0,
     'mix_norm_g_2': 6.57,
     'ssm_a_re_2': 64.0,
     'ssm_a_im_2': 37.848,
     'ssm_log_step_2': 38.888,
     'ssm_b_re_2': 51.016,
     'ssm_b_im_2': 50.744,
     'ssm_c_re_2': 49.728,
     'ssm_c_im_2': 51.296,
     'q_norm_g_2': 8.0,
     'k_norm_g_2': 8.0,
     'ffn_norm_g_2': 25.499}
    for name, (base, spread) in spreads.items():
        noise = np.random.default_rng([zlib.crc32(name.encode()), seed]).standard_normal(out[name].shape)
        drawn = base * np.exp(spread * noise) if base else spread * noise
        out[name] = jnp.asarray(drawn.astype(out[name].dtype))
    for name, factor in factors.items():
        out[name] = (out[name] * factor).astype(out[name].dtype)
    return out
```

```python
import math
from contextlib import ExitStack

import numpy as np

import concourse.bass as bass
from concourse import mybir

F32 = mybir.dt.float32
BF16 = mybir.dt.bfloat16
I32 = mybir.dt.int32
U32 = mybir.dt.uint32
ALU = mybir.AluOpType
ACT = mybir.ActivationFunctionType
AX = mybir.AxisListType
ds = bass.ds

P = 128
SEQ = 512
TT = SEQ // P
D = 1024
KT = D // P
CH = 512
EPS = 1e-6
MASKED = -1.0e30
HD = 64
LAMBDA_INIT = 0.8 - 0.6 * math.exp(-0.3 * 0)
NE, TOPK = 32, 4
DFF = 1024
NBLK = -(-(SEQ * TOPK + NE * (P - 1)) // P)
SWIGLU_LIMIT, SWIGLU_ALPHA = 7.0, 1.702
SSM_W, SSM_G, SSM_H, SSM_N = 512, 32, 16, 64
ST = SSM_G * SSM_N // P
FH, FHD = 8, 128
PH, PK, PT16 = 8, 128, 16
SEL = PH * PT16
GROUP = 4


class Steps:

    def __init__(self, sem):
        self.sem, self.n, self.i, self.per = sem, 0, None, 0

    def on(self, eng):
        self.eng = eng
        return self

    def __call__(self, ins):
        ins.then_inc(self.sem, 1)
        self.n += 1
        at = self.n if self.i is None else self.base + self.i * self.per + (self.n - self.base)
        wait(self.eng, self.sem, at)

    def loop(self, i, per):
        self.i, self.per, self.base = i, per, self.n

    def end(self, count):
        assert self.n - self.base == self.per, f"the body has {self.n - self.base} steps, not {self.per}"
        self.n, self.i = self.base + self.per * count, None


def wait(eng, sem, value):
    eng.wait_ge(sem, value)


def build_program(nc, t, out):
    with ExitStack() as ctx:
        emit(nc, t, out, ctx)


def emit(nc, t, out, ctx):
    era = []

    def sem(name):
        stack = ctx.enter_context(ExitStack())
        s = stack.enter_context(nc.semaphore(name))
        era.append((stack, s))
        return s

    def clear_semaphores():
        with nc.Block() as block:
            @block.gpsimd
            def _(pool):
                for _, s in era:
                    pool.sem_clear(s)
        for stack, _ in era:
            stack.close()
        era.clear()

    def sb(stack, name, shape, dt=F32):
        return stack.enter_context(nc.sbuf_tensor(name, shape, dt))

    ps = ctx.enter_context(nc.psum_tensor("ps", [P, 8, CH], F32))
    dve_steps, act_steps, pool_steps = Steps(sem("dve_steps")), Steps(sem("act_steps")), Steps(sem("pool_steps"))
    era.clear()
    x_sb = sb(ctx, "x_sb", [P, TT, D])
    ident = sb(ctx, "ident", [P, P])
    ones = sb(ctx, "ones", [P, P])
    tri_before = sb(ctx, "tri_before", [P, P])
    tri_upto = sb(ctx, "tri_upto", [P, P])
    iota_row = sb(ctx, "iota_row", [P, P])
    small = sb(ctx, "small", [P, 64])

    def loads(sp, pairs, src, wbuf, s_ld, s_mm, last=()):
        for s in range(2):
            sp.dma_start(wbuf[s], src(s)).then_inc(s_ld[s], 16)
        if pairs > 1:
            with sp.Fori(1, pairs) as i:
                for s in range(2):
                    sp.wait_ge(s_mm, (i * 2 + (s - 1)) * TT)
                    sp.dma_start(wbuf[s], src(i * 2 + s)).then_inc(s_ld[s], 16)
        for s, (chunk, width) in enumerate(last):
            sp.wait_ge(s_mm, (pairs * 2 + s - 1) * TT)
            sp.dma_start(wbuf[s][:, 0:KT * width], chunk).then_inc(s_ld[s], 16)

    def products(pe, pairs, lhs, rhs, s_ld, s_mm, s_bank, kt=KT, last=()):
        def one(i, s, width):
            pe.wait_ge(s_ld[s], (i + 1) * 16)
            for m in range(4):
                pe.wait_ge(s_bank, (i * 2 + s) * 4 + m + 1)
                for k in range(kt):
                    mm = pe.matmul(ps[:, m, 0:width], lhs(s, k, m), rhs(s, k, m, width), start=(k == 0), stop=(k == kt - 1))
                mm.then_inc(s_mm, 1)

        with pe.Fori(0, pairs) as i:
            for s in range(2):
                one(i, s, CH)
        for s, (_, width) in enumerate(last):
            one(pairs, s, width)

    def evacuate(eng, pairs, s_mm, s_bank, op, last=()):
        def one(i, s, width):
            for m in range(4):
                eng.wait_ge(s_mm, (i * 2 + s) * 4 + m + 1)
                op(i, s, m, ps[:, m, 0:width]).then_inc(s_bank, 1)

        eng.sem_inc(s_bank, 4)
        with eng.Fori(0, pairs) as i:
            for s in range(2):
                one(i, s, CH)
        for s, (_, width) in enumerate(last):
            one(pairs, s, width)
        eng.wait_ge(s_bank, 4 + 4 * (2 * pairs + len(last)))

    def turn(pe, src, s_done, s_taken, kt=KT, banks=(4, 5), at=0):
        for k in range(kt):
            if k >= 2:
                pe.wait_ge(s_taken, at + k - 1)
            for m in range(TT):
                tr = pe.transpose(ps[:, banks[k % 2], m * P:(m + 1) * P], src(m, k), ident[:, :])
            tr.then_inc(s_done, 1)

    def turned(act, dst, s_done, s_taken, kt=KT, banks=(4, 5), at=0):
        for k in range(kt):
            act.wait_ge(s_done, at + k + 1)
            act.activation(dst(k), ps[:, banks[k % 2], :], ACT.Copy).then_inc(s_taken, 1)

    def square_sums(act, src, junk, ss, s_ss):
        for m in range(TT):
            act_steps(act.activation(junk[:, :], src[:, m, :], ACT.Square, accum_out=ss[:, m:m + 1]))
        act.sem_inc(s_ss, 1)

    def inverse_root(dve, mean, root, tmp, s_root):
        dve.wait_ge(*s_root)
        dve_steps(dve.reciprocal(root, root))
        dve_steps(dve.tensor_tensor(tmp, root, root, ALU.mult))
        dve_steps(dve.tensor_tensor(tmp, tmp, mean, ALU.mult))
        dve_steps(dve.tensor_scalar(tmp, tmp, -0.5, 1.5, ALU.mult, ALU.add))
        dve_steps(dve.tensor_tensor(mean, root, tmp, ALU.mult))

    def attention(block, name, heads, dq, dv, scale, load, bias_of, diag_mask, v_of, o_dst, extra_tensors):
        st = extra_tensors
        turn_src = st["turn_src"]
        qn, kn, qT, kT, S, Pm, PT, nmax, den = (st[k] for k in ("qn", "kn", "qT", "kT", "S", "Pm", "PT", "nmax", "den"))
        s_n, s_t, s_qk, s_sc, s_max, s_p, s_pt, s_pte, s_pv, s_o = (
            sem(f"{name}_{x}") for x in ("normed", "turned", "qk_here", "scores", "max", "probs", "probs_turned",
                                         "probs_t_here", "values", "heads"))

        @block.vector
        def _(dve):
            dve_steps.on(dve)
            with dve.Fori(0, heads) as i:
                dve_steps.loop(i, st["steps"])
                load(dve, i, qn, kn)
                dve.sem_inc(s_n, 1)
                bias = bias_of(dve, i)
                for q in range(TT):
                    K = (q + 1) * P
                    wait(dve, s_sc, i * TT + q + 1)
                    dve_steps(dve.scalar_tensor_tensor(out=S[:, q, 0:K], in0=ps[:, q, 0:K], scalar=scale,
                                                       in1=bias(q), op0=ALU.mult, op1=ALU.add))
                    if diag_mask is not None:
                        dve_steps(dve.tensor_tensor(S[:, q, q * P:K], S[:, q, q * P:K], diag_mask, ALU.add))
                    dve.tensor_reduce(nmax[:, q:q + 1], S[:, q, 0:K], AX.X, ALU.max, negate=True).then_inc(s_max, 1)
                wait(dve, s_p, i * TT + TT)
                dve_steps(dve.reciprocal(den[:, :], den[:, :]))
                wait(dve, s_pv, i * TT + TT)
                dve_steps(dve.tensor_tensor(o_dst(i), ps[:, 6, 0:TT * dv].rearrange("p (q d) -> p q d", q=TT),
                                            den[:, :].unsqueeze(2).to_broadcast([P, TT, dv]), ALU.mult))
                dve.sem_inc(s_o, 1)
            dve_steps.end(heads)

        @block.tensor
        def _(pe):
            with pe.Fori(0, heads) as i:
                wait(pe, s_n, i + 1)
                for bank, src in enumerate(turn_src, 4):
                    for m in range(TT):
                        tr = pe.transpose(ps[:, bank, m * P:(m + 1) * P], src[:, m, :], ident[:, :])
                    tr.then_inc(s_t, 1)
                pe.wait_ge(s_qk, (i + 1) * 2)
                for q in range(TT):
                    K = (q + 1) * P
                    pe.matmul(ps[:, q, 0:K], qT[:, q * P:K], kT[:, 0:K], start=True, stop=True).then_inc(s_sc, 1)
                for q in range(TT):
                    pe.wait_ge(s_p, i * TT + q + 1)
                    if q >= 2:
                        pe.wait_ge(s_pte, i * TT + q - 1)
                    for b in range(q + 1):
                        tr = pe.transpose(ps[:, 4 + q % 2, b * P:(b + 1) * P], Pm[:, q, b * P:(b + 1) * P], ident[:, :])
                    tr.then_inc(s_pt, 1)
                    pe.wait_ge(s_pte, i * TT + q + 1)
                    for b in range(q + 1):
                        mm = pe.matmul(ps[:, 6, q * dv:(q + 1) * dv], PT[:, q % 2, b, :], v_of(i, b),
                                       start=(b == 0), stop=(b == q))
                    mm.then_inc(s_pv, 1)
                pe.wait_ge(s_o, i + 1)

        @block.scalar
        def _(act):
            act_steps.on(act)
            with act.Fori(0, heads) as i:
                for n, dst in enumerate((qT, kT)):
                    bank = n % len(turn_src)
                    wait(act, s_t, i * len(turn_src) + bank + 1)
                    lo = n * dq % P
                    act.activation(dst[:, :], ps[lo:lo + dq, 4 + bank, :], ACT.Copy).then_inc(s_qk, 1)
                for q in range(TT):
                    wait(act, s_max, i * TT + q + 1)
                    act.activation(Pm[:, q, 0:(q + 1) * P], S[:, q, 0:(q + 1) * P], ACT.Exp, bias=nmax[:, q:q + 1],
                                   accum_out=den[:, q:q + 1]).then_inc(s_p, 1)
                for q in range(TT):
                    wait(act, s_pt, i * TT + q + 1)
                    act.activation(PT[:, q % 2, 0:q + 1, :],
                                   ps[:, 4 + q % 2, 0:(q + 1) * P].rearrange("p (b n) -> p b n", n=P),
                                   ACT.Copy).then_inc(s_pte, 1)

    first = ctx.enter_context(ExitStack())
    mod = sb(first, "mod", [P, 6 * D])
    att = ExitStack()
    negdist = sb(att, "negdist", [P, SEQ])
    mask_a = sb(att, "mask_a", [P, SEQ])
    mask_b = sb(att, "mask_b", [P, SEQ])
    slopes = sb(att, "slopes", [P, 16])
    dist_i = sb(att, "dist_i", [P, SEQ], I32)
    dist_j = sb(att, "dist_j", [P, SEQ], I32)
    scratch = sb(att, "scratch", [P, SEQ])
    proj = sb(att, "proj", [P, TT, 3 * D])
    hT = sb(att, "hT", [P, KT, SEQ])
    o_mix = sb(att, "o_mix", [P, TT, D])
    s_const, s_mask = sem("constants"), sem("masks")
    s_mod_in, s_cast, s_x, s_ld_a, s_mm_a, s_bank_a = (
        sem("mod_inputs"), sem("silu_here"), sem("x_here"), [sem("ada_ld0"), sem("ada_ld1")], sem("ada_mm"), sem("ada_bank"))
    stage = ExitStack()
    wbuf_t = sb(stage, "wbuf_ada", [P, 2, KT * CH])
    wbuf = [wbuf_t[:, s, :] for s in range(2)]
    c_col = sb(stage, "c_col", [P, KT])
    c_rep = sb(stage, "c_rep", [P, KT, P])
    s_sig = sem("sigmoid_c")
    with nc.Block() as block:
        @block.gpsimd
        def _(pool):
            pool_steps.on(pool)
            pool_steps(pool.memset(ident[:, :], 0.0))
            pool_steps(pool.affine_select(out=ident[:, :], in_=ident[:, :], compare_op=ALU.not_equal, fill=1.0, base=0,
                                          pattern=[[-1, P]], channel_multiplier=1))
            pool_steps(pool.memset(ones[:, :], 1.0))
            pool.affine_select(out=tri_before[:, :], in_=ones[:, :], compare_op=ALU.is_gt, fill=0.0, base=0,
                               pattern=[[1, P]], channel_multiplier=-1).then_inc(s_const, 1)
            pool.affine_select(out=tri_upto[:, :], in_=ones[:, :], compare_op=ALU.is_ge, fill=0.0, base=0,
                               pattern=[[1, P]], channel_multiplier=-1).then_inc(s_const, 1)
            pool.iota(iota_row[:, :], [[1, P]], base=0, channel_multiplier=0,
                      allow_small_or_imprecise_dtypes=True).then_inc(s_const, 1)
            pool.iota(negdist[:, :], [[1, SEQ]], base=-(SEQ - P), channel_multiplier=-1,
                      allow_small_or_imprecise_dtypes=True).then_inc(s_const, 1)
            pool.iota(dist_i[:, :], [[-1, SEQ]], base=SEQ - P, channel_multiplier=1).then_inc(s_const, 1)
            pool_steps(pool.memset(mask_b[:, :], 0.0))
            pool.affine_select(out=mask_b[:, :], in_=mask_b[:, :], compare_op=ALU.is_ge, fill=MASKED, base=SEQ - P,
                               pattern=[[-1, SEQ]], channel_multiplier=1).then_inc(s_const, 1)
            for h in range(8):
                pool.memset(slopes[:, h:h + 1], 2.0 ** -(h + 1.0)).then_inc(s_const, 1)
                pool.memset(slopes[:, 8 + h:9 + h], 2.0 ** (-2.0 * (h // 2 + 1))).then_inc(s_const, 1)
            pool.wait_ge(s_mask, 1)
            pool.affine_select(out=mask_a[:, :], in_=mask_a[:, :], compare_op=ALU.is_ge, fill=MASKED, base=SEQ - P,
                               pattern=[[-1, SEQ]], channel_multiplier=1).then_inc(s_const, 1)
            pool.wait_ge(s_const, 23)

        @block.sync
        def _(sp):
            sp.dma_start(c_col[:, :], t["c"]).then_inc(s_mod_in, 16)
            sp.dma_start(mod[:, :], t["b_ada"].partition_broadcast(P)).then_inc(s_cast, 16)
            sp.dma_start(x_sb[:, :, :], t["x"].rearrange("a (m p) d -> p (a m) d", p=P)).then_inc(s_x, 16)
            loads(sp, 6, lambda n: t["w_ada"][n, :, :], wbuf, s_ld_a, s_mm_a)
            sp.wait_ge(s_x, 16)

        @block.scalar
        def _(act):
            act.wait_ge(s_mod_in, 16)
            act.activation(small[:, 0:KT], c_col[:, :], ACT.Sigmoid).then_inc(s_sig, 1)

        @block.vector
        def _(dve):
            dve_steps.on(dve)
            dve.wait_ge(s_sig, 1)
            dve_steps(dve.tensor_tensor(c_col[:, :], c_col[:, :], small[:, 0:KT], ALU.mult))
            dve.wait_ge(s_const, 3)
            for k in range(KT):
                dve_steps(dve.tensor_scalar(c_rep[:, k, :], ones[:, :], c_col[:, k:k + 1], None, ALU.mult))
            dve.sem_inc(s_sig, 1)
            dve.wait_ge(s_const, 5)
            dve_steps(dve.tensor_scalar(mask_a[:, :], dist_i[:, :], float(P), None, ALU.is_le))
            for dil in (4, 16):
                dve_steps(dve.tensor_scalar(dist_j[:, :], dist_i[:, :], dil - 1, None, ALU.bitwise_and))
                dve_steps(dve.tensor_scalar(scratch[:, :], dist_j[:, :], 0.0, None, ALU.is_equal))
                dve_steps(dve.tensor_tensor(mask_a[:, :], mask_a[:, :], scratch[:, :], ALU.add))
            dve_steps(dve.tensor_copy(scratch[:, :], mask_a[:, :]))
            dve_steps(dve.tensor_scalar(mask_a[:, :], scratch[:, :], 0.0, MASKED, ALU.is_equal, ALU.mult))
            for n in (2, 3):
                dve_steps(dve.tensor_scalar(dist_j[:, :].bitcast(F32), scratch[:, :], float(n), math.log(n), ALU.is_equal, ALU.mult))
                dve_steps(dve.tensor_tensor(mask_a[:, :], mask_a[:, :], dist_j[:, :].bitcast(F32), ALU.add))
            dve.sem_inc(s_mask, 1)
            dve.wait_ge(s_cast, 16)

            def add_bias(n, m, bank):
                return dve.tensor_tensor(mod[:, ds(n * CH, CH)], bank, mod[:, ds(n * CH, CH)], ALU.add)
            dve.sem_inc(s_bank_a, 1)
            with dve.Fori(0, 6) as i:
                for s in range(2):
                    wait(dve, s_mm_a, (i * 2 + s + 1) * TT)
                    add_bias(i * 2 + s, 0, ps[:, 0, :]).then_inc(s_bank_a, 1)
            dve.wait_ge(s_bank_a, 13)

        @block.tensor
        def _(pe):
            pe.wait_ge(s_sig, 2)
            with pe.Fori(0, 6) as i:
                for s in range(2):
                    pe.wait_ge(s_ld_a[s], (i + 1) * 16)
                    pe.wait_ge(s_bank_a, i * 2 + s + 1)
                    for k in range(KT):
                        mm = pe.matmul(ps[:, 0, :], c_rep[:, k, :], wbuf[s][:, k * CH:(k + 1) * CH],
                                       start=(k == 0), stop=(k == KT - 1))
                    mm.then_inc(s_mm_a, TT)
    stage.close()

    stage = ExitStack()
    wbuf_t = sb(stage, "wbuf_in", [P, 2, KT * CH])
    wbuf = [wbuf_t[:, s, :] for s in range(2)]
    h = sb(stage, "h", [P, TT, D])
    gain = sb(stage, "gain", [P, D])
    s_ss, s_root, s_g, s_h, s_tp, s_tpe = (sem(f"norm1_{x}") for x in ("sums", "root", "gain", "h", "turned", "taken"))
    s_ld_p, s_mm_p, s_bank_p = [sem("in_ld0"), sem("in_ld1")], sem("in_mm"), sem("in_bank")
    rms = small[:, 8:12]
    root, tmp = small[:, 12:16], small[:, 16:20]
    s_sq = sem("norm1_mean")

    def norm_block(block, gain, g_src, scale_at, shift_at, parts, sems, hh, hTT):
        s_ss, s_sq, s_root, s_g, s_h, s_tp, s_tpe = sems

        @block.sync
        def _(sp):
            sp.dma_start(gain[:, :], g_src.partition_broadcast(P)).then_inc(s_g, 16)
            for n, (pairs, w_src, dst, wb, (s_ld, s_mm, s_bank), last) in enumerate(parts):
                if n:
                    sp.wait_ge(parts[n - 1][4][1], TT * (2 * parts[n - 1][0] + len(parts[n - 1][5])))
                loads(sp, pairs, w_src, wb, s_ld, s_mm, last)

        @block.scalar
        def _(act):
            act_steps.on(act)
            square_sums(act, x_sb, hh[:, 0, :], small[:, 8:12], s_ss)
            act.wait_ge(s_sq, 1)
            act.activation(root, rms, ACT.Sqrt).then_inc(s_root, 1)
            turned(act, lambda k: hTT[:, k, :], s_tp, s_tpe)
            for pairs, w_src, dst, wb, (s_ld, s_mm, s_bank), last in parts:
                evacuate(act, pairs, s_mm, s_bank, lambda i, s, m, bank: act.activation(dst(i, s, m, bank.shape[1]), bank, ACT.Copy),
                         last)

        @block.vector
        def _(dve):
            dve_steps.on(dve)
            dve.wait_ge(s_g, 16)
            if scale_at is not None:
                dve_steps(dve.scalar_tensor_tensor(out=gain[:, :], in0=mod[:, scale_at:scale_at + D], scalar=1.0,
                                                   in1=gain[:, :], op0=ALU.add, op1=ALU.mult))
            dve.wait_ge(s_ss, 1)
            dve_steps(dve.tensor_scalar(rms, rms, 1.0 / D, EPS, ALU.mult, ALU.add))
            dve.sem_inc(s_sq, 1)
            inverse_root(dve, rms, root, tmp, (s_root, 1))
            for m in range(TT):
                dve_steps(dve.scalar_tensor_tensor(out=hh[:, m, :], in0=x_sb[:, m, :], scalar=rms[:, m:m + 1],
                                                   in1=gain[:, :], op0=ALU.mult, op1=ALU.mult))
                if shift_at is not None:
                    dve_steps(dve.tensor_tensor(hh[:, m, :], hh[:, m, :], mod[:, shift_at:shift_at + D], ALU.add))
            dve.sem_inc(s_h, 1)

        @block.tensor
        def _(pe):
            pe.wait_ge(s_h, 1)
            turn(pe, lambda m, k: hh[:, m, k * P:(k + 1) * P], s_tp, s_tpe)
            pe.wait_ge(s_tpe, KT)
            for pairs, w_src, dst, wb, (s_ld, s_mm, s_bank), last in parts:
                products(pe, pairs, lambda s, k, m: hTT[:, k, m * P:(m + 1) * P],
                         lambda s, k, m, w: wb[s][:, k * w:(k + 1) * w], s_ld, s_mm, s_bank, last=last)

    with nc.Block() as block:
        norm_block(block, gain, t["norm1_g"], D, 0,
                   [(3, lambda n: t["w_in"][n, :, :], lambda i, s, m, w: proj[:, m, ds((i * 2 + s) * CH, w)], wbuf,
                     (s_ld_p, s_mm_p, s_bank_p), ())],
                   (s_ss, s_sq, s_root, s_g, s_h, s_tp, s_tpe), h, hT)
    stage.close()

    stage = ExitStack()
    gains = sb(stage, "gains", [P, 4, HD])
    lam_in = sb(stage, "lam_in", [P, 4, HD])
    sq = sb(stage, "sq", [P, TT, SEQ])
    rn = sb(stage, "rn", [P, 4, TT, 8])
    rt = sb(stage, "rt", [P, 4, TT, 8])
    rtmp = sb(stage, "rtmp", [P, 4, TT, 8])
    o_b = sb(stage, "o_b", [P, TT, 8, 2 * HD])
    bias_t = sb(stage, "bias_t", [P, SEQ])
    qk = sb(stage, "qk", [P, TT, 2 * HD])
    tens = dict(qn=qk[:, :, 0:HD], kn=qk[:, :, HD:2 * HD], turn_src=(qk,), qT=sb(stage, "qT", [HD, SEQ]),
                kT=sb(stage, "kT", [HD, SEQ]), S=sb(stage, "S", [P, TT, SEQ]), Pm=sb(stage, "Pm", [P, TT, SEQ]),
                PT=sb(stage, "PT", [P, 2, TT, P]), nmax=sb(stage, "nmax", [P, TT]), den=sb(stage, "den", [P, TT]),
                steps=5 + TT + 2)
    s_gn, s_sqd, s_red, s_rt, s_e = (sem(f"heads_{x}") for x in ("gains", "squared", "reduced", "roots", "lambda_exp"))
    kinds = (0, SEQ, 3 * SEQ, 4 * SEQ)
    with nc.Block() as block:
        @block.sync
        def _(sp):
            for n, g in enumerate(("a_q_norm_g", "a_k_norm_g", "b_q_norm_g", "b_k_norm_g")):
                sp.dma_start(gains[:, n, :], t[g].partition_broadcast(P)).then_inc(s_gn, 16)
            for n, g in enumerate(("lambda_q1", "lambda_k1", "lambda_q2", "lambda_k2")):
                sp.dma_start(lam_in[:, n, :], t[g].partition_broadcast(P)).then_inc(s_gn, 16)

        @block.scalar
        def _(act):
            act_steps.on(act)
            for n, at in enumerate(kinds):
                if n:
                    act.wait_ge(s_red, n)
                act.activation(sq[:, :, :], proj[:, :, at:at + SEQ], ACT.Square).then_inc(s_sqd, 1)
            act.wait_ge(s_red, 5)
            act.activation(rt[:, :, :, :], rn[:, :, :, :], ACT.Sqrt).then_inc(s_rt, 1)
            act.wait_ge(s_e, 1)
            act.activation(small[:, 20:22], small[:, 20:22], ACT.Exp).then_inc(s_e, 1)

        @block.vector
        def _(dve):
            dve_steps.on(dve)
            for n in range(4):
                dve.wait_ge(s_sqd, n + 1)
                dve.tensor_reduce(rn[:, n, :, :], sq[:, :, :].rearrange("p m (h d) -> p m h d", d=HD), AX.X,
                                  ALU.add).then_inc(s_red, 1)
            dve.wait_ge(s_red, 4)
            dve.tensor_scalar(rn[:, :, :, :], rn[:, :, :, :], 1.0 / HD, EPS, ALU.mult, ALU.add).then_inc(s_red, 1)
            dve.wait_ge(s_red, 5)
            inverse_root(dve, rn[:, :, :, :], rt[:, :, :, :], rtmp[:, :, :, :], (s_rt, 1))
            dve.wait_ge(s_gn, 8 * 16)
            for n in range(2):
                dve_steps(dve.tensor_tensor(lam_in[:, 2 * n, :], lam_in[:, 2 * n, :], lam_in[:, 2 * n + 1, :], ALU.mult))
                dve_steps(dve.tensor_reduce(small[:, 20 + n:21 + n], lam_in[:, 2 * n, :], AX.X, ALU.add))
            dve.sem_inc(s_e, 1)
            dve.wait_ge(s_e, 2)
            dve_steps(dve.scalar_tensor_tensor(out=small[:, 22:23], in0=small[:, 21:22], scalar=-LAMBDA_INIT,
                                               in1=small[:, 20:21], op0=ALU.add, op1=ALU.subtract))

    def load_heads(q_at, k_at, kind):
        def load(dve, i, qn, kn):
            for dst, at, n in ((qn, q_at, kind), (kn, k_at, kind + 1)):
                dve_steps(dve.tensor_tensor(dst[:, :, :], proj[:, :, ds(i * HD + at, HD)],
                                            rn[:, n, :, ds(i, 1)].to_broadcast([P, TT, HD]), ALU.mult))
                dve_steps(dve.tensor_tensor(dst[:, :, :], dst[:, :, :],
                                            gains[:, n, :].unsqueeze(1).to_broadcast([P, TT, HD]), ALU.mult))
        return load

    def alibi(slope_at, mask):
        def bias_of(dve, i):
            dve_steps(dve.scalar_tensor_tensor(out=bias_t[:, :], in0=negdist[:, :], scalar=slopes[:, ds(i + slope_at, 1)],
                                               in1=mask[:, :], op0=ALU.mult, op1=ALU.add))
            return lambda q: bias_t[:, (TT - 1 - q) * P:SEQ]
        return bias_of

    with nc.Block() as block:
        attention(block, "dilated", 8, HD, HD, HD ** -0.5, load_heads(kinds[0], kinds[1], 0), alibi(0, mask_a), None,
                  lambda i, b: proj[:, b, ds(i * HD + 2 * SEQ, HD)], lambda i: o_mix[:, :, ds(i * HD, HD)], tens)
    with nc.Block() as block:
        vb = proj[:, :, 5 * SEQ:6 * SEQ]
        attention(block, "differential", 8, HD, 2 * HD, HD ** -0.5, load_heads(kinds[2], kinds[3], 2), alibi(8, mask_b), None,
                  lambda i, b: proj[:, b, ds((i // 2) * 2 * HD + 5 * SEQ, 2 * HD)], lambda i: o_b[:, :, ds(i, 1), :].rearrange("p m h d -> p m (h d)"), tens)
    s_bd, s_bs, s_br, s_bg = sem("diff_sum"), sem("diff_mean"), sem("diff_root"), sem("diff_gain")
    with nc.Block() as block:
        pairs_b = o_b[:, :, :, :].rearrange("p m (h c) d -> p m h c d", c=2)
        diff_g = gains[:, 0:2, :].rearrange("p a d -> p (a d)")
        ob_out = o_mix[:, :, SEQ:D].rearrange("p m (h d) -> p m h d", h=4)

        @block.sync
        def _(sp):
            sp.dma_start(diff_g, t["diff_norm_g"].partition_broadcast(P)).then_inc(s_bg, 16)

        @block.scalar
        def _(act):
            act.wait_ge(s_bd, 1)
            act.activation(sq[:, :, :], o_mix[:, :, SEQ:D], ACT.Square).then_inc(s_bd, 1)
            act.wait_ge(s_bs, 1)
            act.activation(small[:, 40:56], small[:, 24:40], ACT.Sqrt).then_inc(s_br, 1)

        @block.vector
        def _(dve):
            dve_steps.on(dve)
            for m in range(TT):
                dve_steps(dve.scalar_tensor_tensor(out=ob_out[:, m, :, :], in0=pairs_b[:, m, :, 1, :], scalar=small[:, 22:23],
                                                   in1=pairs_b[:, m, :, 0, :], op0=ALU.mult, op1=ALU.add))
            dve.sem_inc(s_bd, 1)
            dve.wait_ge(s_bd, 2)
            mean = small[:, 24:40]
            dve_steps(dve.tensor_reduce(mean.rearrange("p (m h) -> p m h", h=4), sq[:, :, :].rearrange("p m (h d) -> p m h d", h=4), AX.X, ALU.add))
            dve_steps(dve.tensor_scalar(mean, mean, 1.0 / P, EPS, ALU.mult, ALU.add))
            dve.sem_inc(s_bs, 1)
            inverse_root(dve, mean, small[:, 40:56], rtmp[:, 0, 0:2, :].rearrange("p a b -> p (a b)"), (s_br, 1))
            dve.wait_ge(s_bg, 16)
            dve_steps(dve.tensor_scalar(diff_g, diff_g, 1.0 - LAMBDA_INIT, None, ALU.mult))
            for m in range(TT):
                dve_steps(dve.tensor_tensor(ob_out[:, m, :, :], ob_out[:, m, :, :],
                                            mean[:, 4 * m:4 * m + 4].unsqueeze(2).to_broadcast([P, 4, P]), ALU.mult))
                dve_steps(dve.tensor_tensor(ob_out[:, m, :, :], ob_out[:, m, :, :],
                                            diff_g.unsqueeze(1).to_broadcast([P, 4, P]), ALU.mult))
    stage.close()

    def out_projection(name, src, w, dst_T, gate_at):
        stage = ExitStack()
        wbuf_t = sb(stage, f"wbuf_{name}", [P, 2, KT * CH])
        scr = sb(stage, f"scr_{name}", [P, CH])
        wb = [wbuf_t[:, s, :] for s in range(2)]
        s_tp, s_tpe, s_mm, s_bank = (sem(f"{name}_{x}") for x in ("turned", "taken", "mm", "bank"))
        s_ld = [sem(f"{name}_ld0"), sem(f"{name}_ld1")]
        with nc.Block() as block:
            @block.sync
            def _(sp):
                loads(sp, 1, lambda n: w[n, :, :], wb, s_ld, s_mm)

            @block.scalar
            def _(act):
                turned(act, lambda k: dst_T[:, k, :], s_tp, s_tpe)

            @block.tensor
            def _(pe):
                turn(pe, lambda m, k: src[:, m, k * P:(k + 1) * P], s_tp, s_tpe)
                pe.wait_ge(s_tpe, KT)
                products(pe, 1, lambda s, k, m: dst_T[:, k, m * P:(m + 1) * P],
                         lambda s, k, m, w: wb[s][:, k * w:(k + 1) * w], s_ld, s_mm, s_bank)

            @block.vector
            def _(dve):
                dve_steps.on(dve)
                dve.sem_inc(s_bank, 4)
                for n in range(2):
                    for m in range(TT):
                        dve.wait_ge(s_mm, n * TT + m + 1)
                        xs = x_sb[:, m, n * CH:(n + 1) * CH]
                        if gate_at is None:
                            dve.tensor_tensor(xs, ps[:, m, :], xs, ALU.add).then_inc(s_bank, 1)
                        else:
                            dve_steps(dve.tensor_tensor(scr[:, :], ps[:, m, :], mod[:, gate_at + n * CH:gate_at + (n + 1) * CH],
                                                        ALU.mult))
                            dve.sem_inc(s_bank, 1)
                            dve_steps(dve.tensor_tensor(xs, xs, scr[:, :], ALU.add))
        stage.close()

    out_projection("mix", o_mix, t["w_out"], hT, 2 * D)
    att.close()

    moe = ExitStack()
    gate = sb(moe, "gate", [P, TT, TOPK])
    gate_all = sb(moe, "gate_all", [P, TT, NE])
    dest_i = sb(moe, "dest_i", [P, TOPK, TT], I32)
    slot_ids = sb(moe, "slot_ids", [P, NBLK], I32)
    blk_f = sb(moe, "blk_f", [P, NBLK])
    blk_i = sb(moe, "blk_i", [P, NBLK], I32)
    used_i = sb(moe, "used_i", [P, 1], I32)
    h_rows = nc.dram_tensor("h_rows", [SEQ, D], F32, kind="Internal").ap()
    slot_rows = nc.dram_tensor("slot_rows", [P * NBLK, 1], I32, kind="Internal").ap()
    y_rows = nc.dram_tensor("y_rows", [NBLK * P, D], F32, kind="Internal").ap()
    route = ExitStack()
    gain2 = sb(route, "gain2", [P, D])
    h2 = sb(route, "h2", [P, TT, D])
    h2T = sb(route, "h2T", [P, KT, SEQ])
    with nc.Block() as block:
        norm_block(block, gain2, t["norm2_g"], 4 * D, 3 * D, (),
                   tuple(sem(f"norm2_{x}") for x in ("sums", "mean", "root", "gain", "h", "turned", "taken")),
                   h2, h2T)

    wr = sb(route, "wr", [P, KT * NE])
    br = sb(route, "br", [P, NE])
    logits = sb(route, "logits", [P, TT, NE])
    top_v = sb(route, "top_v", [P, TT, 8])
    top_i = sb(route, "top_i", [P, TT, 8], U32)
    top_f = sb(route, "top_f", [P, TT, TOPK])
    gsum = sb(route, "gsum", [P, TT])
    onehot = sb(route, "onehot", [P, TOPK, TT, NE])
    rtmp4 = sb(route, "rtmp4", [P, TT, NE])
    chosen = sb(route, "chosen", [P, TT, NE])
    count = sb(route, "count", [P, NE])
    nblocks = sb(route, "nblocks", [P, NE])
    ends = sb(route, "ends", [P, NE])
    starts = sb(route, "starts", [P, NE])
    slot_f = sb(route, "slot_f", [P, TT, NE])
    dest_f = sb(route, "dest_f", [P, TOPK, TT])
    place_i = sb(route, "place_i", [P, TOPK, TT], I32)
    place_j = sb(route, "place_j", [P, TOPK, TT], I32)
    token_i = sb(route, "token_i", [P, TT], I32)
    zero_i = sb(route, "zero_i", [P, NBLK], I32)
    past = sb(route, "past", [P, NBLK, NE])
    s_rin, s_hst, s_lg, s_gd, s_ge, s_ch, s_pos, s_pl, s_tok, s_zero, s_sc, s_ids, s_tz = (
        sem(f"route_{x}") for x in ("inputs", "h_stored", "logits", "gate_diff", "gate_exp", "chosen", "positions", "places",
                                    "token_ids", "zeroed", "scattered", "slots_here", "zeros"))
    with nc.Block() as block:
        @block.sync
        def _(sp):
            sp.dma_start(wr[:, :], t["w_router"]).then_inc(s_rin, 16)
            sp.dma_start(br[:, :], t["b_router"].partition_broadcast(P)).then_inc(s_rin, 16)
            sp.dma_start(h_rows.rearrange("(m p) d -> p m d", p=P), h2[:, :, :]).then_inc(s_hst, 16)
            sp.wait_ge(s_tz, 1)
            sp.dma_start(slot_rows.rearrange("(p j) o -> p (j o)", p=P), zero_i[:, :]).then_inc(s_zero, 16)
            sp.wait_ge(s_hst, 16)
            sp.wait_ge(s_sc, 16 * TOPK * TT)
            sp.dma_start(slot_ids[:, :], slot_rows.rearrange("(p j) o -> p (j o)", p=P)).then_inc(s_ids, 16)
            sp.wait_ge(s_ids, 16)

        @block.gpsimd
        def _(pool):
            pool.memset(zero_i[:, :], 0).then_inc(s_tz, 1)
            pool.iota(token_i[:, :], [[P, TT]], base=0, channel_multiplier=1).then_inc(s_tok, 1)
            pool.wait_ge(s_tok, 1)
            pool.wait_ge(s_zero, 16)
            pool.wait_ge(s_pl, 1)
            for k in range(TOPK):
                for m in range(TT):
                    pool.indirect_dma_start(slot_rows, bass.IndirectOffsetOnAxis(ap=place_i[:, k, m:m + 1], axis=0),
                                            token_i[:, m:m + 1], None).then_inc(s_sc, 16)

        @block.tensor
        def _(pe):
            pe.wait_ge(s_rin, 32)
            for m in range(TT):
                for k in range(KT):
                    mm = pe.matmul(ps[:, 0, m * NE:(m + 1) * NE], h2T[:, k, m * P:(m + 1) * P], wr[:, k * NE:(k + 1) * NE],
                                   start=(k == 0), stop=(k == KT - 1))
            mm.then_inc(s_lg, 1)
            pe.wait_ge(s_ch, 1)
            for m in range(TT):
                for n in range(m + 1):
                    pe.matmul(ps[:, 1, m * NE:(m + 1) * NE], (tri_before if n == m else ones)[:, :], chosen[:, n, :],
                              start=(n == 0), stop=(n == m))
            for n in range(TT):
                mm = pe.matmul(ps[:, 1, TT * NE:(TT + 1) * NE], ones[:, :], chosen[:, n, :], start=(n == 0), stop=(n == TT - 1))
            mm.then_inc(s_pos, 1)

        @block.scalar
        def _(act):
            act.wait_ge(s_gd, 1)
            act.activation(gate[:, :, :], gate[:, :, :], ACT.Exp).then_inc(s_ge, 1)

        @block.vector
        def _(dve):
            dve_steps.on(dve)
            dve.wait_ge(s_lg, 1)
            dve_steps(dve.tensor_tensor(logits[:, :, :], ps[:, 0, 0:TT * NE].rearrange("p (m e) -> p m e", e=NE),
                                        br[:, :].unsqueeze(1).to_broadcast([P, TT, NE]), ALU.add))
            for m in range(TT):
                dve_steps(dve.max(top_v[:, m, :], logits[:, m, :]))
                dve_steps(dve.max_index(top_i[:, m, :], top_v[:, m, :], logits[:, m, :]))
            dve_steps(dve.tensor_tensor(gate[:, :, :], top_v[:, :, 0:TOPK], top_v[:, :, 0:1].to_broadcast([P, TT, TOPK]),
                                        ALU.subtract))
            dve.sem_inc(s_gd, 1)
            dve_steps(dve.tensor_copy(top_f[:, :, :], top_i[:, :, 0:TOPK]))
            for k in range(TOPK):
                dve_steps(dve.tensor_tensor(onehot[:, k, :, :], iota_row[:, 0:NE].unsqueeze(1).to_broadcast([P, TT, NE]),
                                            top_f[:, :, k:k + 1].to_broadcast([P, TT, NE]), ALU.is_equal))
            dve_steps(dve.tensor_tensor(chosen[:, :, :], onehot[:, 0, :, :], onehot[:, 1, :, :], ALU.add))
            dve_steps(dve.tensor_tensor(chosen[:, :, :], chosen[:, :, :], onehot[:, 2, :, :], ALU.add))
            dve.tensor_tensor(chosen[:, :, :], chosen[:, :, :], onehot[:, 3, :, :], ALU.add).then_inc(s_ch, 1)
            dve.wait_ge(s_ge, 1)
            dve_steps(dve.tensor_reduce(gsum[:, :], gate[:, :, :], AX.X, ALU.add))
            dve_steps(dve.reciprocal(gsum[:, :], gsum[:, :]))
            dve_steps(dve.tensor_tensor(gate[:, :, :], gate[:, :, :], gsum[:, :].unsqueeze(2).to_broadcast([P, TT, TOPK]),
                                        ALU.mult))
            for k in range(TOPK):
                dst = gate_all if k == 0 else rtmp4
                dve_steps(dve.tensor_tensor(dst[:, :, :], onehot[:, k, :, :], gate[:, :, k:k + 1].to_broadcast([P, TT, NE]),
                                            ALU.mult))
                if k:
                    dve_steps(dve.tensor_tensor(gate_all[:, :, :], gate_all[:, :, :], rtmp4[:, :, :], ALU.add))
            dve.wait_ge(s_pos, 1)
            dve_steps(dve.tensor_copy(count[:, :], ps[:, 1, TT * NE:(TT + 1) * NE]))
            dve_steps(dve.tensor_scalar(nblocks[:, :], count[:, :], 0.0, None, ALU.is_gt))
            for n in range(1, TT):
                dve_steps(dve.tensor_scalar(starts[:, :], count[:, :], float(n * P), None, ALU.is_gt))
                dve_steps(dve.tensor_tensor(nblocks[:, :], nblocks[:, :], starts[:, :], ALU.add))
            dve_steps(dve.tensor_tensor_scan(ends[:, :], ones[:, 0:NE], nblocks[:, :], 0.0, ALU.mult, ALU.add))
            dve_steps(dve.tensor_tensor(starts[:, :], ends[:, :], nblocks[:, :], ALU.subtract))
            dve_steps(dve.tensor_scalar(starts[:, :], starts[:, :], float(P), None, ALU.mult))
            dve_steps(dve.tensor_tensor(slot_f[:, :, :], ps[:, 1, 0:TT * NE].rearrange("p (m e) -> p m e", e=NE),
                                        starts[:, :].unsqueeze(1).to_broadcast([P, TT, NE]), ALU.add))
            for k in range(TOPK):
                dve_steps(dve.tensor_tensor(rtmp4[:, :, :], onehot[:, k, :, :], slot_f[:, :, :], ALU.mult))
                dve_steps(dve.tensor_reduce(dest_f[:, k, :], rtmp4[:, :, :], AX.X, ALU.add))
            dve_steps(dve.tensor_copy(dest_i[:, :, :], dest_f[:, :, :]))
            dve_steps(dve.tensor_scalar(place_j[:, :, :], dest_i[:, :, :], 7, None, ALU.arith_shift_right))
            dve_steps(dve.tensor_scalar(place_i[:, :, :], dest_i[:, :, :], P - 1, None, ALU.bitwise_and))
            dve_steps(dve.tensor_scalar(place_i[:, :, :], place_i[:, :, :], float(NBLK), None, ALU.mult))
            dve_steps(dve.tensor_tensor(place_i[:, :, :], place_i[:, :, :], place_j[:, :, :], ALU.add))
            dve.sem_inc(s_pl, 1)
            dve_steps(dve.tensor_tensor(past[:, :, :], iota_row[:, 0:NBLK].unsqueeze(2).to_broadcast([P, NBLK, NE]),
                                        ends[:, :].unsqueeze(1).to_broadcast([P, NBLK, NE]), ALU.is_ge))
            dve_steps(dve.tensor_reduce(blk_f[:, :], past[:, :, :], AX.X, ALU.add))
            dve_steps(dve.tensor_scalar(blk_f[:, :], blk_f[:, :], float(NE - 1), None, ALU.min))
            dve_steps(dve.tensor_copy(blk_i[:, :], blk_f[:, :]))
            dve_steps(dve.tensor_copy(used_i[:, :], ends[:, NE - 1:NE]))
    route.close()

    stage = ExitStack()
    wexp = sb(stage, "wexp", [P, 6, KT * CH])
    b_f = sb(stage, "b_f", [96, 2 * DFF])
    b_part = sb(stage, "b_part", [96, 2 * DFF], BF16)
    row_f = sb(stage, "row_f", [P, 1])
    pick = sb(stage, "pick", [96, P], BF16)
    cur = sb(stage, "cur", [P, 2], I32)
    xe = sb(stage, "xe", [P, 2, D])
    xT = sb(stage, "xT", [P, KT, P])
    gm = sb(stage, "gm", [P, CH])
    sg = sb(stage, "sg", [P, CH])
    um = sb(stage, "um", [P, CH])
    hid = sb(stage, "hid", [P, 2, CH])
    hidT = sb(stage, "hidT", [P, KT, P])
    zero_y = sb(stage, "zero_y", [P, D])
    s_zy = sem("zero_rows")
    y_sb = sb(stage, "y_sb", [P, 2, D])
    s_wl = [sem(f"expert_w{c}") for c in range(6)]
    s_ga, s_st = [sem("rows_here0"), sem("rows_here1")], [sem("y_stored0"), sem("y_stored1")]
    s_bl, s_bp, s_gu, s_dn, s_xt, s_xte, s_gm, s_sg, s_act, s_at, s_ate, s_y, s_pick, s_rowf, s_cur, s_es, s_free = (
        sem(f"expert_{x}") for x in ("bias_here", "bias_parts", "gate_up", "down", "x_turned", "x_here", "gate_clamped",
                                     "sigmoid", "hidden", "hid_turned", "hid_here", "y_here", "picked", "row_ids", "cur", "steps",
                                     "bias_steps"))
    halves = (0, 2, 1, 3)
    with nc.Block() as block:
        @block.gpsimd
        def _(pool):
            pool.memset(zero_y[:, :], 0.0).then_inc(s_zy, 1)
            pool.wait_ge(s_zy, 1)
            for q in range(3):
                pool.iota(row_f[32 * q:32 * q + 32, :], [[1, 1]], base=0, channel_multiplier=1,
                          allow_small_or_imprecise_dtypes=True).then_inc(s_rowf, 1)
            pool.wait_ge(s_rowf, 3)
            used = pool.value_load(used_i[0:1, 0:1], min_val=1, max_val=NBLK)
            with pool.Fori(0, NBLK // 2) as i:
                for s in range(2):
                    with pool.If(i * 2 + s < used):
                        wait(pool, s_xte, (i * 2 + s) * 2 + 2)
                        pool.tensor_copy(cur[:, s:s + 1], slot_ids[:, ds(i * 2 + s, 1)]).then_inc(s_cur, 1)
                        pool.wait_ge(s_cur, 1)
                        pool.sem_clear(s_cur)
                        pool.indirect_dma_start(xe[:, s, :], None, h_rows,
                                                bass.IndirectOffsetOnAxis(ap=cur[:, s:s + 1], axis=0)).then_inc(s_ga[s], 16)

        @block.sync
        def _(sp):
            for q in range(3):
                sp.dma_start(b_f[32 * q:32 * q + 32, :], t["b_gate_up"]).then_inc(s_bl, 16)
            used = sp.value_load(used_i[0:1, 0:1], min_val=1, max_val=NBLK)
            with sp.Fori(0, NBLK) as j:
                with sp.If(j < used):
                    e = sp.value_load(blk_i[0:1, ds(j, 1)], min_val=0, max_val=NE - 1)
                    for c in range(4):
                        sp.wait_ge(s_gu, j * 4 + c + 1)
                        sp.dma_start(wexp[:, c, :], t["w_gate_up"][e, halves[c], :, :]).then_inc(s_wl[c], 16)
                    for c in range(2):
                        sp.wait_ge(s_dn, j * 2 + c + 1)
                        sp.dma_start(wexp[:, 4 + c, :], t["w_down"][e, c, :, :]).then_inc(s_wl[4 + c], 16)

        @block.tensor
        def _(pe):
            pe.sem_inc(s_gu, 4)
            pe.sem_inc(s_dn, 2)
            pe.wait_ge(s_bp, 1)
            used = pe.value_load(used_i[0:1, 0:1], min_val=1, max_val=NBLK)
            with pe.Fori(0, NBLK // 2) as i:
                for s in range(2):
                    j = i * 2 + s
                    with pe.If(j < used):
                        wait(pe, s_ga[s], (i + 1) * 16)
                        for half in range(2):
                            for n in range(4):
                                k = half * 4 + n
                                tr = pe.transpose(ps[:, 4 + half, n * P:(n + 1) * P], xe[:, s, k * P:(k + 1) * P], ident[:, :])
                            tr.then_inc(s_xt, 1)
                        wait(pe, s_xte, j * 2 + 4 + 2)
                        wait(pe, s_pick, j + 1)

                        def gate_up(c):
                            pe.wait_ge(s_wl[c], (j + 1) * 16)
                            bank = halves[c]
                            for k in range(KT):
                                pe.matmul(ps[:, bank, :], xT[:, k, :], wexp[:, c, k * CH:(k + 1) * CH],
                                          start=(k == 0), stop=False)
                            pe.matmul(ps[:, bank, :], pick[:, :], b_part[:, bank * CH:(bank + 1) * CH],
                                      start=False, stop=True).then_inc(s_gu, 1)

                        def turn_hidden(half):
                            wait(pe, s_act, j * 2 + half + 2)
                            for n in range(4):
                                tr = pe.transpose(ps[:, 4 + half, n * P:(n + 1) * P], hid[:, half, n * P:(n + 1) * P],
                                                  ident[:, :])
                            tr.then_inc(s_at, 1)

                        def down(half):
                            wait(pe, s_ate, j * 2 + half + 1)
                            for c in range(2):
                                if half == 0:
                                    pe.wait_ge(s_wl[4 + c], (j + 1) * 16)
                                    wait(pe, s_y, j * 2 + c + 1)
                                for n in range(4):
                                    k = half * 4 + n
                                    mm = pe.matmul(ps[:, 6 + c, :], hidT[:, k, :], wexp[:, 4 + c, k * CH:(k + 1) * CH],
                                                   start=(k == 0), stop=(k == KT - 1))
                                if half == 1:
                                    mm.then_inc(s_dn, 1)

                        gate_up(0)
                        gate_up(1)
                        gate_up(2)
                        turn_hidden(0)
                        gate_up(3)
                        down(0)
                        turn_hidden(1)
                        down(1)

        @block.scalar
        def _(act):
            act.sem_inc(s_xte, 4)
            act.wait_ge(s_zy, 1)
            for s in range(2):
                act.sem_inc(s_st[s], 16)
            act.sem_inc(s_y, 2)
            used = act.value_load(used_i[0:1, 0:1], min_val=1, max_val=NBLK)
            with act.Fori(0, NBLK // 2) as i:
                for s in range(2):
                    j = i * 2 + s
                    with act.If(j < used):
                        for half in range(2):
                            wait(act, s_xt, j * 2 + half + 1)
                            act.activation(xT[:, half * 4:half * 4 + 4, :],
                                           ps[:, 4 + half, :].rearrange("p (k n) -> p k n", n=P), ACT.Copy).then_inc(s_xte, 1)
                        for half in range(2):
                            wait(act, s_gm, j * 2 + half + 1)
                            act.activation(sg[:, :], gm[:, :], ACT.Sigmoid, scale=SWIGLU_ALPHA).then_inc(s_sg, 1)
                            wait(act, s_at, j * 2 + half + 1)
                            act.activation(hidT[:, half * 4:half * 4 + 4, :],
                                           ps[:, 4 + half, :].rearrange("p (k n) -> p k n", n=P), ACT.Copy).then_inc(s_ate, 1)
                        wait(act, s_st[s], i * 16 + 16)
                        for c in range(2):
                            wait(act, s_dn, j * 2 + 2 + c + 1)
                            act.activation(y_sb[:, s, c * CH:(c + 1) * CH], ps[:, 6 + c, :], ACT.Copy).then_inc(s_y, 1)
                        wait(act, s_y, j * 2 + 2 + 2)
                        act.dma_start(y_rows[ds(j * P, P), :], y_sb[:, s, :]).then_inc(s_st[s], 16)
                    with act.If(used <= j):
                        act.dma_start(y_rows[ds(j * P, P), :], zero_y[:, :]).then_inc(s_st[s], 16)
            for s in range(2):
                act.wait_ge(s_st[s], (NBLK // 2 + 1) * 16)

        @block.vector
        def _(dve):
            dve_steps.on(dve)
            dve.wait_ge(s_bl, 48)
            dve.wait_ge(s_rowf, 3)
            dve_steps(dve.tensor_copy(b_part[:, :], b_f[:, :]))
            for at in (32, 64):
                for lo in range(at, 96, 32):
                    dve_steps(dve.tensor_tensor(b_f[lo:lo + 32, :], b_f[lo:lo + 32, :], b_part[lo:lo + 32, :], ALU.subtract))
                    dve_steps(dve.tensor_copy(b_part[lo:lo + 32, :], b_f[lo:lo + 32, :]))
            dve.sem_inc(s_bp, 1)
            dve.sem_inc(s_act, 1)
            used = dve.value_load(used_i[0:1, 0:1], min_val=1, max_val=NBLK)
            with dve.Fori(0, NBLK) as j:
                with dve.If(j < used):
                    dve.tensor_scalar(pick[:, :], row_f[0:96, :].to_broadcast([96, P]), blk_f[0:96, ds(j, 1)], None,
                                      ALU.is_equal).then_inc(s_pick, 1)
                    for half in range(2):
                        wait(dve, s_act, j * 2 + half + 1)
                        wait(dve, s_gu, j * 4 + 4 + half * 2 + 1)
                        dve.tensor_scalar(gm[:, :], ps[:, half, :], SWIGLU_LIMIT, None, ALU.min).then_inc(s_gm, 1)
                        wait(dve, s_gu, j * 4 + 4 + half * 2 + 2)
                        dve.tensor_scalar(um[:, :], ps[:, 2 + half, :], SWIGLU_LIMIT, -SWIGLU_LIMIT, ALU.min,
                                          ALU.max).then_inc(s_es, 1)
                        wait(dve, s_sg, j * 2 + half + 1)
                        dve.tensor_tensor(gm[:, :], gm[:, :], sg[:, :], ALU.mult).then_inc(s_es, 1)
                        wait(dve, s_es, j * 4 + half * 2 + 2)
                        dve.scalar_tensor_tensor(out=hid[:, half, :], in0=um[:, :], scalar=1.0, in1=gm[:, :],
                                                 op0=ALU.add, op1=ALU.mult).then_inc(s_act, 1)
    stage.close()

    stage = ExitStack()
    yk = sb(stage, "yk", [P, 4, D])
    acc = sb(stage, "acc", [P, D])
    b_dn = sb(stage, "b_dn", [NE, D])
    gT = sb(stage, "gT", [NE, SEQ])
    s_yg = [sem(f"y_rows{k}") for k in range(4)]
    s_bd2, s_gt, s_gte, s_bias, s_yu = (sem(f"combine_{x}") for x in ("bias_here", "gates_turned", "gates_here", "bias", "used"))
    with nc.Block() as block:
        @block.sync
        def _(sp):
            sp.dma_start(b_dn[:, :], t["b_down"]).then_inc(s_bd2, 16)

        @block.gpsimd
        def _(pool):
            for m in range(TT):
                for k in range(TOPK):
                    if m:
                        pool.wait_ge(s_yu, (m - 1) * TOPK + k + 1)
                    pool.indirect_dma_start(yk[:, k, :], None, y_rows,
                                            bass.IndirectOffsetOnAxis(ap=dest_i[:, k, m:m + 1], axis=0)).then_inc(s_yg[k], 16)

        @block.tensor
        def _(pe):
            for m in range(TT):
                tr = pe.transpose(ps[0:NE, 7, m * P:(m + 1) * P], gate_all[:, m, :], ident[:, :])
            tr.then_inc(s_gt, 1)
            pe.wait_ge(s_gte, 1)
            pe.wait_ge(s_bd2, 16)
            for m in range(TT):
                for c in range(2):
                    mm = pe.matmul(ps[:, 2 * m + c, :], gT[:, m * P:(m + 1) * P], b_dn[:, c * CH:(c + 1) * CH],
                                   start=True, stop=True)
                mm.then_inc(s_bias, 1)

        @block.scalar
        def _(act):
            act.wait_ge(s_gt, 1)
            act.activation(gT[:, :], ps[0:NE, 7, :], ACT.Copy).then_inc(s_gte, 1)

        @block.vector
        def _(dve):
            dve_steps.on(dve)
            for m in range(TT):
                dve.wait_ge(s_bias, m + 1)
                for k in range(TOPK):
                    dve.wait_ge(s_yg[k], 16 * (m + 1))
                    other = ps[:, 2 * m:2 * m + 2, :].rearrange("p a n -> p (a n)") if k == 0 else acc[:, :]
                    dve_steps(dve.scalar_tensor_tensor(out=acc[:, :], in0=yk[:, k, :], scalar=gate[:, m, k:k + 1], in1=other,
                                                       op0=ALU.mult, op1=ALU.add))
                    dve.sem_inc(s_yu, 1)
                dve_steps(dve.tensor_tensor(acc[:, :], acc[:, :], mod[:, 5 * D:6 * D], ALU.mult))
                dve_steps(dve.tensor_tensor(x_sb[:, m, :], x_sb[:, m, :], acc[:, :], ALU.add))
    stage.close()
    moe.close()
    first.close()
    clear_semaphores()

    second = ExitStack()
    merged = sb(second, "merged", [P, TT, D])
    ug = sb(second, "ug", [P, TT, 5 * CH])
    fox = ExitStack()
    bias_f = sb(fox, "bias_f", [P, FH, SEQ])
    qkv = sb(fox, "qkv", [P, TT, 3 * D])
    f_log = sb(fox, "f_log", [P, TT, FH])
    stage = ExitStack()
    wbuf_t = sb(stage, "wbuf_in2", [P, 2, KT * CH])
    wbuf = [wbuf_t[:, s, :] for s in range(2)]
    h3T = sb(stage, "h3T", [P, KT, SEQ])
    h3 = bias_f[:, :, :].rearrange("p h t -> p (h t)").rearrange("p (m d) -> p m d", m=TT)
    gain3 = sb(stage, "gain3", [P, D])
    with nc.Block() as block:
        norm_block(block, gain3, t["mix_norm_g_2"], None, None,
                   [(3, lambda n: t["w_qkv_2"][n, :, :], lambda i, s, m, w: qkv[:, m, ds((i * 2 + s) * CH, w)], wbuf,
                     ([sem("qkv_ld0"), sem("qkv_ld1")], sem("qkv_mm"), sem("qkv_bank")), ()),
                    (2, lambda n: t["w_ug_2"][n, :, :],
                     lambda i, s, m, w: f_log[:, m, :] if w == FH else ug[:, m, ds((i * 2 + s) * CH, w)], wbuf,
                     ([sem("ug_ld0"), sem("ug_ld1")], sem("ug_mm"), sem("ug_bank")),
                     ((t["w_ug_2"][4, :, :], CH), (t["w_f_2"], FH)))],
                   tuple(sem(f"norm3_{x}") for x in ("sums", "mean", "root", "gain", "h", "turned", "taken")), h3, h3T)
    stage.close()

    prep = ExitStack()
    f_bias = sb(fox, "f_bias", [P, FH])
    f_abs = sb(fox, "f_abs", [P, TT, FH])
    neg_cum = sb(fox, "neg_cum", [P, TT, FH])
    cumT = sb(fox, "cumT", [FH, SEQ])
    head_row = sb(fox, "head_row", [FH, FH, P])
    diag = sb(fox, "diag", [P, P])
    fgain = sb(fox, "fgain", [P, 2, FHD])
    frn = sb(fox, "frn", [P, 2, TT, FH])
    frt = sb(fox, "frt", [P, 2, TT, FH])
    frtmp = sb(fox, "frtmp", [P, 2, TT, FH])
    fsq = sb(prep, "fsq", [P, TT, D])
    s_fin, s_fc, s_fe, s_fl, s_fcum, s_fn, s_ft, s_fte, s_fb, s_fbe, s_fs, s_fr, s_frt, s_fz = (
        sem(f"forget_{x}") for x in ("inputs", "consts", "abs", "logs", "cum", "neg_cum", "turned", "cum_here", "bias", "bias_here",
                                     "squared", "reduced", "roots", "first"))
    with nc.Block() as block:
        @block.sync
        def _(sp):
            sp.dma_start(f_bias[:, :], t["fox_forget_bias_2"].partition_broadcast(P)).then_inc(s_fin, 16)
            sp.dma_start(fgain[:, 0, :], t["q_norm_g_2"].partition_broadcast(P)).then_inc(s_fin, 16)
            sp.dma_start(fgain[:, 1, :], t["k_norm_g_2"].partition_broadcast(P)).then_inc(s_fin, 16)

        @block.gpsimd
        def _(pool):
            pool_steps.on(pool)
            pool_steps(pool.memset(head_row[:, :, :], 0.0))
            pool_steps(pool.affine_select(out=head_row[:, :, :], in_=head_row[:, :, :], compare_op=ALU.not_equal, fill=1.0, base=0,
                                          pattern=[[-1, FH], [0, P]], channel_multiplier=1))
            pool_steps(pool.memset(diag[:, :], 0.0))
            pool_steps(pool.affine_select(out=diag[:, :], in_=diag[:, :], compare_op=ALU.is_ge, fill=MASKED, base=0,
                                          pattern=[[-1, P]], channel_multiplier=1))
            pool.sem_inc(s_fc, 1)

        @block.vector
        def _(dve):
            dve_steps.on(dve)
            dve.wait_ge(s_fin, 48)
            dve_steps(dve.tensor_tensor(f_log[:, :, :], f_log[:, :, :], f_bias[:, :].unsqueeze(1).to_broadcast([P, TT, FH]),
                                        ALU.add))
            dve_steps(dve.tensor_scalar(f_abs[:, :, :], f_log[:, :, :], -1.0, None, ALU.mult))
            dve_steps(dve.tensor_tensor(f_abs[:, :, :], f_abs[:, :, :], f_log[:, :, :], ALU.max))
            dve.sem_inc(s_fe, 1)
            dve_steps(dve.tensor_scalar(f_log[:, :, :], f_log[:, :, :], 0.0, None, ALU.min))
            dve.wait_ge(s_fe, 2)
            dve_steps(dve.tensor_scalar(f_abs[:, :, :], f_abs[:, :, :], 1.0, None, ALU.add))
            dve.sem_inc(s_fe, 1)
            dve.wait_ge(s_fe, 4)
            dve_steps(dve.tensor_tensor(f_log[:, :, :], f_log[:, :, :], f_abs[:, :, :], ALU.subtract))
            dve.sem_inc(s_fl, 1)
            dve.wait_ge(s_fcum, 1)
            dve.tensor_scalar(neg_cum[:, :, :], ps[:, 0, 0:TT * FH].rearrange("p (m h) -> p m h", h=FH), -1.0, None,
                              ALU.mult).then_inc(s_fn, 1)
            for n in range(2):
                dve.wait_ge(s_fs, n + 1)
                dve.tensor_reduce(frn[:, n, :, :], fsq[:, :, :].rearrange("p m (h d) -> p m h d", d=FHD), AX.X,
                                  ALU.add).then_inc(s_fr, 1)
            dve.wait_ge(s_fr, 2)
            dve_steps(dve.tensor_scalar(frn[:, :, :, :], frn[:, :, :, :], 1.0 / FHD, EPS, ALU.mult, ALU.add))
            dve.sem_inc(s_fr, 1)
            inverse_root(dve, frn[:, :, :, :], frt[:, :, :, :], frtmp[:, :, :, :], (s_frt, 1))

        @block.scalar
        def _(act):
            act.wait_ge(s_fe, 1)
            act.activation(f_abs[:, :, :], f_abs[:, :, :], ACT.Exp, scale=-1.0).then_inc(s_fe, 1)
            act.wait_ge(s_fe, 3)
            act.activation(f_abs[:, :, :], f_abs[:, :, :], ACT.Ln).then_inc(s_fe, 1)
            act.activation(fsq[:, :, :], qkv[:, :, 0:D], ACT.Square).then_inc(s_fs, 1)
            act.wait_ge(s_ft, 1)
            act.activation(cumT[:, :], ps[0:FH, 1, :], ACT.Copy).then_inc(s_fte, 1)
            for hd in range(FH):
                act.wait_ge(s_fb, hd + 1)
                act.activation(bias_f[:, hd, :], ps[:, 2 + hd % 2, :], ACT.Copy).then_inc(s_fbe, 1)
            act.wait_ge(s_fr, 1)
            act.activation(fsq[:, :, :], qkv[:, :, D:2 * D], ACT.Square).then_inc(s_fs, 1)
            act.wait_ge(s_fr, 3)
            act.activation(frt[:, :, :, :], frn[:, :, :, :], ACT.Sqrt).then_inc(s_frt, 1)

        @block.tensor
        def _(pe):
            pe.wait_ge(s_fl, 1)
            for m in range(TT):
                for n in range(m + 1):
                    mm = pe.matmul(ps[:, 0, m * FH:(m + 1) * FH], (tri_upto if n == m else ones)[:, :], f_log[:, n, :],
                                   start=(n == 0), stop=(n == m))
            mm.then_inc(s_fcum, 1)
            pe.wait_ge(s_fn, 1)
            for m in range(TT):
                tr = pe.transpose(ps[0:FH, 1, m * P:(m + 1) * P], neg_cum[:, m, :], ident[:, :])
            tr.then_inc(s_ft, 1)
            pe.wait_ge(s_fte, 1)
            pe.wait_ge(s_fc, 1)
            for hd in range(FH):
                if hd >= 2:
                    pe.wait_ge(s_fbe, hd - 1)
                pe.matmul(ps[:, 2 + hd % 2, :], head_row[:, hd, :], cumT[:, :], start=True, stop=True).then_inc(s_fb, 1)
    prep.close()

    stage = ExitStack()
    fqn, fkn = sb(stage, "fqn", [P, TT, FHD]), sb(stage, "fkn", [P, TT, FHD])
    tens = dict(qn=fqn, kn=fkn, turn_src=(fqn, fkn), qT=sb(stage, "fqT", [FHD, SEQ]),
                kT=sb(stage, "fkT", [FHD, SEQ]), S=sb(stage, "fS", [P, TT, SEQ]), Pm=sb(stage, "fPm", [P, TT, SEQ]),
                PT=sb(stage, "fPT", [P, 2, TT, P]), nmax=sb(stage, "fnmax", [P, TT]), den=sb(stage, "fden", [P, TT]),
                steps=4 + 2 * TT + 2)

    def load_fox(dve, i, qn, kn):
        for n, dst in enumerate((qn, kn)):
            dve_steps(dve.tensor_tensor(dst[:, :, :], qkv[:, :, ds(i * FHD + n * D, FHD)],
                                        frn[:, n, :, ds(i, 1)].to_broadcast([P, TT, FHD]), ALU.mult))
            dve_steps(dve.tensor_tensor(dst[:, :, :], dst[:, :, :],
                                        fgain[:, n, :].unsqueeze(1).to_broadcast([P, TT, FHD]), ALU.mult))

    with nc.Block() as block:
        attention(block, "forgetting", FH, FHD, FHD, FHD ** -0.5, load_fox,
                  lambda dve, i: lambda q: bias_f[:, ds(i, 1), 0:(q + 1) * P].rearrange("p a n -> p (a n)"), diag[:, :],
                  lambda i, b: qkv[:, b, ds(i * FHD + 2 * D, FHD)], lambda i: merged[:, :, ds(i * FHD, FHD)], tens)
    stage.close()
    fox.close()

    ssm = ExitStack()
    yT = sb(ssm, "yT", [P, TT, SEQ])
    stage = ExitStack()
    uT = sb(stage, "uT", [P, TT, SEQ])
    bw = sb(stage, "bw", [P, 4, 2, P])
    cw = sb(stage, "cw", [P, 4, 2, P])
    cw_raw = sb(stage, "cw_raw", [P, 4, 2, P])
    par = sb(stage, "par", [P, 24, ST])
    pw = sb(stage, "pw", [P, 9, 2, ST])
    rot = sb(stage, "rot", [P, 2, 2, 4, SEQ])
    ra, rb = sb(stage, "ra", [P, 4, SEQ // 2]), sb(stage, "rb", [P, 4, SEQ // 2])
    f1, f2 = sb(stage, "f1", [P, SEQ]), sb(stage, "f2", [P, SEQ])
    wre, wim = sb(stage, "wre", [P, SEQ]), sb(stage, "wim", [P, SEQ])
    zst = sb(stage, "zst", [P, 2, 2, SEQ])
    yq = sb(stage, "yq", [P, SEQ])
    d_col = sb(stage, "d_col", [P, TT])
    (A_RE, A_IM, LS, STEP, TH, MAG, KF, R, RH, SN, SH, CS, LRE, LIM, NR, DEN, CRE, CIM, T1, T2) = range(20)
    pc = [par[:, n, :] for n in range(20)]
    s_sin, s_a, s_d, s_pw, s_rot, s_rotu, s_u, s_ute, s_v, s_vu, s_z, s_zu, s_cw, s_yp, s_yq, s_yT = (
        sem(f"ssm_{x}") for x in ("params", "act", "dve", "powers", "rotations", "rot_used", "u_turned", "u_here", "inputs", "inputs_used",
                                  "states", "states_used", "c_here", "y", "y_here", "gelu"))
    s_bw, s_cr = sem("ssm_b_here"), sem("ssm_c_raw")
    with nc.Block() as block:
        @block.sync
        def _(sp):
            sp.dma_start(pc[A_RE], t["ssm_a_re_2"]).then_inc(s_sin, 16)
            sp.dma_start(pc[A_IM], t["ssm_a_im_2"]).then_inc(s_sin, 16)
            for g in range(2):
                sp.dma_start(par[64 * g:64 * g + 64, LS, :], t["ssm_log_step_2"][g:g + 1, :].rearrange("a c -> (a c)").partition_broadcast(64)).then_inc(s_sin, 16)
            sp.dma_start(d_col[:, :], t["ssm_d_2"]).then_inc(s_sin, 16)
            for q in range(TT):
                if q:
                    sp.wait_ge(s_vu, 4 * q)
                sp.dma_start(bw[:, :, :, :], t["ssm_b_2"][q]).then_inc(s_bw, 16)
                if q:
                    sp.wait_ge(s_cw, 4 * q)
                sp.dma_start(cw_raw[:, :, :, :], t["ssm_c_2"][q]).then_inc(s_cr, 16)

        @block.gpsimd
        def _(pool):
            pool_steps.on(pool)
            pool.wait_ge(s_pw, 1)
            for q in range(TT):
                b = q % 2
                if q >= 2:
                    pool.wait_ge(s_rotu, q - 1)
                re, im = rot[:, b, 0, :, :], rot[:, b, 1, :, :]
                pool_steps(pool.memset(re[:, :, 0:1], 1.0))
                pool_steps(pool.memset(im[:, :, 0:1], 0.0))
                for k in range(9):
                    n = 1 << k
                    lr, li = (pw[:, k, c, 4 * q:4 * q + 4].unsqueeze(2).to_broadcast([P, 4, n]) for c in range(2))
                    a, c = ra[:, :, 0:n], rb[:, :, 0:n]
                    pool_steps(pool.tensor_tensor(a, re[:, :, 0:n], lr, ALU.mult))
                    pool_steps(pool.tensor_tensor(c, im[:, :, 0:n], li, ALU.mult))
                    pool_steps(pool.tensor_tensor(re[:, :, n:2 * n], a, c, ALU.subtract))
                    pool_steps(pool.tensor_tensor(a, re[:, :, 0:n], li, ALU.mult))
                    pool_steps(pool.tensor_tensor(c, im[:, :, 0:n], lr, ALU.mult))
                    pool_steps(pool.tensor_tensor(im[:, :, n:2 * n], a, c, ALU.add))
                pool.sem_inc(s_rot, 1)

        @block.tensor
        def _(pe):
            turn(pe, lambda m, k: ug[:, m, k * P:(k + 1) * P], s_u, s_ute, kt=TT)
            pe.wait_ge(s_ute, TT)

            def y_out(q, j):
                pe.wait_ge(s_z, 4 * q + j + 1)
                for c in range(2):
                    mm = pe.matmul(ps[:, 4 + q % 2, :], cw[:, j, c, :], zst[:, j % 2, c, :], start=(j == 0 and c == 0),
                                   stop=(j == 3 and c == 1))
                mm.then_inc(s_yp, 1)

            for q in range(TT):
                pe.wait_ge(s_bw, 16 * (q + 1))
                for j in range(4):
                    n = 4 * q + j
                    if n >= 2:
                        pe.wait_ge(s_vu, n - 1)
                    for c in range(2):
                        mm = pe.matmul(ps[:, 2 * (j % 2) + c, :], bw[:, j, c, :], uT[:, q, :], start=True, stop=True)
                    mm.then_inc(s_v, 1)
                    if n:
                        y_out(*divmod(n - 1, 4))
            y_out(TT - 1, 3)

        @block.scalar
        def _(act):
            turned(act, lambda k: uT[:, k, :], s_u, s_ute, kt=TT)
            act.wait_ge(s_sin, 80)
            act.activation(pc[STEP], pc[LS], ACT.Exp).then_inc(s_a, 1)
            act.wait_ge(s_d, 1)
            act.activation(pc[MAG], pc[T1], ACT.Exp).then_inc(s_a, 1)
            act.wait_ge(s_d, 2)
            act.activation(pc[SN], pc[R], ACT.Sin).then_inc(s_a, 1)
            act.activation(pc[SH], pc[RH], ACT.Sin).then_inc(s_a, 1)
            for q in range(TT):
                act.wait_ge(s_yq, q + 1)
                act.activation(yT[:, q, :], yq[:, :], ACT.Gelu_apprx_tanh).then_inc(s_yT, 1)

        @block.vector
        def _(dve):
            st = dve_steps.on(dve)
            dve.wait_ge(s_a, 1)
            st(dve.tensor_tensor(pc[T1], pc[A_RE], pc[STEP], ALU.mult))
            dve.sem_inc(s_d, 1)
            st(dve.tensor_tensor(pc[TH], pc[A_IM], pc[STEP], ALU.mult))
            magic, high = 1.5 * 2.0 ** 23, 6.28125
            st(dve.tensor_scalar(pc[KF], pc[TH], 1.0 / (2.0 * math.pi), magic, ALU.mult, ALU.add))
            st(dve.tensor_scalar(pc[KF], pc[KF], -magic, None, ALU.add))
            st(dve.scalar_tensor_tensor(out=pc[R], in0=pc[KF], scalar=-high, in1=pc[TH], op0=ALU.mult, op1=ALU.add))
            st(dve.scalar_tensor_tensor(out=pc[R], in0=pc[KF], scalar=-(2.0 * math.pi - high), in1=pc[R], op0=ALU.mult,
                                        op1=ALU.add))
            st(dve.tensor_scalar(pc[R], pc[R], 3.1415925, -3.1415925, ALU.min, ALU.max))
            st(dve.tensor_scalar(pc[RH], pc[R], 0.5, None, ALU.mult))
            dve.sem_inc(s_d, 1)
            dve.wait_ge(s_a, 4)
            st(dve.tensor_tensor(pc[T1], pc[SH], pc[SH], ALU.mult))
            st(dve.tensor_scalar(pc[CS], pc[T1], -2.0, 1.0, ALU.mult, ALU.add))
            st(dve.tensor_copy(pw[:, 0, 0, :], pc[CS]))
            st(dve.tensor_copy(pw[:, 0, 1, :], pc[SN]))
            for k in range(8):
                re, im = pw[:, k, 0, :], pw[:, k, 1, :]
                st(dve.tensor_tensor(pc[T1], re, re, ALU.mult))
                st(dve.tensor_tensor(pc[T2], im, im, ALU.mult))
                st(dve.tensor_tensor(pw[:, k + 1, 0, :], pc[T1], pc[T2], ALU.subtract))
                st(dve.scalar_tensor_tensor(out=pw[:, k + 1, 1, :], in0=re, scalar=2.0, in1=im, op0=ALU.mult, op1=ALU.mult))
            dve.sem_inc(s_pw, 1)
            st(dve.tensor_tensor(pc[LRE], pc[MAG], pc[CS], ALU.mult))
            st(dve.tensor_tensor(pc[LIM], pc[MAG], pc[SN], ALU.mult))
            st(dve.tensor_scalar(pc[NR], pc[LRE], -1.0, None, ALU.add))
            st(dve.tensor_tensor(pc[T1], pc[A_RE], pc[A_RE], ALU.mult))
            st(dve.tensor_tensor(pc[T2], pc[A_IM], pc[A_IM], ALU.mult))
            st(dve.tensor_tensor(pc[DEN], pc[T1], pc[T2], ALU.add))
            st(dve.reciprocal(pc[DEN], pc[DEN]))
            for dst, x1, x2, op in ((CRE, A_RE, A_IM, ALU.add), (CIM, A_IM, A_RE, ALU.subtract)):
                first, other = ((NR, A_RE), (LIM, A_IM)) if dst == CRE else ((LIM, A_RE), (NR, A_IM))
                st(dve.tensor_tensor(pc[T1], pc[first[0]], pc[first[1]], ALU.mult))
                st(dve.tensor_tensor(pc[T2], pc[other[0]], pc[other[1]], ALU.mult))
                st(dve.tensor_tensor(pc[T1], pc[T1], pc[T2], op))
                st(dve.tensor_tensor(pc[dst], pc[T1], pc[DEN], ALU.mult))
            for q in range(TT):
                dve.wait_ge(s_rot, q + 1)
                dve.wait_ge(s_cr, 16 * (q + 1))
                for j in range(4):
                    n = 4 * q + j
                    er, ei = rot[:, q % 2, 0, j, :], rot[:, q % 2, 1, j, :]
                    if q:
                        dve.wait_ge(s_yp, 4 * (q - 1) + j + 1)
                    cre, cim, tmp2 = cw_raw[:, j, 0, :], cw_raw[:, j, 1, :], f1[:, 0:P]
                    st(dve.tensor_scalar(tmp2, cim, pc[CIM][:, n:n + 1], None, ALU.mult))
                    st(dve.scalar_tensor_tensor(out=cw[:, j, 0, :], in0=cre, scalar=pc[CRE][:, n:n + 1], in1=tmp2,
                                                op0=ALU.mult, op1=ALU.subtract))
                    st(dve.tensor_scalar(tmp2, cim, pc[CRE][:, n:n + 1], -1.0, ALU.mult, ALU.mult))
                    st(dve.tensor_scalar(f2[:, 0:P], cre, pc[CIM][:, n:n + 1], None, ALU.mult))
                    st(dve.tensor_tensor(cw[:, j, 1, :], tmp2, f2[:, 0:P], ALU.subtract))
                    dve.sem_inc(s_cw, 1)
                    dve.wait_ge(s_v, n + 1)
                    vr, vi = ps[:, 2 * (j % 2), :], ps[:, 2 * (j % 2) + 1, :]
                    st(dve.tensor_tensor(f1[:, :], er, vr, ALU.mult))
                    st(dve.tensor_tensor(f2[:, :], ei, vi, ALU.mult))
                    st(dve.tensor_tensor(wre[:, :], f1[:, :], f2[:, :], ALU.add))
                    st(dve.tensor_tensor(f1[:, :], er, vi, ALU.mult))
                    st(dve.tensor_tensor(f2[:, :], ei, vr, ALU.mult))
                    dve.sem_inc(s_vu, 1)
                    st(dve.tensor_tensor(wim[:, :], f1[:, :], f2[:, :], ALU.subtract))
                    mag = pc[MAG][:, n:n + 1].to_broadcast([P, SEQ])
                    st(dve.tensor_tensor_scan(f1[:, :], mag, wre[:, :], 0.0, ALU.mult, ALU.add))
                    st(dve.tensor_tensor_scan(f2[:, :], mag, wim[:, :], 0.0, ALU.mult, ALU.add))
                    if n >= 2:
                        dve.wait_ge(s_yp, n - 1)
                    st(dve.tensor_tensor(wre[:, :], er, f1[:, :], ALU.mult))
                    st(dve.tensor_tensor(wim[:, :], ei, f2[:, :], ALU.mult))
                    st(dve.tensor_tensor(zst[:, j % 2, 0, :], wre[:, :], wim[:, :], ALU.subtract))
                    st(dve.tensor_tensor(wre[:, :], er, f2[:, :], ALU.mult))
                    st(dve.tensor_tensor(wim[:, :], ei, f1[:, :], ALU.mult))
                    st(dve.tensor_tensor(zst[:, j % 2, 1, :], wre[:, :], wim[:, :], ALU.add))
                    dve.sem_inc(s_z, 1)
                dve.sem_inc(s_rotu, 1)
                dve.wait_ge(s_yp, 4 * q + 4)
                if q:
                    dve.wait_ge(s_yT, q)
                st(dve.scalar_tensor_tensor(out=yq[:, :], in0=uT[:, q, :], scalar=d_col[:, q:q + 1], in1=ps[:, 4 + q % 2, :],
                                            op0=ALU.mult, op1=ALU.add))
                dve.sem_inc(s_yq, 1)
    stage.close()

    stage = ExitStack()
    wglu_t = sb(stage, "wglu", [P, 2, TT * CH])
    wglu = [wglu_t[:, s, :] for s in range(2)]
    zz = sb(stage, "zz", [P, 2, TT, D])
    s_ldg, s_mmg, s_bg2, s_sg2, s_mg = [sem("glu_ld0"), sem("glu_ld1")], sem("glu_mm"), sem("glu_bank"), sem("branch_gates"), sem("merge")
    with nc.Block() as block:
        @block.sync
        def _(sp):
            loads(sp, 2, lambda n: t["ssm_w_glu_2"][n, :, :], wglu, s_ldg, s_mmg)

        @block.tensor
        def _(pe):
            products(pe, 2, lambda s, k, m: yT[:, k, m * P:(m + 1) * P], lambda s, k, m, w: wglu[s][:, k * w:(k + 1) * w],
                     s_ldg, s_mmg, s_bg2, kt=TT)

        @block.scalar
        def _(act):
            for m in range(TT):
                act.activation(ug[:, m, CH:5 * CH], ug[:, m, CH:5 * CH], ACT.Sigmoid).then_inc(s_sg2, 1)
            evacuate(act, 2, s_mmg, s_bg2, lambda i, s, m, bank: act.activation(
                zz[:, s, m, ds(i * CH, CH)], bank, (ACT.Identity, ACT.Sigmoid)[s]))
            act.sem_inc(s_mg, 1)

        @block.vector
        def _(dve):
            dve_steps.on(dve)
            dve.wait_ge(s_sg2, TT)
            for m in range(TT):
                dve_steps(dve.tensor_tensor(merged[:, m, :], merged[:, m, :], ug[:, m, CH + D:CH + 2 * D], ALU.mult))
            dve.wait_ge(s_mg, 1)
            for m in range(TT):
                dve_steps(dve.tensor_tensor(zz[:, 0, m, :], zz[:, 0, m, :], zz[:, 1, m, :], ALU.mult))
                dve_steps(dve.tensor_tensor(zz[:, 0, m, :], zz[:, 0, m, :], ug[:, m, CH:CH + D], ALU.mult))
                dve_steps(dve.tensor_tensor(merged[:, m, :], merged[:, m, :], zz[:, 0, m, :], ALU.add))
    stage.close()
    ssm.close()

    mT = ExitStack()
    mixT = sb(mT, "mixT", [P, KT, SEQ])
    out_projection("mix2", merged, t["w_out_2"], mixT, None)
    mT.close()
    second.close()
    clear_semaphores()

    peer = ExitStack()
    h4T = sb(peer, "h4T", [P, KT, SEQ])
    selT = sb(peer, "selT", [P, 3, SEQ])
    g_rows = nc.dram_tensor("g_rows", [P // GROUP, P, GROUP * SEQ], F32, kind="Internal").ap()
    route = ExitStack()
    qT4 = sb(route, "qT4", [P, 2 * PH, SEQ])
    stage = ExitStack()
    gain4 = sb(stage, "gain4", [P, D])
    h4 = sb(stage, "h4", [P, TT, D])
    wbuf_t = sb(stage, "wbuf_q", [P, 2, KT * CH])
    wbuf = [wbuf_t[:, s, :] for s in range(2)]
    with nc.Block() as block:
        norm_block(block, gain4, t["ffn_norm_g_2"], None, None, (),
                   tuple(sem(f"norm4_{x}") for x in ("sums", "mean", "root", "gain", "h", "turned", "taken")), h4, h4T)
    s_ldq, s_mmq, s_bankq = [sem("query_ld0"), sem("query_ld1")], sem("query_mm"), sem("query_bank")
    with nc.Block() as block:
        @block.sync
        def _(sp):
            loads(sp, 2, lambda n: t["peer_w_query_2"][n, :, :], wbuf, s_ldq, s_mmq)

        @block.tensor
        def _(pe):
            products(pe, 2, lambda s, k, m: wbuf[s][:, k * CH + m * P:k * CH + (m + 1) * P],
                     lambda s, k, m, w: h4T[:, k, :], s_ldq, s_mmq, s_bankq)

        @block.scalar
        def _(act):
            evacuate(act, 2, s_mmq, s_bankq, lambda i, s, m, bank: act.activation(
                qT4[:, ds(i * 8 + (s * 4 + m), 1), :].rearrange("p a n -> p (a n)"), bank, ACT.Copy))
    stage.close()

    stage = ExitStack()
    keysT = sb(stage, "keysT", [P, 2 * PH, PK])
    rest = sb(stage, "rest", [P, 2 * P])
    top_s = sb(stage, "top_s", [P, 2 * PH, PT16])
    top_k = sb(stage, "top_k", [P, 2 * PH, PT16], U32)
    top_kf = sb(stage, "top_kf", [P, 2 * PH, PT16])
    pairs_s = sb(stage, "pairs_s", [P, PT16, PT16])
    best_s = sb(stage, "best_s", [P, PH, PT16])
    best_p = sb(stage, "best_p", [P, PH, PT16], U32)
    part_p = sb(stage, "part_p", [P, PH, PT16], U32)
    part_f = sb(stage, "part_f", [P, PH, PT16])
    match = sb(stage, "match", [P, PH, PT16, PT16])
    sel = sb(stage, "sel", [P, 3, PH, PT16])
    psum_g = sb(stage, "psum_g", [P, PH])
    s_key, s_scr, s_ex, s_exd, s_sel, s_selt, s_selh = (
        sem(f"peer_{x}") for x in ("keys", "scores", "shifted", "exp", "selected", "sel_turned", "sel_here"))
    with nc.Block() as block:
        @block.sync
        def _(sp):
            sp.dma_start(keysT[:, :, :], t["sub_keys_2"]).then_inc(s_key, 16)

        @block.scalar
        def _(act):
            for i in range(TT):
                act.wait_ge(s_ex, i + 1)
                act.activation(sel[:, 2, :, :], best_s[:, :, :], ACT.Exp).then_inc(s_exd, 1)
                act.wait_ge(s_selt, i + 1)
                act.activation(selT[:, :, ds(i * P, P)], ps[:, 4, 0:3 * P].rearrange("p (c n) -> p c n", c=3),
                               ACT.Copy).then_inc(s_selh, 1)
            act.wait_ge(s_selh, TT)

        @block.tensor
        def _(pe):
            pe.wait_ge(s_key, 16)
            for i in range(TT):
                if i:
                    pe.wait_ge(s_sel, i)
                for b in range(4):
                    for n in range(4):
                        mm = pe.matmul(ps[:, b, n * P:(n + 1) * P], qT4[:, 4 * b + n, i * P:(i + 1) * P], keysT[:, 4 * b + n, :],
                                       start=True, stop=True)
                    mm.then_inc(s_scr, 1)
                pe.wait_ge(s_sel, i + 1)
                for c in range(3):
                    tr = pe.transpose(ps[:, 4, c * P:(c + 1) * P], sel[:, c, :, :].rearrange("p h k -> p (h k)"), ident[:, :])
                tr.then_inc(s_selt, 1)

        @block.vector
        def _(dve):
            st = dve_steps.on(dve)

            def best16(values, scores, places, width):
                st(dve.max(scores[:, 0:8], values))
                st(dve.max_index(places[:, 0:8], scores[:, 0:8], values))
                st(dve.match_replace(rest[:, 0:width], scores[:, 0:8], values, -3.0e38))
                st(dve.max(scores[:, 8:16], rest[:, 0:width]))
                st(dve.max_index(places[:, 8:16], scores[:, 8:16], rest[:, 0:width]))

            for i in range(TT):
                for n in range(2 * PH):
                    if n % 4 == 0:
                        dve.wait_ge(s_scr, i * 4 + n // 4 + 1)
                    best16(ps[:, n // 4, (n % 4) * P:(n % 4 + 1) * P], top_s[:, n, :], top_k[:, n, :], P)
                for hd in range(PH):
                    st(dve.tensor_tensor(pairs_s[:, :, :], top_s[:, 2 * hd, :].unsqueeze(2).to_broadcast([P, PT16, PT16]),
                                         top_s[:, 2 * hd + 1, :].unsqueeze(1).to_broadcast([P, PT16, PT16]), ALU.add))
                    best16(pairs_s[:, :, :].rearrange("p a b -> p (a b)"), best_s[:, hd, :], best_p[:, hd, :], PT16 * PT16)
                st(dve.tensor_copy(psum_g[:, :], best_s[:, :, 0]))
                st(dve.tensor_tensor(best_s[:, :, :], best_s[:, :, :], psum_g[:, :].unsqueeze(2).to_broadcast([P, PH, PT16]),
                                     ALU.subtract))
                dve.sem_inc(s_ex, 1)
                st(dve.tensor_copy(top_kf[:, :, :], top_k[:, :, :]))
                halves_of = top_kf[:, :, :].rearrange("p (h c) k -> p h c k", c=2)
                for c in range(2):
                    st(dve.tensor_scalar(part_p[:, :, :], best_p[:, :, :], (4, 15)[c], None,
                                         (ALU.logical_shift_right, ALU.bitwise_and)[c]))
                    st(dve.tensor_copy(part_f[:, :, :], part_p[:, :, :]))
                    st(dve.tensor_tensor(match[:, :, :, :], part_f[:, :, :].unsqueeze(3).to_broadcast([P, PH, PT16, PT16]),
                                         iota_row[:, 0:PT16].unsqueeze(1).unsqueeze(1).to_broadcast([P, PH, PT16, PT16]),
                                         ALU.is_equal))
                    st(dve.tensor_tensor(match[:, :, :, :], match[:, :, :, :],
                                         halves_of[:, :, c, :].unsqueeze(2).to_broadcast([P, PH, PT16, PT16]), ALU.mult))
                    st(dve.tensor_reduce(sel[:, c, :, :], match[:, :, :, :], AX.X, ALU.add))
                dve.wait_ge(s_exd, i + 1)
                st(dve.tensor_reduce(psum_g[:, :], sel[:, 2, :, :], AX.X, ALU.add))
                st(dve.reciprocal(psum_g[:, :], psum_g[:, :]))
                dve.tensor_tensor(sel[:, 2, :, :], sel[:, 2, :, :], psum_g[:, :].unsqueeze(2).to_broadcast([P, PH, PT16]),
                                  ALU.mult).then_inc(s_sel, 1)
                dve.wait_ge(s_selh, i + 1)
    stage.close()
    route.close()

    stage = ExitStack()
    first_hot = sb(stage, "first_hot", [P, 2, 4, P])
    second_hot = sb(stage, "second_hot", [P, 2, 4, P])
    spread = sb(stage, "spread", [P, 2, PK, P])
    s_hot, s_gb, s_gt2, s_gst = sem("one_hots"), sem("gate_products"), sem("gates_spread"), [sem("gates_stored0"), sem("gates_stored1")]
    PAIRS = P // 8
    with nc.Block() as block:
        @block.vector
        def _(dve):
            dve_steps.on(dve)
            dve.sem_inc(s_gb, 2)
            for m in range(TT):
                with dve.Fori(0, PAIRS) as i:
                    for s in range(2):
                        dve.wait_ge(s_gb, i * 2 + (m * PAIRS * 2 + s + 1))
                        for r in range(4):
                            tok = i * 8 + (m * P + 4 * s + r)
                            dve.tensor_scalar(first_hot[:, s, r, :], iota_row[:, :], selT[:, 0, ds(tok, 1)],
                                              selT[:, 2, ds(tok, 1)], ALU.is_equal, ALU.mult).then_inc(s_hot, 1)
                            dve.tensor_scalar(second_hot[:, s, r, :], iota_row[:, :], selT[:, 1, ds(tok, 1)], None,
                                              ALU.is_equal).then_inc(s_hot, 1)

        @block.tensor
        def _(pe):
            for m in range(TT):
                with pe.Fori(0, PAIRS) as i:
                    for s in range(2):
                        pe.wait_ge(s_hot, i * 16 + (m * PAIRS * 16 + 8 * s + 8))
                        pe.wait_ge(s_gt2, i * 2 + (m * PAIRS * 2 + s + 1))
                        for r in range(4):
                            mm = pe.matmul(ps[:, s, r * P:(r + 1) * P], first_hot[:, s, r, :], second_hot[:, s, r, :],
                                           start=True, stop=True)
                        mm.then_inc(s_gb, 1)

        @block.scalar
        def _(act):
            act.sem_inc(s_gt2, 2)
            for m in range(TT):
                if m >= 2:
                    act.wait_ge(s_gst[m % 2], 16 * GROUP)
                with act.Fori(0, PAIRS) as i:
                    for s in range(2):
                        act.wait_ge(s_gb, i * 2 + (m * PAIRS * 2 + s + 3))
                        act.activation(spread[:, m % 2, :, ds(i * 8 + 4 * s, 4)].rearrange("p k n -> p n k"),
                                       ps[:, s, :].rearrange("p (n k) -> p n k", n=4), ACT.Copy).then_inc(s_gt2, 1)

        @block.sync
        def _(sp):
            for m in range(TT):
                sp.wait_ge(s_gt2, 2 + (m + 1) * PAIRS * 2)
                for j in range(GROUP):
                    sp.dma_start(g_rows.rearrange("g p (j n) -> p g j n", j=GROUP)[:, :, j, m * P:(m + 1) * P],
                                 spread[:, m % 2, :, :].rearrange("p (g j) n -> p g j n", j=GROUP)[:, :, j, :])\
                      .then_inc(s_gst[m % 2], 16)
            for s in range(2):
                sp.wait_ge(s_gst[s], 2 * 16 * GROUP)
    stage.close()

    NG = P // GROUP
    stage = ExitStack()
    u_sb = sb(stage, "u_sb", [P, 2, GROUP * D])
    v_sb = sb(stage, "v_sb", [P, 2, GROUP * D])
    g_sb = sb(stage, "g_sb", [P, 2, GROUP * SEQ])
    w_sb = sb(stage, "w_sb", [P, 2, GROUP, SEQ])
    gl = sb(stage, "gl", [P, 2, SEQ])
    s_lu, s_lv, s_lg2 = ([sem(f"peer_{x}{s}") for s in range(2)] for x in ("u", "v", "g"))
    s_pa, s_gelu, s_w, s_po, s_add, s_outd = (sem(f"peer_{x}") for x in ("dots", "gelu", "weights", "outputs", "added", "stored"))
    with nc.Block() as block:
        @block.sync
        def _(sp):
            def load(n, s, earlier):
                if earlier is not None:
                    sp.wait_ge(s_pa, earlier * GROUP)
                sp.dma_start(u_sb[:, s, :], t["peer_u_2"][n, :, :]).then_inc(s_lu[s], 16)
                if earlier is not None:
                    sp.wait_ge(s_w, earlier * GROUP + 2)
                sp.dma_start(g_sb[:, s, :], g_rows[n, :, :]).then_inc(s_lg2[s], 16)
                if earlier is not None:
                    sp.wait_ge(s_po, earlier * 8)
                sp.dma_start(v_sb[:, s, :], t["peer_v_2"][:, n, :]).then_inc(s_lv[s], 16)
            for s in range(2):
                load(s, s, None)
            with sp.Fori(1, NG // 2) as i:
                for s in range(2):
                    load(i * 2 + s, s, i * 2 + (s - 1))
            sp.wait_ge(s_add, 4 + 8 * NG)
            sp.dma_start(out.rearrange("a (m p) d -> p (a m) d", p=P), x_sb[:, :, :]).then_inc(s_outd, 16)
            sp.wait_ge(s_outd, 16)

        def in_order(eng, ahead, behind):
            ahead(0, 0)
            with eng.Fori(0, NG // 2 - 1) as i:
                ahead(i, 1)
                behind(i, 0)
                ahead(i + 1, 0)
                behind(i, 1)
            ahead(NG // 2 - 1, 1)
            behind(NG // 2 - 1, 0)
            behind(NG // 2 - 1, 1)

        @block.tensor
        def _(pe):
            def dots(i, s):
                pe.wait_ge(s_lu[s], (i + 1) * 16)
                for j in range(GROUP):
                    pe.wait_ge(s_gelu, i * 8 + (s * 4 + j + 1))
                    for k in range(KT):
                        mm = pe.matmul(ps[:, j % 2, :], u_sb[:, s, (j * KT + k) * P:(j * KT + k + 1) * P], h4T[:, k, :],
                                       start=(k == 0), stop=(k == KT - 1))
                    mm.then_inc(s_pa, 1)

            def outputs(i, s):
                pe.wait_ge(s_lv[s], (i + 1) * 16)
                pe.wait_ge(s_w, i * 8 + (s * 4 + 4 + 2))
                for n in range(8):
                    m, c = divmod(n, 2)
                    pe.wait_ge(s_add, i * 16 + (s * 8 + n + 1))
                    for j in range(GROUP):
                        mm = pe.matmul(ps[:, 2 + n % 4, :], w_sb[:, s, j, m * P:(m + 1) * P],
                                       v_sb[:, s, j * D + c * CH:j * D + (c + 1) * CH], start=(j == 0), stop=(j == GROUP - 1))
                    mm.then_inc(s_po, 1)

            in_order(pe, dots, outputs)

        @block.scalar
        def _(act):
            act.sem_inc(s_gelu, 2)
            with act.Fori(0, NG * GROUP // 2) as i:
                for s in range(2):
                    act.wait_ge(s_w, i * 2 + (s + 1))
                    act.wait_ge(s_pa, i * 2 + (s + 1))
                    act.activation(gl[:, s, :], ps[:, s, :], ACT.Gelu_apprx_tanh).then_inc(s_gelu, 1)

        @block.vector
        def _(dve):
            def weights(i, s):
                dve.wait_ge(s_lg2[s], (i + 1) * 16)
                for j in range(GROUP):
                    dve.wait_ge(s_gelu, i * 8 + (s * 4 + j + 3))
                    dve.tensor_tensor(w_sb[:, s, j, :], gl[:, j % 2, :], g_sb[:, s, j * SEQ:(j + 1) * SEQ],
                                      ALU.mult).then_inc(s_w, 1)

            def add(i, s):
                for n in range(8):
                    m, c = divmod(n, 2)
                    dve.wait_ge(s_po, i * 16 + (s * 8 + n + 1))
                    xs = x_sb[:, m, c * CH:(c + 1) * CH]
                    dve.tensor_tensor(xs, ps[:, 2 + n % 4, :], xs, ALU.add).then_inc(s_add, 1)

            dve.sem_inc(s_w, 2)
            dve.sem_inc(s_add, 4)
            in_order(dve, weights, add)
    stage.close()
    peer.close()
    clear_semaphores()


def chunks(w, n=512):
    k, cols = w.shape[-2:]
    lead = w.shape[:-2]
    a = w.reshape(*lead, k // 128, 128, cols // n, n)
    nd = len(lead)
    a = a.transpose(*range(nd), nd + 2, nd + 1, nd, nd + 3)
    return np.ascontiguousarray(a.reshape(*lead, cols // n, 128, (k // 128) * n))

def state_tiles(b, stationary_in):
    parts, groups, states, width = b.shape
    per = 128 // states
    out = np.zeros((4, 4, parts, 128, 128), b.dtype)
    for g in range(groups):
        n, r = divmod(g, per)
        q, j = divmod(n, 4)
        f = (g * width) % 128
        for c in range(parts):
            out[q, j, c, f:f + width, r * states:(r + 1) * states] = b[c, g].T
    if stationary_in:
        return np.ascontiguousarray(out.transpose(0, 3, 1, 2, 4))
    return np.ascontiguousarray(out.transpose(0, 4, 1, 2, 3))

def lay_out(i):
    A = {}
    one = lambda n: np.ascontiguousarray(i[n][0])
    for n in ('b_ada','norm1_g','a_q_norm_g','a_k_norm_g','b_q_norm_g','b_k_norm_g','lambda_q1','lambda_k1','lambda_q2',
              'lambda_k2','diff_norm_g','norm2_g','b_router','b_gate_up','b_down','mix_norm_g_2','fox_forget_bias_2',
              'q_norm_g_2','k_norm_g_2','ffn_norm_g_2'):
        A[n] = one(n)
    A['x'] = i['x']
    A['c'] = np.ascontiguousarray(i['c'].reshape(8,128).T)
    for n in ('w_ada','w_in','w_out','w_gate_up','w_down','w_out_2','peer_w_query_2'):
        A[n] = chunks(i[n][0])
    A['w_router'] = chunks(i['w_router'][0], 32)[0]
    w = i['w_in_2'][0]
    A['w_qkv_2'] = chunks(w[:, 512:3584])
    A['w_f_2'] = chunks(w[:, 3584:3592], 8)[0]
    A['w_ug_2'] = chunks(np.concatenate([w[:, :512], w[:, 3592:]], 1))
    A['ssm_w_glu_2'] = np.ascontiguousarray(chunks(i['ssm_w_glu_2'][0])[[0, 2, 1, 3]])
    A['ssm_a_re_2'] = np.ascontiguousarray(i['ssm_a_re_2'][0].reshape(16,128).T)
    A['ssm_a_im_2'] = np.ascontiguousarray(i['ssm_a_im_2'][0].reshape(16,128).T)
    A['ssm_log_step_2'] = np.ascontiguousarray(i['ssm_log_step_2'][0].reshape(16,2).T)
    A['ssm_d_2'] = np.ascontiguousarray(i['ssm_d_2'][0].reshape(4,128).T)
    A['ssm_b_2'] = state_tiles(np.stack([i['ssm_b_re_2'][0], i['ssm_b_im_2'][0]]), True)
    A['ssm_c_2'] = state_tiles(np.stack([i['ssm_c_re_2'][0], i['ssm_c_im_2'][0]]).transpose(0,1,3,2), False)
    A['sub_keys_2'] = np.ascontiguousarray(i['peer_sub_keys_2'][0].reshape(16,128,128).transpose(2,0,1))
    u = i['peer_u_2'][0].reshape(128, 32, 4, 8, 128)
    A['peer_u_2'] = np.ascontiguousarray(u.transpose(1, 4, 2, 3, 0).reshape(32, 128, 4 * 8 * 128))
    A['peer_v_2'] = np.ascontiguousarray(i['peer_v_2'][0].reshape(128, 32, 4 * 1024))
    return A


def kernel(**inputs):
    import concourse.bacc as bacc
    from concourse.bass_utils import run_bass_kernel_spmd

    nc = bacc.Bacc("TRN2", target_bir_lowering=False, num_devices=1)
    arrays = {f"in_{name}": a for name, a in lay_out({k: np.asarray(v) for k, v in inputs.items()}).items()}
    t = {name[3:]: nc.dram_tensor(name, a.shape, mybir.dt.from_np(a.dtype), kind="ExternalInput").ap()
         for name, a in arrays.items()}
    out = nc.dram_tensor("out_0_dram", (1, SEQ, D), F32, kind="ExternalOutput").ap()
    build_program(nc, t, out)
    r = run_bass_kernel_spmd(nc, [arrays], core_ids=[0])
    return r.results[0]["out_0_dram"]
```

```python
import math
from contextlib import ExitStack

import numpy as np

import concourse.bass as bass
from concourse import mybir

F32 = mybir.dt.float32
BF16 = mybir.dt.bfloat16
F32R = mybir.dt.float32r
I32 = mybir.dt.int32
U32 = mybir.dt.uint32
ALU = mybir.AluOpType
ACT = mybir.ActivationFunctionType
AX = mybir.AxisListType
ds = bass.ds

P = 128
SEQ = 512
TT = SEQ // P
D = 1024
KT = D // P
CH = 512
EPS = 1e-6
MASKED = -1.0e30
HD = 64
LAMBDA_INIT = 0.8 - 0.6 * math.exp(-0.3 * 0)
NE, TOPK = 32, 4
DFF = 1024
NBLK = (SEQ * TOPK + NE * (P - 1)) // P + 1
SWIGLU_LIMIT, SWIGLU_ALPHA = 7.0, 1.702
SSM_W, SSM_G, SSM_H, SSM_N = 512, 32, 16, 64
ST = SSM_G * SSM_N // P
FH, FHD = 8, 128
PH, PK, PT16 = 8, 128, 16
SEL = PH * PT16
GROUP = 2


class Steps:

    def __init__(self, sem):
        self.sem, self.n, self.i, self.per = sem, 0, None, 0

    def on(self, eng):
        self.eng = eng
        return self

    def __call__(self, ins):
        ins.then_inc(self.sem, 1)
        self.n += 1
        at = self.n if self.i is None else self.base + self.i * self.per + (self.n - self.base)
        wait(self.eng, self.sem, at)

    def loop(self, i, per):
        self.i, self.per, self.base = i, per, self.n

    def end(self, count):
        assert self.n - self.base == self.per, f"the body has {self.n - self.base} steps, not {self.per}"
        self.n, self.i = self.base + self.per * count, None


def wait(eng, sem, value):
    eng.wait_ge(sem, value)


def build_program(nc, t, out):
    with ExitStack() as ctx:
        emit(nc, t, out, ctx)


def emit(nc, t, out, ctx):
    era = []

    def sem(name):
        stack = ctx.enter_context(ExitStack())
        s = stack.enter_context(nc.semaphore(name))
        era.append((stack, s))
        return s

    def clear_semaphores():
        with nc.Block() as block:
            @block.gpsimd
            def _(pool):
                for _, s in era:
                    pool.sem_clear(s)
        for stack, _ in era:
            stack.close()
        era.clear()

    def sb(stack, name, shape, dt=F32):
        return stack.enter_context(nc.sbuf_tensor(name, shape, dt))

    ps = ctx.enter_context(nc.psum_tensor("ps", [P, 8, CH], F32))
    dve_steps, act_steps, pool_steps = Steps(sem("dve_steps")), Steps(sem("act_steps")), Steps(sem("pool_steps"))
    era.clear()
    x_sb = sb(ctx, "x_sb", [P, TT, D])
    ident = sb(ctx, "ident", [P, P])
    ones = sb(ctx, "ones", [P, P])
    tri_before = sb(ctx, "tri_before", [P, P])
    tri_upto = sb(ctx, "tri_upto", [P, P])
    iota_row = sb(ctx, "iota_row", [P, P])
    small = sb(ctx, "small", [P, 64])

    def loads(sp, pairs, src, wbuf, s_ld, s_mm, last=()):
        for s in range(2):
            sp.dma_start(wbuf[s], src(s)).then_inc(s_ld[s], 16)
        if pairs > 1:
            with sp.Fori(1, pairs) as i:
                for s in range(2):
                    sp.wait_ge(s_mm, (i * 2 + (s - 1)) * TT)
                    sp.dma_start(wbuf[s], src(i * 2 + s)).then_inc(s_ld[s], 16)
        for s, (chunk, width) in enumerate(last):
            sp.wait_ge(s_mm, (pairs * 2 + s - 1) * TT)
            sp.dma_start(wbuf[s][:, 0:KT * width], chunk).then_inc(s_ld[s], 16)

    def products(pe, pairs, lhs, rhs, s_ld, s_mm, s_bank, kt=KT, last=()):
        def one(i, s, width):
            pe.wait_ge(s_ld[s], (i + 1) * 16)
            for m in range(4):
                pe.wait_ge(s_bank, (i * 2 + s) * 4 + m + 1)
                for k in range(kt):
                    mm = pe.matmul(ps[:, m, 0:width], lhs(s, k, m), rhs(s, k, m, width), start=(k == 0), stop=(k == kt - 1))
                mm.then_inc(s_mm, 1)

        with pe.Fori(0, pairs) as i:
            for s in range(2):
                one(i, s, CH)
        for s, (_, width) in enumerate(last):
            one(pairs, s, width)

    def evacuate(eng, pairs, s_mm, s_bank, op, last=()):
        def one(i, s, width):
            for m in range(4):
                eng.wait_ge(s_mm, (i * 2 + s) * 4 + m + 1)
                op(i, s, m, ps[:, m, 0:width]).then_inc(s_bank, 1)

        eng.sem_inc(s_bank, 4)
        with eng.Fori(0, pairs) as i:
            for s in range(2):
                one(i, s, CH)
        for s, (_, width) in enumerate(last):
            one(pairs, s, width)
        eng.wait_ge(s_bank, 4 + 4 * (2 * pairs + len(last)))

    def three(pe, out, l_hi, l_lo, r_hi, r_lo, first, last):
        pe.matmul(out, l_hi, r_hi, start=first, stop=False)
        pe.matmul(out, l_hi, r_lo, start=False, stop=False)
        return pe.matmul(out, l_lo, r_hi, start=False, stop=last)

    def turn(pe, src, s_done, s_taken, kt=KT, banks=(4, 5), at=0):
        for k in range(kt):
            if k >= 2:
                pe.wait_ge(s_taken, at + k - 1)
            for m in range(TT):
                tr = pe.transpose(ps[:, banks[k % 2], m * P:(m + 1) * P], src(m, k), ident[:, :])
            tr.then_inc(s_done, 1)

    def turned(act, dst, s_done, s_taken, kt=KT, banks=(4, 5), at=0):
        for k in range(kt):
            act.wait_ge(s_done, at + k + 1)
            act.activation(dst(k), ps[:, banks[k % 2], :], ACT.Copy).then_inc(s_taken, 1)

    def square_sums(act, src, junk, ss, s_ss):
        for m in range(TT):
            act_steps(act.activation(junk[:, :], src[:, m, :], ACT.Square, accum_out=ss[:, m:m + 1]))
        act.sem_inc(s_ss, 1)

    def inverse_root(dve, mean, root, tmp, s_root):
        dve.wait_ge(*s_root)
        dve_steps(dve.reciprocal(root, root))
        dve_steps(dve.tensor_tensor(tmp, root, root, ALU.mult))
        dve_steps(dve.tensor_tensor(tmp, tmp, mean, ALU.mult))
        dve_steps(dve.tensor_scalar(tmp, tmp, -0.5, 1.5, ALU.mult, ALU.add))
        dve_steps(dve.tensor_tensor(mean, root, tmp, ALU.mult))

    def attention(block, name, heads, dq, dv, scale, load, bias_of, diag_mask, v_of, o_dst, extra_tensors):
        st = extra_tensors
        turn_src = st["turn_src"]
        L = len(turn_src)
        qn, kn, qT, kT, S, Pm, PT, nmax, den = (st[k] for k in ("qn", "kn", "qT", "kT", "S", "Pm", "PT", "nmax", "den"))
        s_n, s_t, s_qk, s_sc, s_max, s_p, s_pt, s_pte, s_pv, s_o = (
            sem(f"{name}_{x}") for x in ("normed", "turned", "qk_here", "scores", "max", "probs", "probs_turned",
                                         "probs_t_here", "values", "heads"))

        def pipeline(eng, scores_of, output_of):
            scores_of(0)
            with eng.Fori(0, heads - 1) as i:
                scores_of(i + 1)
                output_of(i)
            output_of(heads - 1)

        @block.gpsimd
        def _(pool):
            pool_steps.on(pool)
            pool.sem_inc(s_t, L)
            with pool.Fori(0, heads) as i:
                pool_steps.loop(i, 4)
                pool.wait_ge(s_t, i * L + L)
                load(pool, i, qn, kn)
                pool.sem_inc(s_n, 1)
            pool_steps.end(heads)

        @block.vector
        def _(dve):
            def scores_of(i):
                bias = bias_of(dve, i)
                for q in range(TT):
                    K = (q + 1) * P
                    dve.wait_ge(s_p, i * TT + (q + 1))
                    dve.wait_ge(s_sc, i * TT + (q + 1))
                    dve_steps(dve.scalar_tensor_tensor(out=S[:, q, 0:K], in0=ps[:, q, 0:K], scalar=scale,
                                                       in1=bias(q), op0=ALU.mult, op1=ALU.add))
                    if diag_mask is not None:
                        dve_steps(dve.tensor_tensor(S[:, q, q * P:K], S[:, q, q * P:K], diag_mask, ALU.add))
                    dve.tensor_reduce(nmax[:, q:q + 1], S[:, q, 0:K], AX.X, ALU.max, negate=True).then_inc(s_max, 1)

            def output_of(i):
                dve.wait_ge(s_p, i * TT + (TT + TT))
                dve_steps(dve.reciprocal(den[:, :], den[:, :]))
                dve.wait_ge(s_pv, i * TT + TT)
                dve_steps(dve.tensor_tensor(o_dst(i), ps[:, 6, 0:TT * dv].rearrange("p (q d) -> p q d", q=TT),
                                            den[:, :].unsqueeze(2).to_broadcast([P, TT, dv]), ALU.mult))
                dve.sem_inc(s_o, 1)

            dve_steps.on(dve)
            dve.sem_inc(s_max, TT)
            dve.sem_inc(s_p, TT)
            dve.sem_inc(s_o, 1)
            scores_of(0)
            with dve.Fori(0, heads - 1) as i:
                dve_steps.loop(i, st["steps"])
                scores_of(i + 1)
                output_of(i)
            dve_steps.end(heads - 1)
            output_of(heads - 1)

        @block.tensor
        def _(pe):
            def scores_of(i):
                pe.wait_ge(s_max, i * TT + TT)
                pe.wait_ge(s_n, i + 1)
                for bank, src in enumerate(turn_src):
                    for m in range(TT):
                        tr = pe.transpose(ps[:, bank, m * P:(m + 1) * P], src[:, m, :], ident[:, :])
                    tr.then_inc(s_t, 1)
                pe.wait_ge(s_qk, i * 2 + 2)
                for q in range(TT):
                    K = (q + 1) * P
                    pe.matmul(ps[:, q, 0:K], qT[:, q * P:K], kT[:, 0:K], start=True, stop=True).then_inc(s_sc, 1)

            def output_of(i):
                def turn_probs(q):
                    pe.wait_ge(s_p, i * TT + (TT + q + 1))
                    if q >= 2:
                        pe.wait_ge(s_pte, i * TT + (q - 1))
                    for b in range(q + 1):
                        tr = pe.transpose(ps[:, 4 + q % 2, b * P:(b + 1) * P], Pm[:, q, b * P:(b + 1) * P], ident[:, :])
                    tr.then_inc(s_pt, 1)

                turn_probs(0)
                for q in range(TT):
                    if q + 1 < TT:
                        turn_probs(q + 1)
                    if q == 0:
                        pe.wait_ge(s_o, i + 1)
                    pe.wait_ge(s_pte, i * TT + (q + 1))
                    for b in range(q + 1):
                        mm = pe.matmul(ps[:, 6, q * dv:(q + 1) * dv], PT[:, q % 2, b, :], v_of(i, b),
                                       start=(b == 0), stop=(b == q))
                    mm.then_inc(s_pv, 1)

            pipeline(pe, scores_of, output_of)

        @block.scalar
        def _(act):
            def scores_of(i):
                for n, dst in enumerate((qT, kT)):
                    bank = n % L
                    act.wait_ge(s_t, i * L + (L + bank + 1))
                    lo = n * dq % P
                    act.activation(dst[:, :], ps[lo:lo + dq, bank, :], ACT.Copy).then_inc(s_qk, 1)

            def output_of(i):
                act.wait_ge(s_o, i + 1)
                for q in range(TT):
                    act.wait_ge(s_max, i * TT + (TT + q + 1))
                    act.activation(Pm[:, q, 0:(q + 1) * P], S[:, q, 0:(q + 1) * P], ACT.Exp, bias=nmax[:, q:q + 1],
                                   accum_out=den[:, q:q + 1]).then_inc(s_p, 1)
                for q in range(TT):
                    act.wait_ge(s_pt, i * TT + (q + 1))
                    act.activation(PT[:, q % 2, 0:q + 1, :],
                                   ps[:, 4 + q % 2, 0:(q + 1) * P].rearrange("p (b n) -> p b n", n=P),
                                   ACT.Copy).then_inc(s_pte, 1)

            pipeline(act, scores_of, output_of)

    first = ctx.enter_context(ExitStack())
    mod = sb(first, "mod", [P, 6 * D])
    att = ExitStack()
    negdist = sb(att, "negdist", [P, SEQ])
    mask_a = sb(att, "mask_a", [P, SEQ])
    mask_b = sb(att, "mask_b", [P, SEQ])
    slopes = sb(att, "slopes", [P, 16])
    dist_i = sb(att, "dist_i", [P, SEQ], I32)
    dist_j = sb(att, "dist_j", [P, SEQ], I32)
    scratch = sb(att, "scratch", [P, SEQ])
    proj = sb(att, "proj", [P, TT, 3 * D])
    hT = sb(att, "hT", [P, KT, SEQ])
    o_mix = sb(att, "o_mix", [P, TT, D])
    s_const, s_mask = sem("constants"), sem("masks")
    s_mod_in, s_cast, s_x, s_ld_a, s_mm_a, s_bank_a = (
        sem("mod_inputs"), sem("silu_here"), sem("x_here"), [sem("ada_ld0"), sem("ada_ld1")], sem("ada_mm"), sem("ada_bank"))
    stage = ExitStack()
    wbuf_t = sb(stage, "wbuf_ada", [P, 2, KT * CH])
    wbuf = [wbuf_t[:, s, :] for s in range(2)]
    c_col = sb(stage, "c_col", [P, KT])
    c_rep = sb(stage, "c_rep", [P, KT, P])
    s_sig = sem("sigmoid_c")
    with nc.Block() as block:
        @block.gpsimd
        def _(pool):
            pool_steps.on(pool)
            pool_steps(pool.memset(ident[:, :], 0.0))
            pool_steps(pool.affine_select(out=ident[:, :], in_=ident[:, :], compare_op=ALU.not_equal, fill=1.0, base=0,
                                          pattern=[[-1, P]], channel_multiplier=1))
            pool_steps(pool.memset(ones[:, :], 1.0))
            pool.affine_select(out=tri_before[:, :], in_=ones[:, :], compare_op=ALU.is_gt, fill=0.0, base=0,
                               pattern=[[1, P]], channel_multiplier=-1).then_inc(s_const, 1)
            pool.affine_select(out=tri_upto[:, :], in_=ones[:, :], compare_op=ALU.is_ge, fill=0.0, base=0,
                               pattern=[[1, P]], channel_multiplier=-1).then_inc(s_const, 1)
            pool.iota(iota_row[:, :], [[1, P]], base=0, channel_multiplier=0,
                      allow_small_or_imprecise_dtypes=True).then_inc(s_const, 1)
            pool.iota(negdist[:, :], [[1, SEQ]], base=-(SEQ - P), channel_multiplier=-1,
                      allow_small_or_imprecise_dtypes=True).then_inc(s_const, 1)
            pool.iota(dist_i[:, :], [[-1, SEQ]], base=SEQ - P, channel_multiplier=1).then_inc(s_const, 1)
            pool_steps(pool.memset(mask_b[:, :], 0.0))
            pool.affine_select(out=mask_b[:, :], in_=mask_b[:, :], compare_op=ALU.is_ge, fill=MASKED, base=SEQ - P,
                               pattern=[[-1, SEQ]], channel_multiplier=1).then_inc(s_const, 1)
            for h in range(8):
                pool.memset(slopes[:, h:h + 1], 2.0 ** -(h + 1.0)).then_inc(s_const, 1)
                pool.memset(slopes[:, 8 + h:9 + h], 2.0 ** (-2.0 * (h // 2 + 1))).then_inc(s_const, 1)
            pool.wait_ge(s_mask, 1)
            pool.affine_select(out=mask_a[:, :], in_=mask_a[:, :], compare_op=ALU.is_ge, fill=MASKED, base=SEQ - P,
                               pattern=[[-1, SEQ]], channel_multiplier=1).then_inc(s_const, 1)
            pool.wait_ge(s_const, 23)

        @block.sync
        def _(sp):
            sp.dma_start(c_col[:, :], t["c"]).then_inc(s_mod_in, 16)
            sp.dma_start(mod[:, :], t["b_ada"].partition_broadcast(P)).then_inc(s_cast, 16)
            sp.dma_start(x_sb[:, :, :], t["x"].rearrange("a (m p) d -> p (a m) d", p=P)).then_inc(s_x, 16)
            loads(sp, 6, lambda n: t["w_ada"][n, :, :], wbuf, s_ld_a, s_mm_a)
            sp.wait_ge(s_x, 16)

        @block.scalar
        def _(act):
            act.wait_ge(s_mod_in, 16)
            act.activation(small[:, 0:KT], c_col[:, :], ACT.Sigmoid).then_inc(s_sig, 1)

        @block.vector
        def _(dve):
            dve_steps.on(dve)
            dve.wait_ge(s_sig, 1)
            dve_steps(dve.tensor_tensor(c_col[:, :], c_col[:, :], small[:, 0:KT], ALU.mult))
            dve.wait_ge(s_const, 3)
            for k in range(KT):
                dve_steps(dve.tensor_scalar(c_rep[:, k, :], ones[:, :], c_col[:, k:k + 1], None, ALU.mult))
            dve.sem_inc(s_sig, 1)
            dve.wait_ge(s_const, 5)
            dve_steps(dve.tensor_scalar(mask_a[:, :], dist_i[:, :], float(P), None, ALU.is_le))
            for dil in (4, 16):
                dve_steps(dve.tensor_scalar(dist_j[:, :], dist_i[:, :], dil - 1, None, ALU.bitwise_and))
                dve_steps(dve.tensor_scalar(scratch[:, :], dist_j[:, :], 0.0, None, ALU.is_equal))
                dve_steps(dve.tensor_tensor(mask_a[:, :], mask_a[:, :], scratch[:, :], ALU.add))
            dve_steps(dve.tensor_copy(scratch[:, :], mask_a[:, :]))
            dve_steps(dve.tensor_scalar(mask_a[:, :], scratch[:, :], 0.0, MASKED, ALU.is_equal, ALU.mult))
            for n in (2, 3):
                dve_steps(dve.tensor_scalar(dist_j[:, :].bitcast(F32), scratch[:, :], float(n), math.log(n), ALU.is_equal, ALU.mult))
                dve_steps(dve.tensor_tensor(mask_a[:, :], mask_a[:, :], dist_j[:, :].bitcast(F32), ALU.add))
            dve.sem_inc(s_mask, 1)
            dve.wait_ge(s_cast, 16)

            def add_bias(n, m, bank):
                return dve.tensor_tensor(mod[:, ds(n * CH, CH)], bank, mod[:, ds(n * CH, CH)], ALU.add)
            dve.sem_inc(s_bank_a, 1)
            with dve.Fori(0, 6) as i:
                for s in range(2):
                    wait(dve, s_mm_a, (i * 2 + s + 1) * TT)
                    add_bias(i * 2 + s, 0, ps[:, 0, :]).then_inc(s_bank_a, 1)
            dve.wait_ge(s_bank_a, 13)

        @block.tensor
        def _(pe):
            pe.wait_ge(s_sig, 2)
            with pe.Fori(0, 6) as i:
                for s in range(2):
                    pe.wait_ge(s_ld_a[s], (i + 1) * 16)
                    pe.wait_ge(s_bank_a, i * 2 + s + 1)
                    for k in range(KT):
                        mm = pe.matmul(ps[:, 0, :], c_rep[:, k, :], wbuf[s][:, k * CH:(k + 1) * CH],
                                       start=(k == 0), stop=(k == KT - 1))
                    mm.then_inc(s_mm_a, TT)
    stage.close()

    stage = ExitStack()
    wbuf_t = sb(stage, "wbuf_in", [P, 2, KT * CH])
    wbuf = [wbuf_t[:, s, :] for s in range(2)]
    h = sb(stage, "h", [P, TT, D])
    gain = sb(stage, "gain", [P, D])
    s_ss, s_root, s_g, s_h, s_tp, s_tpe = (sem(f"norm1_{x}") for x in ("sums", "root", "gain", "h", "turned", "taken"))
    s_ld_p, s_mm_p, s_bank_p = [sem("in_ld0"), sem("in_ld1")], sem("in_mm"), sem("in_bank")
    rms = small[:, 8:12]
    root, tmp = small[:, 12:16], small[:, 16:20]
    s_sq = sem("norm1_mean")

    def norm_block(block, gain, g_src, scale_at, shift_at, parts, sems, hh, hTT):
        s_ss, s_sq, s_root, s_g, s_h, s_tp, s_tpe = sems

        @block.sync
        def _(sp):
            sp.dma_start(gain[:, :], g_src.partition_broadcast(P)).then_inc(s_g, 16)
            for n, (pairs, w_src, dst, wb, (s_ld, s_mm, s_bank), last) in enumerate(parts):
                if n:
                    sp.wait_ge(parts[n - 1][4][1], TT * (2 * parts[n - 1][0] + len(parts[n - 1][5])))
                loads(sp, pairs, w_src, wb, s_ld, s_mm, last)

        @block.scalar
        def _(act):
            act_steps.on(act)
            square_sums(act, x_sb, hh[:, 0, :], small[:, 8:12], s_ss)
            act.wait_ge(s_sq, 1)
            act.activation(root, rms, ACT.Sqrt).then_inc(s_root, 1)
            turned(act, lambda k: hTT[:, k, :], s_tp, s_tpe)
            for pairs, w_src, dst, wb, (s_ld, s_mm, s_bank), last in parts:
                evacuate(act, pairs, s_mm, s_bank, lambda i, s, m, bank: act.activation(dst(i, s, m, bank.shape[1]), bank, ACT.Copy),
                         last)

        @block.vector
        def _(dve):
            dve_steps.on(dve)
            dve.wait_ge(s_g, 16)
            if scale_at is not None:
                dve_steps(dve.scalar_tensor_tensor(out=gain[:, :], in0=mod[:, scale_at:scale_at + D], scalar=1.0,
                                                   in1=gain[:, :], op0=ALU.add, op1=ALU.mult))
            dve.wait_ge(s_ss, 1)
            dve_steps(dve.tensor_scalar(rms, rms, 1.0 / D, EPS, ALU.mult, ALU.add))
            dve.sem_inc(s_sq, 1)
            inverse_root(dve, rms, root, tmp, (s_root, 1))
            for m in range(TT):
                dve_steps(dve.scalar_tensor_tensor(out=hh[:, m, :], in0=x_sb[:, m, :], scalar=rms[:, m:m + 1],
                                                   in1=gain[:, :], op0=ALU.mult, op1=ALU.mult))
                if shift_at is not None:
                    dve_steps(dve.tensor_tensor(hh[:, m, :], hh[:, m, :], mod[:, shift_at:shift_at + D], ALU.add))
            dve.sem_inc(s_h, 1)

        @block.tensor
        def _(pe):
            pe.wait_ge(s_h, 1)
            turn(pe, lambda m, k: hh[:, m, k * P:(k + 1) * P], s_tp, s_tpe)
            pe.wait_ge(s_tpe, KT)
            for pairs, w_src, dst, wb, (s_ld, s_mm, s_bank), last in parts:
                products(pe, pairs, lambda s, k, m: hTT[:, k, m * P:(m + 1) * P],
                         lambda s, k, m, w: wb[s][:, k * w:(k + 1) * w], s_ld, s_mm, s_bank, last=last)

    with nc.Block() as block:
        norm_block(block, gain, t["norm1_g"], D, 0,
                   [(3, lambda n: t["w_in"][n, :, :], lambda i, s, m, w: proj[:, m, ds((i * 2 + s) * CH, w)], wbuf,
                     (s_ld_p, s_mm_p, s_bank_p), ())],
                   (s_ss, s_sq, s_root, s_g, s_h, s_tp, s_tpe), h, hT)
    stage.close()

    stage = ExitStack()
    gains = sb(stage, "gains", [P, 4, HD])
    lam_in = sb(stage, "lam_in", [P, 4, HD])
    sq = sb(stage, "sq", [P, TT, SEQ])
    rn = sb(stage, "rn", [P, 4, TT, 8])
    rt = sb(stage, "rt", [P, 4, TT, 8])
    rtmp = sb(stage, "rtmp", [P, 4, TT, 8])
    o_b = sb(stage, "o_b", [P, TT, 8, 2 * HD])
    bias_t = sb(stage, "bias_t", [P, SEQ])
    qk = sb(stage, "qk", [P, TT, 2 * HD])
    tens = dict(qn=qk[:, :, 0:HD], kn=qk[:, :, HD:2 * HD], turn_src=(qk,), qT=sb(stage, "qT", [HD, SEQ]),
                kT=sb(stage, "kT", [HD, SEQ]), S=sb(stage, "S", [P, TT, SEQ]), Pm=sb(stage, "Pm", [P, TT, SEQ]),
                PT=sb(stage, "PT", [P, 2, TT, P]), nmax=sb(stage, "nmax", [P, TT]), den=sb(stage, "den", [P, TT]),
                steps=1 + TT + 2)
    s_gn, s_sqd, s_red, s_rt, s_e = (sem(f"heads_{x}") for x in ("gains", "squared", "reduced", "roots", "lambda_exp"))
    kinds = (0, SEQ, 3 * SEQ, 4 * SEQ)
    with nc.Block() as block:
        @block.sync
        def _(sp):
            for n, g in enumerate(("a_q_norm_g", "a_k_norm_g", "b_q_norm_g", "b_k_norm_g")):
                sp.dma_start(gains[:, n, :], t[g].partition_broadcast(P)).then_inc(s_gn, 16)
            for n, g in enumerate(("lambda_q1", "lambda_k1", "lambda_q2", "lambda_k2")):
                sp.dma_start(lam_in[:, n, :], t[g].partition_broadcast(P)).then_inc(s_gn, 16)

        @block.scalar
        def _(act):
            act_steps.on(act)
            for n, at in enumerate(kinds):
                if n:
                    act.wait_ge(s_red, n)
                act.activation(sq[:, :, :], proj[:, :, at:at + SEQ], ACT.Square).then_inc(s_sqd, 1)
            act.wait_ge(s_red, 5)
            act.activation(rt[:, :, :, :], rn[:, :, :, :], ACT.Sqrt).then_inc(s_rt, 1)
            act.wait_ge(s_e, 1)
            act.activation(small[:, 20:22], small[:, 20:22], ACT.Exp).then_inc(s_e, 1)

        @block.vector
        def _(dve):
            dve_steps.on(dve)
            for n in range(4):
                dve.wait_ge(s_sqd, n + 1)
                dve.tensor_reduce(rn[:, n, :, :], sq[:, :, :].rearrange("p m (h d) -> p m h d", d=HD), AX.X,
                                  ALU.add).then_inc(s_red, 1)
            dve.wait_ge(s_red, 4)
            dve.tensor_scalar(rn[:, :, :, :], rn[:, :, :, :], 1.0 / HD, EPS, ALU.mult, ALU.add).then_inc(s_red, 1)
            dve.wait_ge(s_red, 5)
            inverse_root(dve, rn[:, :, :, :], rt[:, :, :, :], rtmp[:, :, :, :], (s_rt, 1))
            dve.wait_ge(s_gn, 8 * 16)
            for n in range(2):
                dve_steps(dve.tensor_tensor(lam_in[:, 2 * n, :], lam_in[:, 2 * n, :], lam_in[:, 2 * n + 1, :], ALU.mult))
                dve_steps(dve.tensor_reduce(small[:, 20 + n:21 + n], lam_in[:, 2 * n, :], AX.X, ALU.add))
            dve.sem_inc(s_e, 1)
            dve.wait_ge(s_e, 2)
            dve_steps(dve.scalar_tensor_tensor(out=small[:, 22:23], in0=small[:, 21:22], scalar=-LAMBDA_INIT,
                                               in1=small[:, 20:21], op0=ALU.add, op1=ALU.subtract))

    def load_heads(q_at, k_at, kind):
        def load(pool, i, qn, kn):
            for dst, at, n in ((qn, q_at, kind), (kn, k_at, kind + 1)):
                pool_steps(pool.tensor_tensor(dst[:, :, :], proj[:, :, ds(i * HD + at, HD)],
                                            rn[:, n, :, ds(i, 1)].to_broadcast([P, TT, HD]), ALU.mult))
                pool_steps(pool.tensor_tensor(dst[:, :, :], dst[:, :, :],
                                            gains[:, n, :].unsqueeze(1).to_broadcast([P, TT, HD]), ALU.mult))
        return load

    def alibi(slope_at, mask):
        def bias_of(dve, i):
            dve_steps(dve.scalar_tensor_tensor(out=bias_t[:, :], in0=negdist[:, :], scalar=slopes[:, ds(i + slope_at, 1)],
                                               in1=mask[:, :], op0=ALU.mult, op1=ALU.add))
            return lambda q: bias_t[:, (TT - 1 - q) * P:SEQ]
        return bias_of

    with nc.Block() as block:
        attention(block, "dilated", 8, HD, HD, HD ** -0.5, load_heads(kinds[0], kinds[1], 0), alibi(0, mask_a), None,
                  lambda i, b: proj[:, b, ds(i * HD + 2 * SEQ, HD)], lambda i: o_mix[:, :, ds(i * HD, HD)], tens)
    with nc.Block() as block:
        vb = proj[:, :, 5 * SEQ:6 * SEQ]
        attention(block, "differential", 8, HD, 2 * HD, HD ** -0.5, load_heads(kinds[2], kinds[3], 2), alibi(8, mask_b), None,
                  lambda i, b: proj[:, b, ds((i // 2) * 2 * HD + 5 * SEQ, 2 * HD)], lambda i: o_b[:, :, ds(i, 1), :].rearrange("p m h d -> p m (h d)"), tens)
    s_bd, s_bs, s_br, s_bg = sem("diff_sum"), sem("diff_mean"), sem("diff_root"), sem("diff_gain")
    with nc.Block() as block:
        pairs_b = o_b[:, :, :, :].rearrange("p m (h c) d -> p m h c d", c=2)
        diff_g = gains[:, 0:2, :].rearrange("p a d -> p (a d)")
        ob_out = o_mix[:, :, SEQ:D].rearrange("p m (h d) -> p m h d", h=4)

        @block.sync
        def _(sp):
            sp.dma_start(diff_g, t["diff_norm_g"].partition_broadcast(P)).then_inc(s_bg, 16)

        @block.scalar
        def _(act):
            act.wait_ge(s_bd, 1)
            act.activation(sq[:, :, :], o_mix[:, :, SEQ:D], ACT.Square).then_inc(s_bd, 1)
            act.wait_ge(s_bs, 1)
            act.activation(small[:, 40:56], small[:, 24:40], ACT.Sqrt).then_inc(s_br, 1)

        @block.vector
        def _(dve):
            dve_steps.on(dve)
            for m in range(TT):
                dve_steps(dve.scalar_tensor_tensor(out=ob_out[:, m, :, :], in0=pairs_b[:, m, :, 1, :], scalar=small[:, 22:23],
                                                   in1=pairs_b[:, m, :, 0, :], op0=ALU.mult, op1=ALU.add))
            dve.sem_inc(s_bd, 1)
            dve.wait_ge(s_bd, 2)
            mean = small[:, 24:40]
            dve_steps(dve.tensor_reduce(mean.rearrange("p (m h) -> p m h", h=4), sq[:, :, :].rearrange("p m (h d) -> p m h d", h=4), AX.X, ALU.add))
            dve_steps(dve.tensor_scalar(mean, mean, 1.0 / P, EPS, ALU.mult, ALU.add))
            dve.sem_inc(s_bs, 1)
            inverse_root(dve, mean, small[:, 40:56], rtmp[:, 0, 0:2, :].rearrange("p a b -> p (a b)"), (s_br, 1))
            dve.wait_ge(s_bg, 16)
            dve_steps(dve.tensor_scalar(diff_g, diff_g, 1.0 - LAMBDA_INIT, None, ALU.mult))
            for m in range(TT):
                dve_steps(dve.tensor_tensor(ob_out[:, m, :, :], ob_out[:, m, :, :],
                                            mean[:, 4 * m:4 * m + 4].unsqueeze(2).to_broadcast([P, 4, P]), ALU.mult))
                dve_steps(dve.tensor_tensor(ob_out[:, m, :, :], ob_out[:, m, :, :],
                                            diff_g.unsqueeze(1).to_broadcast([P, 4, P]), ALU.mult))
    stage.close()

    def out_projection(name, src, w, dst_T, gate_at):
        stage = ExitStack()
        wbuf_t = sb(stage, f"wbuf_{name}", [P, 2, KT * CH])
        scr = sb(stage, f"scr_{name}", [P, CH])
        wb = [wbuf_t[:, s, :] for s in range(2)]
        s_tp, s_tpe, s_mm, s_bank = (sem(f"{name}_{x}") for x in ("turned", "taken", "mm", "bank"))
        s_ld = [sem(f"{name}_ld0"), sem(f"{name}_ld1")]
        with nc.Block() as block:
            @block.sync
            def _(sp):
                loads(sp, 1, lambda n: w[n, :, :], wb, s_ld, s_mm)

            @block.scalar
            def _(act):
                turned(act, lambda k: dst_T[:, k, :], s_tp, s_tpe)

            @block.tensor
            def _(pe):
                turn(pe, lambda m, k: src[:, m, k * P:(k + 1) * P], s_tp, s_tpe)
                pe.wait_ge(s_tpe, KT)
                products(pe, 1, lambda s, k, m: dst_T[:, k, m * P:(m + 1) * P],
                         lambda s, k, m, w: wb[s][:, k * w:(k + 1) * w], s_ld, s_mm, s_bank)

            @block.vector
            def _(dve):
                dve_steps.on(dve)
                dve.sem_inc(s_bank, 4)
                for n in range(2):
                    for m in range(TT):
                        dve.wait_ge(s_mm, n * TT + m + 1)
                        xs = x_sb[:, m, n * CH:(n + 1) * CH]
                        if gate_at is None:
                            dve.tensor_tensor(xs, ps[:, m, :], xs, ALU.add).then_inc(s_bank, 1)
                        else:
                            dve_steps(dve.tensor_tensor(scr[:, :], ps[:, m, :], mod[:, gate_at + n * CH:gate_at + (n + 1) * CH],
                                                        ALU.mult))
                            dve.sem_inc(s_bank, 1)
                            dve_steps(dve.tensor_tensor(xs, xs, scr[:, :], ALU.add))
        stage.close()

    out_projection("mix", o_mix, t["w_out"], hT, 2 * D)
    att.close()

    moe = ExitStack()
    gate = sb(moe, "gate", [P, TT, TOPK])
    gate_all = sb(moe, "gate_all", [P, TT, NE])
    dest_i = sb(moe, "dest_i", [P, TOPK, TT], I32)
    slot_ids = sb(moe, "slot_ids", [P, NBLK + 1], I32)
    blk_f = sb(moe, "blk_f", [P, NBLK])
    blk_i = sb(moe, "blk_i", [P, NBLK], I32)
    used_i = sb(moe, "used_i", [P, 1], I32)
    h_rows = nc.dram_tensor("h_rows", [SEQ, D], F32, kind="Internal").ap()
    slot_rows = nc.dram_tensor("slot_rows", [P * NBLK, 1], I32, kind="Internal").ap()
    y_rows = nc.dram_tensor("y_rows", [NBLK * P, D], F32, kind="Internal").ap()
    route = ExitStack()
    gain2 = sb(route, "gain2", [P, D])
    h2 = sb(route, "h2", [P, TT, D])
    h2T = sb(route, "h2T", [P, KT, SEQ])
    with nc.Block() as block:
        norm_block(block, gain2, t["norm2_g"], 4 * D, 3 * D, (),
                   tuple(sem(f"norm2_{x}") for x in ("sums", "mean", "root", "gain", "h", "turned", "taken")),
                   h2, h2T)

    wr = sb(route, "wr", [P, KT * NE])
    br = sb(route, "br", [P, NE])
    logits = sb(route, "logits", [P, TT, NE])
    top_v = sb(route, "top_v", [P, TT, 8])
    top_i = sb(route, "top_i", [P, TT, 8], U32)
    top_f = sb(route, "top_f", [P, TT, TOPK])
    gsum = sb(route, "gsum", [P, TT])
    onehot = sb(route, "onehot", [P, TOPK, TT, NE])
    rtmp4 = sb(route, "rtmp4", [P, TT, NE])
    chosen = sb(route, "chosen", [P, TT, NE])
    count = sb(route, "count", [P, NE])
    nblocks = sb(route, "nblocks", [P, NE])
    ends = sb(route, "ends", [P, NE])
    starts = sb(route, "starts", [P, NE])
    slot_f = sb(route, "slot_f", [P, TT, NE])
    dest_f = sb(route, "dest_f", [P, TOPK, TT])
    place_i = sb(route, "place_i", [P, TOPK, TT], I32)
    place_j = sb(route, "place_j", [P, TOPK, TT], I32)
    token_i = sb(route, "token_i", [P, TT], I32)
    zero_i = sb(route, "zero_i", [P, NBLK], I32)
    past = sb(route, "past", [P, NBLK, NE])
    s_rin, s_hst, s_lg, s_gd, s_ge, s_ch, s_pos, s_pl, s_tok, s_zero, s_sc, s_ids, s_tz = (
        sem(f"route_{x}") for x in ("inputs", "h_stored", "logits", "gate_diff", "gate_exp", "chosen", "positions", "places",
                                    "token_ids", "zeroed", "scattered", "slots_here", "zeros"))
    with nc.Block() as block:
        @block.sync
        def _(sp):
            sp.dma_start(wr[:, :], t["w_router"]).then_inc(s_rin, 16)
            sp.dma_start(br[:, :], t["b_router"].partition_broadcast(P)).then_inc(s_rin, 16)
            sp.dma_start(h_rows.rearrange("(m p) d -> p m d", p=P), h2[:, :, :]).then_inc(s_hst, 16)
            sp.wait_ge(s_tz, 1)
            sp.dma_start(slot_rows.rearrange("(p j) o -> p (j o)", p=P), zero_i[:, :]).then_inc(s_zero, 16)
            sp.wait_ge(s_hst, 16)
            sp.wait_ge(s_sc, 16 * TOPK * TT)
            sp.dma_start(slot_ids[:, 0:NBLK], slot_rows.rearrange("(p j) o -> p (j o)", p=P)).then_inc(s_ids, 16)
            sp.wait_ge(s_ids, 16)

        @block.gpsimd
        def _(pool):
            pool.memset(zero_i[:, :], 0).then_inc(s_tz, 1)
            pool.iota(token_i[:, :], [[P, TT]], base=0, channel_multiplier=1).then_inc(s_tok, 1)
            pool.wait_ge(s_tok, 1)
            pool.wait_ge(s_zero, 16)
            pool.wait_ge(s_pl, 1)
            for k in range(TOPK):
                for m in range(TT):
                    pool.indirect_dma_start(slot_rows, bass.IndirectOffsetOnAxis(ap=place_i[:, k, m:m + 1], axis=0),
                                            token_i[:, m:m + 1], None).then_inc(s_sc, 16)

        @block.tensor
        def _(pe):
            pe.wait_ge(s_rin, 32)
            for m in range(TT):
                for k in range(KT):
                    mm = pe.matmul(ps[:, 0, m * NE:(m + 1) * NE], h2T[:, k, m * P:(m + 1) * P], wr[:, k * NE:(k + 1) * NE],
                                   start=(k == 0), stop=(k == KT - 1))
            mm.then_inc(s_lg, 1)
            pe.wait_ge(s_ch, 1)
            for m in range(TT):
                for n in range(m + 1):
                    pe.matmul(ps[:, 1, m * NE:(m + 1) * NE], (tri_before if n == m else ones)[:, :], chosen[:, n, :],
                              start=(n == 0), stop=(n == m))
            for n in range(TT):
                mm = pe.matmul(ps[:, 1, TT * NE:(TT + 1) * NE], ones[:, :], chosen[:, n, :], start=(n == 0), stop=(n == TT - 1))
            mm.then_inc(s_pos, 1)

        @block.scalar
        def _(act):
            act.wait_ge(s_gd, 1)
            act.activation(gate[:, :, :], gate[:, :, :], ACT.Exp).then_inc(s_ge, 1)

        @block.vector
        def _(dve):
            dve_steps.on(dve)
            dve.wait_ge(s_lg, 1)
            dve_steps(dve.tensor_tensor(logits[:, :, :], ps[:, 0, 0:TT * NE].rearrange("p (m e) -> p m e", e=NE),
                                        br[:, :].unsqueeze(1).to_broadcast([P, TT, NE]), ALU.add))
            for m in range(TT):
                dve_steps(dve.max(top_v[:, m, :], logits[:, m, :]))
                dve_steps(dve.max_index(top_i[:, m, :], top_v[:, m, :], logits[:, m, :]))
            dve_steps(dve.tensor_tensor(gate[:, :, :], top_v[:, :, 0:TOPK], top_v[:, :, 0:1].to_broadcast([P, TT, TOPK]),
                                        ALU.subtract))
            dve.sem_inc(s_gd, 1)
            dve_steps(dve.tensor_copy(top_f[:, :, :], top_i[:, :, 0:TOPK]))
            for k in range(TOPK):
                dve_steps(dve.tensor_tensor(onehot[:, k, :, :], iota_row[:, 0:NE].unsqueeze(1).to_broadcast([P, TT, NE]),
                                            top_f[:, :, k:k + 1].to_broadcast([P, TT, NE]), ALU.is_equal))
            dve_steps(dve.tensor_tensor(chosen[:, :, :], onehot[:, 0, :, :], onehot[:, 1, :, :], ALU.add))
            dve_steps(dve.tensor_tensor(chosen[:, :, :], chosen[:, :, :], onehot[:, 2, :, :], ALU.add))
            dve.tensor_tensor(chosen[:, :, :], chosen[:, :, :], onehot[:, 3, :, :], ALU.add).then_inc(s_ch, 1)
            dve.wait_ge(s_ge, 1)
            dve_steps(dve.tensor_reduce(gsum[:, :], gate[:, :, :], AX.X, ALU.add))
            dve_steps(dve.reciprocal(gsum[:, :], gsum[:, :]))
            dve_steps(dve.tensor_tensor(gate[:, :, :], gate[:, :, :], gsum[:, :].unsqueeze(2).to_broadcast([P, TT, TOPK]),
                                        ALU.mult))
            for k in range(TOPK):
                dst = gate_all if k == 0 else rtmp4
                dve_steps(dve.tensor_tensor(dst[:, :, :], onehot[:, k, :, :], gate[:, :, k:k + 1].to_broadcast([P, TT, NE]),
                                            ALU.mult))
                if k:
                    dve_steps(dve.tensor_tensor(gate_all[:, :, :], gate_all[:, :, :], rtmp4[:, :, :], ALU.add))
            dve.wait_ge(s_pos, 1)
            dve_steps(dve.tensor_copy(count[:, :], ps[:, 1, TT * NE:(TT + 1) * NE]))
            dve_steps(dve.tensor_scalar(nblocks[:, :], count[:, :], 0.0, None, ALU.is_gt))
            for n in range(1, TT):
                dve_steps(dve.tensor_scalar(starts[:, :], count[:, :], float(n * P), None, ALU.is_gt))
                dve_steps(dve.tensor_tensor(nblocks[:, :], nblocks[:, :], starts[:, :], ALU.add))
            dve_steps(dve.tensor_tensor_scan(ends[:, :], ones[:, 0:NE], nblocks[:, :], 0.0, ALU.mult, ALU.add))
            dve_steps(dve.tensor_tensor(starts[:, :], ends[:, :], nblocks[:, :], ALU.subtract))
            dve_steps(dve.tensor_scalar(starts[:, :], starts[:, :], float(P), None, ALU.mult))
            dve_steps(dve.tensor_tensor(slot_f[:, :, :], ps[:, 1, 0:TT * NE].rearrange("p (m e) -> p m e", e=NE),
                                        starts[:, :].unsqueeze(1).to_broadcast([P, TT, NE]), ALU.add))
            for k in range(TOPK):
                dve_steps(dve.tensor_tensor(rtmp4[:, :, :], onehot[:, k, :, :], slot_f[:, :, :], ALU.mult))
                dve_steps(dve.tensor_reduce(dest_f[:, k, :], rtmp4[:, :, :], AX.X, ALU.add))
            dve_steps(dve.tensor_copy(dest_i[:, :, :], dest_f[:, :, :]))
            dve_steps(dve.tensor_scalar(place_j[:, :, :], dest_i[:, :, :], 7, None, ALU.arith_shift_right))
            dve_steps(dve.tensor_scalar(place_i[:, :, :], dest_i[:, :, :], P - 1, None, ALU.bitwise_and))
            dve_steps(dve.tensor_scalar(place_i[:, :, :], place_i[:, :, :], float(NBLK), None, ALU.mult))
            dve_steps(dve.tensor_tensor(place_i[:, :, :], place_i[:, :, :], place_j[:, :, :], ALU.add))
            dve.sem_inc(s_pl, 1)
            dve_steps(dve.tensor_tensor(past[:, :, :], iota_row[:, 0:NBLK].unsqueeze(2).to_broadcast([P, NBLK, NE]),
                                        ends[:, :].unsqueeze(1).to_broadcast([P, NBLK, NE]), ALU.is_ge))
            dve_steps(dve.tensor_reduce(blk_f[:, :], past[:, :, :], AX.X, ALU.add))
            dve_steps(dve.tensor_scalar(blk_f[:, :], blk_f[:, :], float(NE - 1), None, ALU.min))
            dve_steps(dve.tensor_copy(blk_i[:, :], blk_f[:, :]))
            dve_steps(dve.tensor_copy(used_i[:, :], ends[:, NE - 1:NE]))
    route.close()

    stage = ExitStack()
    HW = KT // 2 * CH
    RAW, SPLIT, AHEAD, UNITS = 6, 3, 3, 12
    w_raw = sb(stage, "w_raw", [P, RAW, HW])
    w_hi, w_lo = (sb(stage, f"w_{x}", [P, SPLIT, HW], F32R) for x in ("high", "low"))
    b_f = sb(stage, "b_f", [96, 2 * DFF])
    b_part = sb(stage, "b_part", [96, 2 * DFF], BF16)
    row_f = sb(stage, "row_f", [P, 1])
    pick = sb(stage, "pick", [96, P], BF16)
    cur = sb(stage, "cur", [P, 1], I32)
    xe = sb(stage, "xe", [P, D])
    xT_hi, xT_lo = (sb(stage, f"xT_{x}", [P, 2, 4 * P], F32R) for x in ("high", "low"))
    gm = sb(stage, "gm", [P, CH])
    sg = sb(stage, "sg", [P, CH])
    um = sb(stage, "um", [P, CH])
    hid = sb(stage, "hid", [P, 2, CH])
    hidT_hi, hidT_lo = (sb(stage, f"hidT_{x}", [P, 2, 4 * P], F32R) for x in ("high", "low"))
    zero_y = sb(stage, "zero_y", [P, D])
    y_sb = sb(stage, "y_sb", [P, D])
    s_raw = [sem(f"expert_w{r}") for r in range(RAW)]
    s_st, s_zst = sem("y_stored"), sem("zeros_stored")
    (s_zy, s_ga, s_bl, s_bp, s_wh, s_wl, s_used, s_xt, s_xh, s_xl, s_gm, s_sg, s_act, s_at, s_hh, s_hl, s_y, s_pick, s_rowf,
     s_cur, s_es) = (sem(f"expert_{x}") for x in (
         "zero_rows", "rows_here", "bias_here", "bias_parts", "w_high", "w_low", "w_used", "x_turned", "x_high", "x_low",
         "gate_clamped", "sigmoid", "hidden", "hid_turned", "hid_high", "hid_low", "y_here", "picked", "row_ids", "cur",
         "steps"))
    halves = (0, 2, 1, 3)
    with nc.Block() as block:
        @block.gpsimd
        def _(pool):
            def gather(j):
                pool.wait_ge(s_xt, j * 2 + 2)
                pool.tensor_copy(cur[:, :], slot_ids[:, ds(j, 1)]).then_inc(s_cur, 1)
                pool.wait_ge(s_cur, 1)
                pool.sem_clear(s_cur)
                pool.indirect_dma_start(xe[:, :], None, h_rows,
                                        bass.IndirectOffsetOnAxis(ap=cur[:, :], axis=0)).then_inc(s_ga, 16)

            pool.sem_inc(s_xt, 2)
            gather(0)
            for q in range(3):
                pool.iota(row_f[32 * q:32 * q + 32, :], [[1, 1]], base=0, channel_multiplier=1,
                          allow_small_or_imprecise_dtypes=True).then_inc(s_rowf, 1)
            pool.wait_ge(s_rowf, 3)
            pool.memset(zero_y[:, :], 0.0).then_inc(s_zy, 1)
            pool.wait_ge(s_zy, 1)
            used = pool.value_load(used_i[0:1, 0:1], min_val=1, max_val=NBLK - 1)
            with pool.Fori(0, NBLK - 1) as j:
                with pool.If(j < used):
                    gather(j + 1)

        @block.sync
        def _(sp):
            def load(j, e, n):
                sp.wait_ge(s_wl, j * UNITS + n + 1)
                if n < 8:
                    src = t["w_gate_up"][e, halves[n // 2], :, (n % 2) * HW:(n % 2 + 1) * HW]
                else:
                    src = t["w_down"][e, n % 2, :, (n // 2 - 4) * HW:(n // 2 - 3) * HW]
                sp.dma_start(w_raw[:, n % RAW, :], src).then_inc(s_raw[n % RAW], 16)

            sp.sem_inc(s_wl, RAW)
            used = sp.value_load(used_i[0:1, 0:1], min_val=1, max_val=NBLK - 1)
            e = sp.value_load(blk_i[0:1, 0:1], min_val=0, max_val=NE - 1)
            for n in range(AHEAD):
                load(0, e, n)
            for q in range(3):
                sp.dma_start(b_f[32 * q:32 * q + 32, :], t["b_gate_up"]).then_inc(s_bl, 16)
            with sp.Fori(0, NBLK - 1) as j:
                with sp.If(j < used):
                    e = sp.value_load(blk_i[0:1, ds(j, 1)], min_val=0, max_val=NE - 1)
                    for n in range(AHEAD, UNITS):
                        load(j, e, n)
                    e = sp.value_load(blk_i[0:1, ds(j + 1, 1)], min_val=0, max_val=NE - 1)
                    for n in range(AHEAD):
                        load(j + 1, e, n)

        @block.tensor
        def _(pe):
            def turn_rows(j):
                pe.wait_ge(s_ga, (j + 1) * 16)
                for half in range(2):
                    for n in range(4):
                        k = half * 4 + n
                        tr = pe.transpose(ps[:, half, n * P:(n + 1) * P], xe[:, k * P:(k + 1) * P], ident[:, :])
                    tr.then_inc(s_xt, 1)

            pe.sem_inc(s_used, SPLIT)
            turn_rows(0)
            pe.wait_ge(s_bp, 1)
            used = pe.value_load(used_i[0:1, 0:1], min_val=1, max_val=NBLK - 1)
            with pe.Fori(0, NBLK - 1) as j:
                with pe.If(j < used):
                    def unit(n, bank, lhs, half, first, last):
                        pe.wait_ge(s_wl, j * UNITS + (RAW + n + 1))
                        for k in range(4):
                            tile = slice(k * P, (k + 1) * P)
                            mm = three(pe, ps[:, bank, :], lhs[0][:, half, tile], lhs[1][:, half, tile],
                                       w_hi[:, n % SPLIT, k * CH:(k + 1) * CH], w_lo[:, n % SPLIT, k * CH:(k + 1) * CH],
                                       first and k == 0, last and k == 3)
                        return mm

                    def gate_up(c):
                        bank = halves[c]
                        unit(2 * c, bank, (xT_hi, xT_lo), 0, True, False).then_inc(s_used, 1)
                        unit(2 * c + 1, bank, (xT_hi, xT_lo), 1, False, False)
                        if c == 0:
                            pe.wait_ge(s_pick, j + 1)
                        pe.matmul(ps[:, bank, :], pick[:, :], b_part[:, bank * CH:(bank + 1) * CH],
                                  start=False, stop=True).then_inc(s_used, 1)

                    def turn_hidden(half):
                        pe.wait_ge(s_act, j * 2 + half + 2)
                        for n in range(4):
                            tr = pe.transpose(ps[:, 4 + half, n * P:(n + 1) * P], hid[:, half, n * P:(n + 1) * P],
                                              ident[:, :])
                        tr.then_inc(s_at, 1)

                    def down(half):
                        pe.wait_ge(s_hl, j * 2 + half + 1)
                        for c in range(2):
                            if half == 0:
                                pe.wait_ge(s_y, j * 2 + c + 1)
                            unit(8 + 2 * half + c, 6 + c, (hidT_hi, hidT_lo), half, half == 0, half == 1).then_inc(s_used, 1)

                    pe.wait_ge(s_xl, j * 2 + 2)
                    gate_up(0)
                    gate_up(1)
                    gate_up(2)
                    turn_hidden(0)
                    gate_up(3)
                    down(0)
                    turn_hidden(1)
                    turn_rows(j + 1)
                    down(1)

        @block.scalar
        def _(act):
            def high(j, n):
                act.wait_ge(s_raw[n % RAW], (j * 2 + (n // RAW + 1)) * 16)
                act.wait_ge(s_used, j * UNITS + n + 1)
                act.activation(w_hi[:, n % SPLIT, :], w_raw[:, n % RAW, :], ACT.Copy).then_inc(s_wh, 1)

            def rows_high(j):
                for half in range(2):
                    act.wait_ge(s_xt, j * 2 + 2 + half + 1)
                    act.activation(xT_hi[:, half, :], ps[:, half, :], ACT.Copy).then_inc(s_xh, 1)

            for n in range(AHEAD):
                high(0, n)
            rows_high(0)
            act.wait_ge(s_zy, 1)
            act.sem_inc(s_st, 16)
            act.sem_inc(s_y, 2)

            def store_before(j):
                act.wait_ge(s_st, j * 16)
                for c in range(2):
                    act.wait_ge(s_used, j * UNITS + (SPLIT + c - 1))
                    act.activation(y_sb[:, c * CH:(c + 1) * CH], ps[:, 6 + c, :], ACT.Copy).then_inc(s_y, 1)
                act.wait_ge(s_y, j * 2 + 2)
                act.dma_start(y_rows[ds((j - 1) * P, P), :], y_sb[:, :]).then_inc(s_st, 16)

            def sigmoid(j, half):
                act.wait_ge(s_gm, j * 2 + half + 1)
                act.activation(sg[:, :], gm[:, :], ACT.Sigmoid, scale=SWIGLU_ALPHA).then_inc(s_sg, 1)

            def hidden_high(j, half):
                act.wait_ge(s_at, j * 2 + half + 1)
                act.activation(hidT_hi[:, half, :], ps[:, 4 + half, :], ACT.Copy).then_inc(s_hh, 1)

            def body(j, first):
                high(j, 3)
                high(j, 4)
                sigmoid(j, 0)
                high(j, 5)
                if not first:
                    store_before(j)
                high(j, 6)
                high(j, 7)
                hidden_high(j, 0)
                high(j, 8)
                sigmoid(j, 1)
                high(j, 9)
                high(j, 10)
                high(j, 11)
                hidden_high(j, 1)
                high(j + 1, 0)
                rows_high(j + 1)
                high(j + 1, 1)
                high(j + 1, 2)

            body(0, True)
            used = act.value_load(used_i[0:1, 0:1], min_val=1, max_val=NBLK - 1)
            act.sem_inc(s_zst, 16)
            with act.Fori(1, NBLK) as j:
                with act.If(j < used):
                    body(j, False)
                    act.sem_inc(s_zst, 16)
                with act.If(used <= j):
                    act.dma_start(y_rows[ds(j * P, P), :], zero_y[:, :]).then_inc(s_zst, 16)
            store_before(used)
            act.wait_ge(s_st, used * 16 + 16)
            act.sem_inc(s_zst, 16)
            act.wait_ge(s_zst, NBLK * 16 + 16)

        @block.vector
        def _(dve):
            def low(j, n):
                dve.wait_ge(s_wh, j * UNITS + n + 1)
                dve.tensor_tensor(w_lo[:, n % SPLIT, :], w_raw[:, n % RAW, :], w_hi[:, n % SPLIT, :].bitcast(F32),
                                  ALU.subtract).then_inc(s_wl, 1)

            def rows_low(j):
                for half in range(2):
                    dve.wait_ge(s_xh, j * 2 + half + 1)
                    dve.tensor_tensor(xT_lo[:, half, :], ps[:, half, :], xT_hi[:, half, :].bitcast(F32),
                                      ALU.subtract).then_inc(s_xl, 1)

            dve_steps.on(dve)
            for n in range(AHEAD):
                low(0, n)
            rows_low(0)
            dve.wait_ge(s_bl, 48)
            dve.wait_ge(s_rowf, 3)
            dve_steps(dve.tensor_copy(b_part[:, :], b_f[:, :]))
            for at in (32, 64):
                for lo in range(at, 96, 32):
                    dve_steps(dve.tensor_tensor(b_f[lo:lo + 32, :], b_f[lo:lo + 32, :], b_part[lo:lo + 32, :], ALU.subtract))
                    dve_steps(dve.tensor_copy(b_part[lo:lo + 32, :], b_f[lo:lo + 32, :]))
            dve.sem_inc(s_bp, 1)
            dve.sem_inc(s_act, 1)
            used = dve.value_load(used_i[0:1, 0:1], min_val=1, max_val=NBLK - 1)
            with dve.Fori(0, NBLK - 1) as j:
                with dve.If(j < used):
                    def clamp_gate(half):
                        dve.wait_ge(s_act, j * 2 + half + 1)
                        dve.wait_ge(s_used, j * UNITS + (SPLIT + 4 * half + 2))
                        dve.tensor_scalar(gm[:, :], ps[:, half, :], SWIGLU_LIMIT, None, ALU.min).then_inc(s_gm, 1)

                    def gate_times_sigmoid(half):
                        dve.wait_ge(s_sg, j * 2 + half + 1)
                        dve.tensor_tensor(gm[:, :], gm[:, :], sg[:, :], ALU.mult).then_inc(s_es, 1)

                    def hidden(half):
                        dve.wait_ge(s_used, j * UNITS + (SPLIT + 4 * half + 4))
                        dve.tensor_scalar(um[:, :], ps[:, 2 + half, :], SWIGLU_LIMIT, -SWIGLU_LIMIT, ALU.min,
                                          ALU.max).then_inc(s_es, 1)
                        dve.wait_ge(s_es, j * 4 + half * 2 + 2)
                        dve.scalar_tensor_tensor(out=hid[:, half, :], in0=um[:, :], scalar=1.0, in1=gm[:, :],
                                                 op0=ALU.add, op1=ALU.mult).then_inc(s_act, 1)

                    def hidden_low(half):
                        dve.wait_ge(s_hh, j * 2 + half + 1)
                        dve.tensor_tensor(hidT_lo[:, half, :], ps[:, 4 + half, :], hidT_hi[:, half, :].bitcast(F32),
                                          ALU.subtract).then_inc(s_hl, 1)

                    dve.tensor_scalar(pick[:, :], row_f[0:96, :].to_broadcast([96, P]), blk_f[0:96, ds(j, 1)], None,
                                      ALU.is_equal).then_inc(s_pick, 1)
                    low(j, 3)
                    clamp_gate(0)
                    low(j, 4)
                    gate_times_sigmoid(0)
                    low(j, 5)
                    hidden(0)
                    low(j, 6)
                    low(j, 7)
                    clamp_gate(1)
                    hidden_low(0)
                    low(j, 8)
                    gate_times_sigmoid(1)
                    low(j, 9)
                    hidden(1)
                    low(j, 10)
                    low(j, 11)
                    hidden_low(1)
                    low(j + 1, 0)
                    rows_low(j + 1)
                    low(j + 1, 1)
                    low(j + 1, 2)
    stage.close()

    stage = ExitStack()
    yk = sb(stage, "yk", [P, 4, D])
    acc = sb(stage, "acc", [P, D])
    b_dn = sb(stage, "b_dn", [NE, D])
    gT = sb(stage, "gT", [NE, SEQ])
    s_yg = [sem(f"y_rows{k}") for k in range(4)]
    s_bd2, s_gt, s_gte, s_bias, s_yu = (sem(f"combine_{x}") for x in ("bias_here", "gates_turned", "gates_here", "bias", "used"))
    with nc.Block() as block:
        @block.sync
        def _(sp):
            sp.dma_start(b_dn[:, :], t["b_down"]).then_inc(s_bd2, 16)

        @block.gpsimd
        def _(pool):
            for m in range(TT):
                for k in range(TOPK):
                    if m:
                        pool.wait_ge(s_yu, (m - 1) * TOPK + k + 1)
                    pool.indirect_dma_start(yk[:, k, :], None, y_rows,
                                            bass.IndirectOffsetOnAxis(ap=dest_i[:, k, m:m + 1], axis=0)).then_inc(s_yg[k], 16)

        @block.tensor
        def _(pe):
            for m in range(TT):
                tr = pe.transpose(ps[0:NE, 7, m * P:(m + 1) * P], gate_all[:, m, :], ident[:, :])
            tr.then_inc(s_gt, 1)
            pe.wait_ge(s_gte, 1)
            pe.wait_ge(s_bd2, 16)
            for m in range(TT):
                for c in range(2):
                    mm = pe.matmul(ps[:, 2 * m + c, :], gT[:, m * P:(m + 1) * P], b_dn[:, c * CH:(c + 1) * CH],
                                   start=True, stop=True)
                mm.then_inc(s_bias, 1)

        @block.scalar
        def _(act):
            act.wait_ge(s_gt, 1)
            act.activation(gT[:, :], ps[0:NE, 7, :], ACT.Copy).then_inc(s_gte, 1)

        @block.vector
        def _(dve):
            dve_steps.on(dve)
            for m in range(TT):
                dve.wait_ge(s_bias, m + 1)
                for k in range(TOPK):
                    dve.wait_ge(s_yg[k], 16 * (m + 1))
                    other = ps[:, 2 * m:2 * m + 2, :].rearrange("p a n -> p (a n)") if k == 0 else acc[:, :]
                    dve_steps(dve.scalar_tensor_tensor(out=acc[:, :], in0=yk[:, k, :], scalar=gate[:, m, k:k + 1], in1=other,
                                                       op0=ALU.mult, op1=ALU.add))
                    dve.sem_inc(s_yu, 1)
                dve_steps(dve.tensor_tensor(acc[:, :], acc[:, :], mod[:, 5 * D:6 * D], ALU.mult))
                dve_steps(dve.tensor_tensor(x_sb[:, m, :], x_sb[:, m, :], acc[:, :], ALU.add))
    stage.close()
    moe.close()
    first.close()
    clear_semaphores()

    second = ExitStack()
    merged = sb(second, "merged", [P, TT, D])
    ug = sb(second, "ug", [P, TT, 5 * CH])
    fox = ExitStack()
    bias_f = sb(fox, "bias_f", [P, FH, SEQ])
    qkv = sb(fox, "qkv", [P, TT, 3 * D])
    f_log = sb(fox, "f_log", [P, TT, FH])
    stage = ExitStack()
    wbuf_t = sb(stage, "wbuf_in2", [P, 2, KT * CH])
    wbuf = [wbuf_t[:, s, :] for s in range(2)]
    h3T = sb(stage, "h3T", [P, KT, SEQ])
    h3 = bias_f[:, :, :].rearrange("p h t -> p (h t)").rearrange("p (m d) -> p m d", m=TT)
    gain3 = sb(stage, "gain3", [P, D])
    with nc.Block() as block:
        norm_block(block, gain3, t["mix_norm_g_2"], None, None,
                   [(3, lambda n: t["w_qkv_2"][n, :, :], lambda i, s, m, w: qkv[:, m, ds((i * 2 + s) * CH, w)], wbuf,
                     ([sem("qkv_ld0"), sem("qkv_ld1")], sem("qkv_mm"), sem("qkv_bank")), ()),
                    (2, lambda n: t["w_ug_2"][n, :, :],
                     lambda i, s, m, w: f_log[:, m, :] if w == FH else ug[:, m, ds((i * 2 + s) * CH, w)], wbuf,
                     ([sem("ug_ld0"), sem("ug_ld1")], sem("ug_mm"), sem("ug_bank")),
                     ((t["w_ug_2"][4, :, :], CH), (t["w_f_2"], FH)))],
                   tuple(sem(f"norm3_{x}") for x in ("sums", "mean", "root", "gain", "h", "turned", "taken")), h3, h3T)
    stage.close()

    prep = ExitStack()
    f_bias = sb(fox, "f_bias", [P, FH])
    f_abs = sb(fox, "f_abs", [P, TT, FH])
    neg_cum = sb(fox, "neg_cum", [P, TT, FH])
    cumT = sb(fox, "cumT", [FH, SEQ])
    head_row = sb(fox, "head_row", [FH, FH, P])
    diag = sb(fox, "diag", [P, P])
    fgain = sb(fox, "fgain", [P, 2, FHD])
    frn = sb(fox, "frn", [P, 2, TT, FH])
    frt = sb(fox, "frt", [P, 2, TT, FH])
    frtmp = sb(fox, "frtmp", [P, 2, TT, FH])
    fsq = sb(prep, "fsq", [P, TT, D])
    s_fin, s_fc, s_fe, s_fl, s_fcum, s_fn, s_ft, s_fte, s_fb, s_fbe, s_fs, s_fr, s_frt, s_fz = (
        sem(f"forget_{x}") for x in ("inputs", "consts", "abs", "logs", "cum", "neg_cum", "turned", "cum_here", "bias", "bias_here",
                                     "squared", "reduced", "roots", "first"))
    with nc.Block() as block:
        @block.sync
        def _(sp):
            sp.dma_start(f_bias[:, :], t["fox_forget_bias_2"].partition_broadcast(P)).then_inc(s_fin, 16)
            sp.dma_start(fgain[:, 0, :], t["q_norm_g_2"].partition_broadcast(P)).then_inc(s_fin, 16)
            sp.dma_start(fgain[:, 1, :], t["k_norm_g_2"].partition_broadcast(P)).then_inc(s_fin, 16)

        @block.gpsimd
        def _(pool):
            pool_steps.on(pool)
            pool_steps(pool.memset(head_row[:, :, :], 0.0))
            pool_steps(pool.affine_select(out=head_row[:, :, :], in_=head_row[:, :, :], compare_op=ALU.not_equal, fill=1.0, base=0,
                                          pattern=[[-1, FH], [0, P]], channel_multiplier=1))
            pool_steps(pool.memset(diag[:, :], 0.0))
            pool_steps(pool.affine_select(out=diag[:, :], in_=diag[:, :], compare_op=ALU.is_ge, fill=MASKED, base=0,
                                          pattern=[[-1, P]], channel_multiplier=1))
            pool.sem_inc(s_fc, 1)

        @block.vector
        def _(dve):
            dve_steps.on(dve)
            dve.wait_ge(s_fin, 48)
            dve_steps(dve.tensor_tensor(f_log[:, :, :], f_log[:, :, :], f_bias[:, :].unsqueeze(1).to_broadcast([P, TT, FH]),
                                        ALU.add))
            dve_steps(dve.tensor_scalar(f_abs[:, :, :], f_log[:, :, :], -1.0, None, ALU.mult))
            dve_steps(dve.tensor_tensor(f_abs[:, :, :], f_abs[:, :, :], f_log[:, :, :], ALU.max))
            dve.sem_inc(s_fe, 1)
            dve_steps(dve.tensor_scalar(f_log[:, :, :], f_log[:, :, :], 0.0, None, ALU.min))
            dve.wait_ge(s_fe, 2)
            dve_steps(dve.tensor_scalar(f_abs[:, :, :], f_abs[:, :, :], 1.0, None, ALU.add))
            dve.sem_inc(s_fe, 1)
            dve.wait_ge(s_fe, 4)
            dve_steps(dve.tensor_tensor(f_log[:, :, :], f_log[:, :, :], f_abs[:, :, :], ALU.subtract))
            dve.sem_inc(s_fl, 1)
            dve.wait_ge(s_fcum, 1)
            dve.tensor_scalar(neg_cum[:, :, :], ps[:, 0, 0:TT * FH].rearrange("p (m h) -> p m h", h=FH), -1.0, None,
                              ALU.mult).then_inc(s_fn, 1)
            for n in range(2):
                dve.wait_ge(s_fs, n + 1)
                dve.tensor_reduce(frn[:, n, :, :], fsq[:, :, :].rearrange("p m (h d) -> p m h d", d=FHD), AX.X,
                                  ALU.add).then_inc(s_fr, 1)
            dve.wait_ge(s_fr, 2)
            dve_steps(dve.tensor_scalar(frn[:, :, :, :], frn[:, :, :, :], 1.0 / FHD, EPS, ALU.mult, ALU.add))
            dve.sem_inc(s_fr, 1)
            inverse_root(dve, frn[:, :, :, :], frt[:, :, :, :], frtmp[:, :, :, :], (s_frt, 1))

        @block.scalar
        def _(act):
            act.wait_ge(s_fe, 1)
            act.activation(f_abs[:, :, :], f_abs[:, :, :], ACT.Exp, scale=-1.0).then_inc(s_fe, 1)
            act.wait_ge(s_fe, 3)
            act.activation(f_abs[:, :, :], f_abs[:, :, :], ACT.Ln).then_inc(s_fe, 1)
            act.activation(fsq[:, :, :], qkv[:, :, 0:D], ACT.Square).then_inc(s_fs, 1)
            act.wait_ge(s_ft, 1)
            act.activation(cumT[:, :], ps[0:FH, 1, :], ACT.Copy).then_inc(s_fte, 1)
            for hd in range(FH):
                act.wait_ge(s_fb, hd + 1)
                act.activation(bias_f[:, hd, :], ps[:, 2 + hd % 2, :], ACT.Copy).then_inc(s_fbe, 1)
            act.wait_ge(s_fr, 1)
            act.activation(fsq[:, :, :], qkv[:, :, D:2 * D], ACT.Square).then_inc(s_fs, 1)
            act.wait_ge(s_fr, 3)
            act.activation(frt[:, :, :, :], frn[:, :, :, :], ACT.Sqrt).then_inc(s_frt, 1)

        @block.tensor
        def _(pe):
            pe.wait_ge(s_fl, 1)
            for m in range(TT):
                for n in range(m + 1):
                    mm = pe.matmul(ps[:, 0, m * FH:(m + 1) * FH], (tri_upto if n == m else ones)[:, :], f_log[:, n, :],
                                   start=(n == 0), stop=(n == m))
            mm.then_inc(s_fcum, 1)
            pe.wait_ge(s_fn, 1)
            for m in range(TT):
                tr = pe.transpose(ps[0:FH, 1, m * P:(m + 1) * P], neg_cum[:, m, :], ident[:, :])
            tr.then_inc(s_ft, 1)
            pe.wait_ge(s_fte, 1)
            pe.wait_ge(s_fc, 1)
            for hd in range(FH):
                if hd >= 2:
                    pe.wait_ge(s_fbe, hd - 1)
                pe.matmul(ps[:, 2 + hd % 2, :], head_row[:, hd, :], cumT[:, :], start=True, stop=True).then_inc(s_fb, 1)
    prep.close()

    stage = ExitStack()
    fqn, fkn = sb(stage, "fqn", [P, TT, FHD]), sb(stage, "fkn", [P, TT, FHD])
    tens = dict(qn=fqn, kn=fkn, turn_src=(fqn, fkn), qT=sb(stage, "fqT", [FHD, SEQ]),
                kT=sb(stage, "fkT", [FHD, SEQ]), S=sb(stage, "fS", [P, TT, SEQ]), Pm=sb(stage, "fPm", [P, TT, SEQ]),
                PT=sb(stage, "fPT", [P, 2, TT, P]), nmax=sb(stage, "fnmax", [P, TT]), den=sb(stage, "fden", [P, TT]),
                steps=2 * TT + 2)

    def load_fox(pool, i, qn, kn):
        for n, dst in enumerate((qn, kn)):
            pool_steps(pool.tensor_tensor(dst[:, :, :], qkv[:, :, ds(i * FHD + n * D, FHD)],
                                        frn[:, n, :, ds(i, 1)].to_broadcast([P, TT, FHD]), ALU.mult))
            pool_steps(pool.tensor_tensor(dst[:, :, :], dst[:, :, :],
                                        fgain[:, n, :].unsqueeze(1).to_broadcast([P, TT, FHD]), ALU.mult))

    with nc.Block() as block:
        attention(block, "forgetting", FH, FHD, FHD, FHD ** -0.5, load_fox,
                  lambda dve, i: lambda q: bias_f[:, ds(i, 1), 0:(q + 1) * P].rearrange("p a n -> p (a n)"), diag[:, :],
                  lambda i, b: qkv[:, b, ds(i * FHD + 2 * D, FHD)], lambda i: merged[:, :, ds(i * FHD, FHD)], tens)
    stage.close()
    fox.close()

    ssm = ExitStack()
    yT = sb(ssm, "yT", [P, TT, SEQ])
    stage = ExitStack()
    uT = sb(stage, "uT", [P, TT, SEQ])
    bw = sb(stage, "bw", [P, 4, 2, P])
    cw = sb(stage, "cw", [P, 4, 2, P])
    cw_raw = sb(stage, "cw_raw", [P, 4, 2, P])
    par = sb(stage, "par", [P, 24, ST])
    pw = sb(stage, "pw", [P, 9, 2, ST])
    rot = sb(stage, "rot", [P, 2, 2, 4, SEQ])
    ra, rb = sb(stage, "ra", [P, 4, SEQ // 2]), sb(stage, "rb", [P, 4, SEQ // 2])
    f1, f2 = sb(stage, "f1", [P, SEQ]), sb(stage, "f2", [P, SEQ])
    wre, wim = sb(stage, "wre", [P, SEQ]), sb(stage, "wim", [P, SEQ])
    zst = sb(stage, "zst", [P, 2, 2, SEQ])
    yq = sb(stage, "yq", [P, SEQ])
    d_col = sb(stage, "d_col", [P, TT])
    (A_RE, A_IM, LS, STEP, TH, MAG, KF, R, RH, SN, SH, CS, LRE, LIM, NR, DEN, CRE, CIM, T1, T2) = range(20)
    pc = [par[:, n, :] for n in range(20)]
    s_sin, s_a, s_d, s_pw, s_rot, s_rotu, s_u, s_ute, s_v, s_vu, s_z, s_zu, s_cw, s_yp, s_yq, s_yT = (
        sem(f"ssm_{x}") for x in ("params", "act", "dve", "powers", "rotations", "rot_used", "u_turned", "u_here", "inputs", "inputs_used",
                                  "states", "states_used", "c_here", "y", "y_here", "gelu"))
    s_bw, s_cr = sem("ssm_b_here"), sem("ssm_c_raw")
    with nc.Block() as block:
        @block.sync
        def _(sp):
            sp.dma_start(pc[A_RE], t["ssm_a_re_2"]).then_inc(s_sin, 16)
            sp.dma_start(pc[A_IM], t["ssm_a_im_2"]).then_inc(s_sin, 16)
            for g in range(2):
                sp.dma_start(par[64 * g:64 * g + 64, LS, :], t["ssm_log_step_2"][g:g + 1, :].rearrange("a c -> (a c)").partition_broadcast(64)).then_inc(s_sin, 16)
            sp.dma_start(d_col[:, :], t["ssm_d_2"]).then_inc(s_sin, 16)
            for q in range(TT):
                if q:
                    sp.wait_ge(s_vu, 4 * q)
                sp.dma_start(bw[:, :, :, :], t["ssm_b_2"][q]).then_inc(s_bw, 16)
                if q:
                    sp.wait_ge(s_cw, 4 * q)
                sp.dma_start(cw_raw[:, :, :, :], t["ssm_c_2"][q]).then_inc(s_cr, 16)

        @block.gpsimd
        def _(pool):
            pool_steps.on(pool)
            pool.wait_ge(s_pw, 1)
            for q in range(TT):
                b = q % 2
                if q >= 2:
                    pool.wait_ge(s_rotu, q - 1)
                re, im = rot[:, b, 0, :, :], rot[:, b, 1, :, :]
                pool_steps(pool.memset(re[:, :, 0:1], 1.0))
                pool_steps(pool.memset(im[:, :, 0:1], 0.0))
                for k in range(9):
                    n = 1 << k
                    lr, li = (pw[:, k, c, 4 * q:4 * q + 4].unsqueeze(2).to_broadcast([P, 4, n]) for c in range(2))
                    a, c = ra[:, :, 0:n], rb[:, :, 0:n]
                    pool_steps(pool.tensor_tensor(a, re[:, :, 0:n], lr, ALU.mult))
                    pool_steps(pool.tensor_tensor(c, im[:, :, 0:n], li, ALU.mult))
                    pool_steps(pool.tensor_tensor(re[:, :, n:2 * n], a, c, ALU.subtract))
                    pool_steps(pool.tensor_tensor(a, re[:, :, 0:n], li, ALU.mult))
                    pool_steps(pool.tensor_tensor(c, im[:, :, 0:n], lr, ALU.mult))
                    pool_steps(pool.tensor_tensor(im[:, :, n:2 * n], a, c, ALU.add))
                pool.sem_inc(s_rot, 1)

        @block.tensor
        def _(pe):
            turn(pe, lambda m, k: ug[:, m, k * P:(k + 1) * P], s_u, s_ute, kt=TT)
            pe.wait_ge(s_ute, TT)

            def y_out(q, j):
                pe.wait_ge(s_z, 4 * q + j + 1)
                for c in range(2):
                    mm = pe.matmul(ps[:, 4 + q % 2, :], cw[:, j, c, :], zst[:, j % 2, c, :], start=(j == 0 and c == 0),
                                   stop=(j == 3 and c == 1))
                mm.then_inc(s_yp, 1)

            for q in range(TT):
                pe.wait_ge(s_bw, 16 * (q + 1))
                for j in range(4):
                    n = 4 * q + j
                    if n >= 2:
                        pe.wait_ge(s_vu, n - 1)
                    for c in range(2):
                        mm = pe.matmul(ps[:, 2 * (j % 2) + c, :], bw[:, j, c, :], uT[:, q, :], start=True, stop=True)
                    mm.then_inc(s_v, 1)
                    if n:
                        y_out(*divmod(n - 1, 4))
            y_out(TT - 1, 3)

        @block.scalar
        def _(act):
            turned(act, lambda k: uT[:, k, :], s_u, s_ute, kt=TT)
            act.wait_ge(s_sin, 80)
            act.activation(pc[STEP], pc[LS], ACT.Exp).then_inc(s_a, 1)
            act.wait_ge(s_d, 1)
            act.activation(pc[MAG], pc[T1], ACT.Exp).then_inc(s_a, 1)
            act.wait_ge(s_d, 2)
            act.activation(pc[SN], pc[R], ACT.Sin).then_inc(s_a, 1)
            act.activation(pc[SH], pc[RH], ACT.Sin).then_inc(s_a, 1)
            for q in range(TT):
                act.wait_ge(s_yq, q + 1)
                act.activation(yT[:, q, :], yq[:, :], ACT.Gelu_apprx_tanh).then_inc(s_yT, 1)

        @block.vector
        def _(dve):
            st = dve_steps.on(dve)
            dve.wait_ge(s_a, 1)
            st(dve.tensor_tensor(pc[T1], pc[A_RE], pc[STEP], ALU.mult))
            dve.sem_inc(s_d, 1)
            st(dve.tensor_tensor(pc[TH], pc[A_IM], pc[STEP], ALU.mult))
            magic, high = 1.5 * 2.0 ** 23, 6.28125
            st(dve.tensor_scalar(pc[KF], pc[TH], 1.0 / (2.0 * math.pi), magic, ALU.mult, ALU.add))
            st(dve.tensor_scalar(pc[KF], pc[KF], -magic, None, ALU.add))
            st(dve.scalar_tensor_tensor(out=pc[R], in0=pc[KF], scalar=-high, in1=pc[TH], op0=ALU.mult, op1=ALU.add))
            st(dve.scalar_tensor_tensor(out=pc[R], in0=pc[KF], scalar=-(2.0 * math.pi - high), in1=pc[R], op0=ALU.mult,
                                        op1=ALU.add))
            st(dve.tensor_scalar(pc[R], pc[R], 3.1415925, -3.1415925, ALU.min, ALU.max))
            st(dve.tensor_scalar(pc[RH], pc[R], 0.5, None, ALU.mult))
            dve.sem_inc(s_d, 1)
            dve.wait_ge(s_a, 4)
            st(dve.tensor_tensor(pc[T1], pc[SH], pc[SH], ALU.mult))
            st(dve.tensor_scalar(pc[CS], pc[T1], -2.0, 1.0, ALU.mult, ALU.add))
            st(dve.tensor_copy(pw[:, 0, 0, :], pc[CS]))
            st(dve.tensor_copy(pw[:, 0, 1, :], pc[SN]))
            for k in range(8):
                re, im = pw[:, k, 0, :], pw[:, k, 1, :]
                st(dve.tensor_tensor(pc[T1], re, re, ALU.mult))
                st(dve.tensor_tensor(pc[T2], im, im, ALU.mult))
                st(dve.tensor_tensor(pw[:, k + 1, 0, :], pc[T1], pc[T2], ALU.subtract))
                st(dve.scalar_tensor_tensor(out=pw[:, k + 1, 1, :], in0=re, scalar=2.0, in1=im, op0=ALU.mult, op1=ALU.mult))
            dve.sem_inc(s_pw, 1)
            st(dve.tensor_tensor(pc[LRE], pc[MAG], pc[CS], ALU.mult))
            st(dve.tensor_tensor(pc[LIM], pc[MAG], pc[SN], ALU.mult))
            st(dve.tensor_scalar(pc[NR], pc[LRE], -1.0, None, ALU.add))
            st(dve.tensor_tensor(pc[T1], pc[A_RE], pc[A_RE], ALU.mult))
            st(dve.tensor_tensor(pc[T2], pc[A_IM], pc[A_IM], ALU.mult))
            st(dve.tensor_tensor(pc[DEN], pc[T1], pc[T2], ALU.add))
            st(dve.reciprocal(pc[DEN], pc[DEN]))
            for dst, x1, x2, op in ((CRE, A_RE, A_IM, ALU.add), (CIM, A_IM, A_RE, ALU.subtract)):
                first, other = ((NR, A_RE), (LIM, A_IM)) if dst == CRE else ((LIM, A_RE), (NR, A_IM))
                st(dve.tensor_tensor(pc[T1], pc[first[0]], pc[first[1]], ALU.mult))
                st(dve.tensor_tensor(pc[T2], pc[other[0]], pc[other[1]], ALU.mult))
                st(dve.tensor_tensor(pc[T1], pc[T1], pc[T2], op))
                st(dve.tensor_tensor(pc[dst], pc[T1], pc[DEN], ALU.mult))
            for q in range(TT):
                dve.wait_ge(s_rot, q + 1)
                dve.wait_ge(s_cr, 16 * (q + 1))
                for j in range(4):
                    n = 4 * q + j
                    er, ei = rot[:, q % 2, 0, j, :], rot[:, q % 2, 1, j, :]
                    if q:
                        dve.wait_ge(s_yp, 4 * (q - 1) + j + 1)
                    cre, cim, tmp2 = cw_raw[:, j, 0, :], cw_raw[:, j, 1, :], f1[:, 0:P]
                    st(dve.tensor_scalar(tmp2, cim, pc[CIM][:, n:n + 1], None, ALU.mult))
                    st(dve.scalar_tensor_tensor(out=cw[:, j, 0, :], in0=cre, scalar=pc[CRE][:, n:n + 1], in1=tmp2,
                                                op0=ALU.mult, op1=ALU.subtract))
                    st(dve.tensor_scalar(tmp2, cim, pc[CRE][:, n:n + 1], -1.0, ALU.mult, ALU.mult))
                    st(dve.tensor_scalar(f2[:, 0:P], cre, pc[CIM][:, n:n + 1], None, ALU.mult))
                    st(dve.tensor_tensor(cw[:, j, 1, :], tmp2, f2[:, 0:P], ALU.subtract))
                    dve.sem_inc(s_cw, 1)
                    dve.wait_ge(s_v, n + 1)
                    vr, vi = ps[:, 2 * (j % 2), :], ps[:, 2 * (j % 2) + 1, :]
                    st(dve.tensor_tensor(f1[:, :], er, vr, ALU.mult))
                    st(dve.tensor_tensor(f2[:, :], ei, vi, ALU.mult))
                    st(dve.tensor_tensor(wre[:, :], f1[:, :], f2[:, :], ALU.add))
                    st(dve.tensor_tensor(f1[:, :], er, vi, ALU.mult))
                    st(dve.tensor_tensor(f2[:, :], ei, vr, ALU.mult))
                    dve.sem_inc(s_vu, 1)
                    st(dve.tensor_tensor(wim[:, :], f1[:, :], f2[:, :], ALU.subtract))
                    mag = pc[MAG][:, n:n + 1].to_broadcast([P, SEQ])
                    st(dve.tensor_tensor_scan(f1[:, :], mag, wre[:, :], 0.0, ALU.mult, ALU.add))
                    st(dve.tensor_tensor_scan(f2[:, :], mag, wim[:, :], 0.0, ALU.mult, ALU.add))
                    if n >= 2:
                        dve.wait_ge(s_yp, n - 1)
                    st(dve.tensor_tensor(wre[:, :], er, f1[:, :], ALU.mult))
                    st(dve.tensor_tensor(wim[:, :], ei, f2[:, :], ALU.mult))
                    st(dve.tensor_tensor(zst[:, j % 2, 0, :], wre[:, :], wim[:, :], ALU.subtract))
                    st(dve.tensor_tensor(wre[:, :], er, f2[:, :], ALU.mult))
                    st(dve.tensor_tensor(wim[:, :], ei, f1[:, :], ALU.mult))
                    st(dve.tensor_tensor(zst[:, j % 2, 1, :], wre[:, :], wim[:, :], ALU.add))
                    dve.sem_inc(s_z, 1)
                dve.sem_inc(s_rotu, 1)
                dve.wait_ge(s_yp, 4 * q + 4)
                if q:
                    dve.wait_ge(s_yT, q)
                st(dve.scalar_tensor_tensor(out=yq[:, :], in0=uT[:, q, :], scalar=d_col[:, q:q + 1], in1=ps[:, 4 + q % 2, :],
                                            op0=ALU.mult, op1=ALU.add))
                dve.sem_inc(s_yq, 1)
    stage.close()

    stage = ExitStack()
    wglu_t = sb(stage, "wglu", [P, 2, TT * CH])
    wglu = [wglu_t[:, s, :] for s in range(2)]
    zz = sb(stage, "zz", [P, 2, TT, D])
    s_ldg, s_mmg, s_bg2, s_sg2, s_mg = [sem("glu_ld0"), sem("glu_ld1")], sem("glu_mm"), sem("glu_bank"), sem("branch_gates"), sem("merge")
    with nc.Block() as block:
        @block.sync
        def _(sp):
            loads(sp, 2, lambda n: t["ssm_w_glu_2"][n, :, :], wglu, s_ldg, s_mmg)

        @block.tensor
        def _(pe):
            products(pe, 2, lambda s, k, m: yT[:, k, m * P:(m + 1) * P], lambda s, k, m, w: wglu[s][:, k * w:(k + 1) * w],
                     s_ldg, s_mmg, s_bg2, kt=TT)

        @block.scalar
        def _(act):
            for m in range(TT):
                act.activation(ug[:, m, CH:5 * CH], ug[:, m, CH:5 * CH], ACT.Sigmoid).then_inc(s_sg2, 1)
            evacuate(act, 2, s_mmg, s_bg2, lambda i, s, m, bank: act.activation(
                zz[:, s, m, ds(i * CH, CH)], bank, (ACT.Identity, ACT.Sigmoid)[s]))
            act.sem_inc(s_mg, 1)

        @block.vector
        def _(dve):
            dve_steps.on(dve)
            dve.wait_ge(s_sg2, TT)
            for m in range(TT):
                dve_steps(dve.tensor_tensor(merged[:, m, :], merged[:, m, :], ug[:, m, CH + D:CH + 2 * D], ALU.mult))
            dve.wait_ge(s_mg, 1)
            for m in range(TT):
                dve_steps(dve.tensor_tensor(zz[:, 0, m, :], zz[:, 0, m, :], zz[:, 1, m, :], ALU.mult))
                dve_steps(dve.tensor_tensor(zz[:, 0, m, :], zz[:, 0, m, :], ug[:, m, CH:CH + D], ALU.mult))
                dve_steps(dve.tensor_tensor(merged[:, m, :], merged[:, m, :], zz[:, 0, m, :], ALU.add))
    stage.close()
    ssm.close()

    mT = ExitStack()
    mixT = sb(mT, "mixT", [P, KT, SEQ])
    out_projection("mix2", merged, t["w_out_2"], mixT, None)
    mT.close()
    second.close()
    clear_semaphores()

    peer = ExitStack()
    h4T = [sb(peer, f"h4T_{x}", [P, KT, SEQ], F32R) for x in ("high", "low")]
    selT = sb(peer, "selT", [P, 3, SEQ])
    g_rows = nc.dram_tensor("g_rows", [P // GROUP, P, GROUP * SEQ], F32, kind="Internal").ap()
    route = ExitStack()
    qT4 = sb(route, "qT4", [P, 2 * PH, SEQ])
    stage = ExitStack()
    h4T_full = sb(stage, "h4T_full", [P, KT, SEQ])
    gain4 = sb(stage, "gain4", [P, D])
    h4 = sb(stage, "h4", [P, TT, D])
    wbuf_t = sb(stage, "wbuf_q", [P, 2, KT * CH])
    wbuf = [wbuf_t[:, s, :] for s in range(2)]
    with nc.Block() as block:
        norm_block(block, gain4, t["ffn_norm_g_2"], None, None, (),
                   tuple(sem(f"norm4_{x}") for x in ("sums", "mean", "root", "gain", "h", "turned", "taken")), h4, h4T_full)
    s_ldq, s_mmq, s_bankq = [sem("query_ld0"), sem("query_ld1")], sem("query_mm"), sem("query_bank")
    s_h4hi, s_h4lo = sem("h4_high"), sem("h4_low")
    with nc.Block() as block:
        @block.sync
        def _(sp):
            loads(sp, 2, lambda n: t["peer_w_query_2"][n, :, :], wbuf, s_ldq, s_mmq)

        @block.tensor
        def _(pe):
            products(pe, 2, lambda s, k, m: wbuf[s][:, k * CH + m * P:k * CH + (m + 1) * P],
                     lambda s, k, m, w: h4T_full[:, k, :], s_ldq, s_mmq, s_bankq)

        @block.vector
        def _(dve):
            dve.wait_ge(s_h4hi, 1)
            dve.tensor_tensor(h4T[1][:, :, :], h4T_full[:, :, :], h4T[0][:, :, :].bitcast(F32), ALU.subtract)\
               .then_inc(s_h4lo, 1)
            dve.wait_ge(s_h4lo, 1)

        @block.scalar
        def _(act):
            act.activation(h4T[0][:, :, :], h4T_full[:, :, :], ACT.Copy).then_inc(s_h4hi, 1)
            evacuate(act, 2, s_mmq, s_bankq, lambda i, s, m, bank: act.activation(
                qT4[:, ds(i * 8 + (s * 4 + m), 1), :].rearrange("p a n -> p (a n)"), bank, ACT.Copy))
    stage.close()

    stage = ExitStack()
    keysT = sb(stage, "keysT", [P, 2 * PH, PK])
    rest = sb(stage, "rest", [P, 2 * P])
    top_s = sb(stage, "top_s", [P, 2 * PH, PT16])
    top_k = sb(stage, "top_k", [P, 2 * PH, PT16], U32)
    top_kf = sb(stage, "top_kf", [P, 2 * PH, PT16])
    pairs_s = sb(stage, "pairs_s", [P, PT16, PT16])
    best_s = sb(stage, "best_s", [P, PH, PT16])
    best_p = sb(stage, "best_p", [P, PH, PT16], U32)
    part_p = sb(stage, "part_p", [P, PH, PT16], U32)
    part_f = sb(stage, "part_f", [P, PH, PT16])
    match = sb(stage, "match", [P, PH, PT16, PT16])
    sel = sb(stage, "sel", [P, 3, PH, PT16])
    psum_g = sb(stage, "psum_g", [P, PH])
    s_key, s_scr, s_ex, s_exd, s_sel, s_selt, s_selh = (
        sem(f"peer_{x}") for x in ("keys", "scores", "shifted", "exp", "selected", "sel_turned", "sel_here"))
    with nc.Block() as block:
        @block.sync
        def _(sp):
            sp.dma_start(keysT[:, :, :], t["sub_keys_2"]).then_inc(s_key, 16)

        @block.scalar
        def _(act):
            for i in range(TT):
                act.wait_ge(s_ex, i + 1)
                act.activation(sel[:, 2, :, :], best_s[:, :, :], ACT.Exp).then_inc(s_exd, 1)
                act.wait_ge(s_selt, i + 1)
                act.activation(selT[:, :, ds(i * P, P)], ps[:, 4, 0:3 * P].rearrange("p (c n) -> p c n", c=3),
                               ACT.Copy).then_inc(s_selh, 1)
            act.wait_ge(s_selh, TT)

        @block.tensor
        def _(pe):
            pe.wait_ge(s_key, 16)
            for i in range(TT):
                if i:
                    pe.wait_ge(s_sel, i)
                for b in range(4):
                    for n in range(4):
                        mm = pe.matmul(ps[:, b, n * P:(n + 1) * P], qT4[:, 4 * b + n, i * P:(i + 1) * P], keysT[:, 4 * b + n, :],
                                       start=True, stop=True)
                    mm.then_inc(s_scr, 1)
                pe.wait_ge(s_sel, i + 1)
                for c in range(3):
                    tr = pe.transpose(ps[:, 4, c * P:(c + 1) * P], sel[:, c, :, :].rearrange("p h k -> p (h k)"), ident[:, :])
                tr.then_inc(s_selt, 1)

        @block.vector
        def _(dve):
            st = dve_steps.on(dve)

            def best16(values, scores, places, width):
                st(dve.max(scores[:, 0:8], values))
                st(dve.max_index(places[:, 0:8], scores[:, 0:8], values))
                st(dve.match_replace(rest[:, 0:width], scores[:, 0:8], values, -3.0e38))
                st(dve.max(scores[:, 8:16], rest[:, 0:width]))
                st(dve.max_index(places[:, 8:16], scores[:, 8:16], rest[:, 0:width]))

            for i in range(TT):
                for n in range(2 * PH):
                    if n % 4 == 0:
                        dve.wait_ge(s_scr, i * 4 + n // 4 + 1)
                    best16(ps[:, n // 4, (n % 4) * P:(n % 4 + 1) * P], top_s[:, n, :], top_k[:, n, :], P)
                for hd in range(PH):
                    st(dve.tensor_tensor(pairs_s[:, :, :], top_s[:, 2 * hd, :].unsqueeze(2).to_broadcast([P, PT16, PT16]),
                                         top_s[:, 2 * hd + 1, :].unsqueeze(1).to_broadcast([P, PT16, PT16]), ALU.add))
                    best16(pairs_s[:, :, :].rearrange("p a b -> p (a b)"), best_s[:, hd, :], best_p[:, hd, :], PT16 * PT16)
                st(dve.tensor_copy(psum_g[:, :], best_s[:, :, 0]))
                st(dve.tensor_tensor(best_s[:, :, :], best_s[:, :, :], psum_g[:, :].unsqueeze(2).to_broadcast([P, PH, PT16]),
                                     ALU.subtract))
                dve.sem_inc(s_ex, 1)
                st(dve.tensor_copy(top_kf[:, :, :], top_k[:, :, :]))
                halves_of = top_kf[:, :, :].rearrange("p (h c) k -> p h c k", c=2)
                for c in range(2):
                    st(dve.tensor_scalar(part_p[:, :, :], best_p[:, :, :], (4, 15)[c], None,
                                         (ALU.logical_shift_right, ALU.bitwise_and)[c]))
                    st(dve.tensor_copy(part_f[:, :, :], part_p[:, :, :]))
                    st(dve.tensor_tensor(match[:, :, :, :], part_f[:, :, :].unsqueeze(3).to_broadcast([P, PH, PT16, PT16]),
                                         iota_row[:, 0:PT16].unsqueeze(1).unsqueeze(1).to_broadcast([P, PH, PT16, PT16]),
                                         ALU.is_equal))
                    st(dve.tensor_tensor(match[:, :, :, :], match[:, :, :, :],
                                         halves_of[:, :, c, :].unsqueeze(2).to_broadcast([P, PH, PT16, PT16]), ALU.mult))
                    st(dve.tensor_reduce(sel[:, c, :, :], match[:, :, :, :], AX.X, ALU.add))
                dve.wait_ge(s_exd, i + 1)
                st(dve.tensor_reduce(psum_g[:, :], sel[:, 2, :, :], AX.X, ALU.add))
                st(dve.reciprocal(psum_g[:, :], psum_g[:, :]))
                dve.tensor_tensor(sel[:, 2, :, :], sel[:, 2, :, :], psum_g[:, :].unsqueeze(2).to_broadcast([P, PH, PT16]),
                                  ALU.mult).then_inc(s_sel, 1)
                dve.wait_ge(s_selh, i + 1)
    stage.close()
    route.close()

    stage = ExitStack()
    first_hot = sb(stage, "first_hot", [P, 2, 4, P])
    second_hot = sb(stage, "second_hot", [P, 2, 4, P])
    spread = sb(stage, "spread", [P, 2, PK, P])
    s_gated = sem("gated_one_hots")
    s_hot, s_gb, s_gt2, s_gst = sem("one_hots"), sem("gate_products"), sem("gates_spread"), [sem("gates_stored0"), sem("gates_stored1")]
    PAIRS = P // 8
    with nc.Block() as block:
        def of_tokens(c, i, m, s):
            return selT[:, c, ds(i * 8 + (m * P + 4 * s), 4)].unsqueeze(2).to_broadcast([P, 4, P])

        @block.vector
        def _(dve):
            dve.sem_inc(s_gb, 2)
            keys = iota_row[:, :].unsqueeze(1).to_broadcast([P, 4, P])
            for m in range(TT):
                with dve.Fori(0, PAIRS) as i:
                    for s in range(2):
                        dve.wait_ge(s_gb, i * 2 + (m * PAIRS * 2 + s + 1))
                        for c, dst in enumerate((first_hot, second_hot)):
                            dve.tensor_tensor(dst[:, s, :, :], keys, of_tokens(c, i, m, s), ALU.is_equal).then_inc(s_hot, 1)

        @block.gpsimd
        def _(pool):
            for m in range(TT):
                with pool.Fori(0, PAIRS) as i:
                    for s in range(2):
                        pool.wait_ge(s_hot, i * 4 + (m * PAIRS * 4 + 2 * s + 1))
                        pool.tensor_tensor(first_hot[:, s, :, :], first_hot[:, s, :, :], of_tokens(2, i, m, s),
                                           ALU.mult).then_inc(s_gated, 1)

        @block.tensor
        def _(pe):
            for m in range(TT):
                with pe.Fori(0, PAIRS) as i:
                    for s in range(2):
                        pe.wait_ge(s_gated, i * 2 + (m * PAIRS * 2 + s + 1))
                        pe.wait_ge(s_hot, i * 4 + (m * PAIRS * 4 + 2 * s + 2))
                        pe.wait_ge(s_gt2, i * 2 + (m * PAIRS * 2 + s + 1))
                        for r in range(4):
                            mm = pe.matmul(ps[:, s, r * P:(r + 1) * P], first_hot[:, s, r, :], second_hot[:, s, r, :],
                                           start=True, stop=True)
                        mm.then_inc(s_gb, 1)

        @block.scalar
        def _(act):
            act.sem_inc(s_gt2, 2)
            for m in range(TT):
                if m >= 2:
                    act.wait_ge(s_gst[m % 2], 16 * GROUP)
                with act.Fori(0, PAIRS) as i:
                    for s in range(2):
                        act.wait_ge(s_gb, i * 2 + (m * PAIRS * 2 + s + 3))
                        act.activation(spread[:, m % 2, :, ds(i * 8 + 4 * s, 4)].rearrange("p k n -> p n k"),
                                       ps[:, s, :].rearrange("p (n k) -> p n k", n=4), ACT.Copy).then_inc(s_gt2, 1)

        @block.sync
        def _(sp):
            for m in range(TT):
                sp.wait_ge(s_gt2, 2 + (m + 1) * PAIRS * 2)
                for j in range(GROUP):
                    sp.dma_start(g_rows.rearrange("g p (j n) -> p g j n", j=GROUP)[:, :, j, m * P:(m + 1) * P],
                                 spread[:, m % 2, :, :].rearrange("p (g j) n -> p g j n", j=GROUP)[:, :, j, :])\
                      .then_inc(s_gst[m % 2], 16)
            for s in range(2):
                sp.wait_ge(s_gst[s], 2 * 16 * GROUP)
    stage.close()

    NG = P // GROUP
    stage = ExitStack()
    u_raw = sb(stage, "u_raw", [P, 2, GROUP * D])
    v_raw = sb(stage, "v_raw", [P, 2, GROUP * D])
    u_hi, u_lo = (sb(stage, f"u_{x}", [P, 2, GROUP * D], F32R) for x in ("hi", "lo"))
    v_hi, v_lo = (sb(stage, f"v_{x}", [P, 2, GROUP * D], F32R) for x in ("hi", "lo"))
    g_sb = sb(stage, "g_sb", [P, 2, GROUP * SEQ])
    gl = sb(stage, "gl", [P, GROUP, SEQ])
    wf = sb(stage, "wf", [P, GROUP, SEQ])
    w_hi, w_lo = (sb(stage, f"w_{x}", [P, 2, GROUP, SEQ], F32R) for x in ("hi", "lo"))
    s_lu, s_lv, s_lg2 = ([sem(f"peer_{x}{s}") for s in range(2)] for x in ("u", "v", "g"))
    s_uh, s_ul, s_vh, s_vl, s_pa, s_gelu, s_wf, s_wh, s_wl2, s_po, s_add, s_outd = (
        sem(f"peer_{x}") for x in ("u_high", "u_low", "v_high", "v_low", "dots", "gelu", "weights", "weights_high",
                                   "weights_low", "outputs", "added", "stored"))
    G2 = GROUP
    with nc.Block() as block:
        @block.sync
        def _(sp):
            def load(n, s, later):
                if later:
                    sp.wait_ge(s_ul, n - 1)
                sp.dma_start(u_raw[:, s, :], t["peer_u_2"][n, :, :]).then_inc(s_lu[s], 16)
                if later:
                    sp.wait_ge(s_wf, n * G2)
                sp.dma_start(g_sb[:, s, :], g_rows[n, :, :]).then_inc(s_lg2[s], 16)
                if later:
                    sp.wait_ge(s_vl, n - 1)
                sp.dma_start(v_raw[:, s, :], t["peer_v_2"][:, n, :]).then_inc(s_lv[s], 16)
            for s in range(2):
                load(s, s, False)
            with sp.Fori(1, NG // 2) as i:
                for s in range(2):
                    load(i * 2 + s, s, True)
            sp.wait_ge(s_add, 4 + 8 * NG)
            sp.dma_start(out.rearrange("a (m p) d -> p (a m) d", p=P), x_sb[:, :, :]).then_inc(s_outd, 16)
            sp.wait_ge(s_outd, 16)

        def steps(eng, first_step, step, last_step):
            first_step()
            with eng.Fori(0, NG // 2 - 1) as i:
                step(i, 1)
                step(i, 2)
            last_step()

        @block.tensor
        def _(pe):
            def dots(i, s):
                pe.wait_ge(s_ul, i * 2 + (s + 1))
                for j in range(GROUP):
                    pe.wait_ge(s_gelu, i * 2 * G2 + (s * G2 + j + 1))
                    for k in range(KT):
                        at = (j * KT + k) * P
                        hi, lo = u_hi[:, s % 2, at:at + P], u_lo[:, s % 2, at:at + P]
                        mm = three(pe, ps[:, j % 2, :], hi, lo, h4T[0][:, k, :], h4T[1][:, k, :], k == 0, k == KT - 1)
                    mm.then_inc(s_pa, 1)

            def outputs(i, s):
                pe.wait_ge(s_vl, i * 2 + (s + 1))
                pe.wait_ge(s_wl2, i * 2 * G2 + (s * G2 + 2 * G2))
                for n in range(8):
                    m, c = divmod(n, 2)
                    pe.wait_ge(s_add, i * 16 + (s * 8 + n + 1))
                    for j in range(GROUP):
                        at = j * D + c * CH
                        mm = three(pe, ps[:, 2 + n % 4, :], w_hi[:, s % 2, j, m * P:(m + 1) * P], w_lo[:, s % 2, j, m * P:(m + 1) * P],
                                   v_hi[:, s % 2, at:at + CH], v_lo[:, s % 2, at:at + CH], j == 0, j == GROUP - 1)
                    mm.then_inc(s_po, 1)

            def step(i, s):
                dots(i, s)
                outputs(i, s - 1)

            def last():
                step(NG // 2 - 1, 1)
                outputs(NG // 2 - 1, 1)

            steps(pe, lambda: dots(0, 0), step, last)

        @block.scalar
        def _(act):
            def high_u(i, s):
                act.wait_ge(s_lu[s % 2], (i + (s // 2 + 1)) * 16)
                if not (isinstance(i, int) and i * 2 + s < 2):
                    act.wait_ge(s_pa, i * 2 * G2 + (s - 1) * G2)
                act.activation(u_hi[:, s % 2, :], u_raw[:, s % 2, :], ACT.Copy).then_inc(s_uh, 1)

            def step(i, s, more=True):
                if more:
                    high_u(i, s + 1)
                act.wait_ge(s_lv[s % 2], (i + (s // 2 + 1)) * 16)
                if not (isinstance(i, int) and i * 2 + s < 2):
                    act.wait_ge(s_po, i * 16 + (s - 1) * 8)
                act.activation(v_hi[:, s % 2, :], v_raw[:, s % 2, :], ACT.Copy).then_inc(s_vh, 1)
                for j in range(GROUP):
                    act.wait_ge(s_pa, i * 2 * G2 + (s * G2 + j + 1))
                    act.wait_ge(s_wf, i * 2 * G2 + (s * G2 + j + 1))
                    act.activation(gl[:, j, :], ps[:, j % 2, :], ACT.Gelu_apprx_tanh).then_inc(s_gelu, 1)
                for j in range(GROUP):
                    act.wait_ge(s_wf, i * 2 * G2 + (s * G2 + G2 + j + 1))
                    act.activation(w_hi[:, s % 2, j, :], wf[:, j, :], ACT.Copy).then_inc(s_wh, 1)

            act.sem_inc(s_gelu, 2)
            high_u(0, 0)
            steps(act, lambda: step(0, 0), step, lambda: step(NG // 2 - 1, 1, False))

        @block.vector
        def _(dve):
            def low_u(i, s):
                dve.wait_ge(s_uh, i * 2 + (s + 1))
                dve.tensor_tensor(u_lo[:, s % 2, :], u_raw[:, s % 2, :], u_hi[:, s % 2, :].bitcast(F32),
                                  ALU.subtract).then_inc(s_ul, 1)

            def low_v(i, s):
                dve.wait_ge(s_vh, i * 2 + (s + 1))
                dve.tensor_tensor(v_lo[:, s % 2, :], v_raw[:, s % 2, :], v_hi[:, s % 2, :].bitcast(F32),
                                  ALU.subtract).then_inc(s_vl, 1)

            def weights(i, s):
                dve.wait_ge(s_lg2[s % 2], (i + (s // 2 + 1)) * 16)
                for j in range(GROUP):
                    dve.wait_ge(s_gelu, i * 2 * G2 + (s * G2 + j + 3))
                    dve.wait_ge(s_wl2, i * 2 * G2 + (s * G2 + j + 1))
                    dve.tensor_tensor(wf[:, j, :], gl[:, j, :], g_sb[:, s % 2, j * SEQ:(j + 1) * SEQ],
                                      ALU.mult).then_inc(s_wf, 1)

            def low_weights(i, s):
                for j in range(GROUP):
                    dve.wait_ge(s_wh, i * 2 * G2 + (s * G2 + j + 1))
                    dve.tensor_tensor(w_lo[:, s % 2, j, :], wf[:, j, :], w_hi[:, s % 2, j, :].bitcast(F32),
                                      ALU.subtract).then_inc(s_wl2, 1)

            def add(i, s):
                for n in range(8):
                    m, c = divmod(n, 2)
                    dve.wait_ge(s_po, i * 16 + (s * 8 + n + 1))
                    xs = x_sb[:, m, c * CH:(c + 1) * CH]
                    dve.tensor_tensor(xs, ps[:, 2 + n % 4, :], xs, ALU.add).then_inc(s_add, 1)

            def step(i, s, more=True):
                if more:
                    low_u(i, s + 1)
                low_v(i, s)
                weights(i, s)
                low_weights(i, s)
                if not (isinstance(i, int) and i * 2 + s == 0):
                    add(i, s - 1)

            dve.sem_inc(s_wf, G2)
            dve.sem_inc(s_wl2, G2)
            dve.sem_inc(s_add, 4)
            low_u(0, 0)

            def last():
                step(NG // 2 - 1, 1, False)
                add(NG // 2 - 1, 1)
            steps(dve, lambda: step(0, 0), step, last)
    stage.close()
    peer.close()
    clear_semaphores()


def chunks(w, n=512):
    k, cols = w.shape[-2:]
    lead = w.shape[:-2]
    a = w.reshape(*lead, k // 128, 128, cols // n, n)
    nd = len(lead)
    a = a.transpose(*range(nd), nd + 2, nd + 1, nd, nd + 3)
    return np.ascontiguousarray(a.reshape(*lead, cols // n, 128, (k // 128) * n))

def state_tiles(b, stationary_in):
    parts, groups, states, width = b.shape
    per = 128 // states
    out = np.zeros((4, 4, parts, 128, 128), b.dtype)
    for g in range(groups):
        n, r = divmod(g, per)
        q, j = divmod(n, 4)
        f = (g * width) % 128
        for c in range(parts):
            out[q, j, c, f:f + width, r * states:(r + 1) * states] = b[c, g].T
    if stationary_in:
        return np.ascontiguousarray(out.transpose(0, 3, 1, 2, 4))
    return np.ascontiguousarray(out.transpose(0, 4, 1, 2, 3))

def lay_out(i):
    A = {}
    one = lambda n: np.ascontiguousarray(i[n][0])
    for n in ('b_ada','norm1_g','a_q_norm_g','a_k_norm_g','b_q_norm_g','b_k_norm_g','lambda_q1','lambda_k1','lambda_q2',
              'lambda_k2','diff_norm_g','norm2_g','b_router','b_gate_up','b_down','mix_norm_g_2','fox_forget_bias_2',
              'q_norm_g_2','k_norm_g_2','ffn_norm_g_2'):
        A[n] = one(n)
    A['x'] = i['x']
    A['c'] = np.ascontiguousarray(i['c'].reshape(8,128).T)
    for n in ('w_ada','w_in','w_out','w_gate_up','w_down','w_out_2','peer_w_query_2'):
        A[n] = chunks(i[n][0])
    A['w_router'] = chunks(i['w_router'][0], 32)[0]
    w = i['w_in_2'][0]
    A['w_qkv_2'] = chunks(w[:, 512:3584])
    A['w_f_2'] = chunks(w[:, 3584:3592], 8)[0]
    A['w_ug_2'] = chunks(np.concatenate([w[:, :512], w[:, 3592:]], 1))
    A['ssm_w_glu_2'] = np.ascontiguousarray(chunks(i['ssm_w_glu_2'][0])[[0, 2, 1, 3]])
    A['ssm_a_re_2'] = np.ascontiguousarray(i['ssm_a_re_2'][0].reshape(16,128).T)
    A['ssm_a_im_2'] = np.ascontiguousarray(i['ssm_a_im_2'][0].reshape(16,128).T)
    A['ssm_log_step_2'] = np.ascontiguousarray(i['ssm_log_step_2'][0].reshape(16,2).T)
    A['ssm_d_2'] = np.ascontiguousarray(i['ssm_d_2'][0].reshape(4,128).T)
    A['ssm_b_2'] = state_tiles(np.stack([i['ssm_b_re_2'][0], i['ssm_b_im_2'][0]]), True)
    A['ssm_c_2'] = state_tiles(np.stack([i['ssm_c_re_2'][0], i['ssm_c_im_2'][0]]).transpose(0,1,3,2), False)
    A['sub_keys_2'] = np.ascontiguousarray(i['peer_sub_keys_2'][0].reshape(16,128,128).transpose(2,0,1))
    u = i['peer_u_2'][0].reshape(128, 64, 2, 8, 128)
    A['peer_u_2'] = np.ascontiguousarray(u.transpose(1, 4, 2, 3, 0).reshape(64, 128, 2 * 8 * 128))
    A['peer_v_2'] = np.ascontiguousarray(i['peer_v_2'][0].reshape(128, 64, 2 * 1024))
    return A


def kernel(**inputs):
    import concourse.bacc as bacc
    from concourse.bass_utils import run_bass_kernel_spmd

    nc = bacc.Bacc("TRN2", target_bir_lowering=False, num_devices=1)
    arrays = {f"in_{name}": a for name, a in lay_out({k: np.asarray(v) for k, v in inputs.items()}).items()}
    t = {name[3:]: nc.dram_tensor(name, a.shape, mybir.dt.from_np(a.dtype), kind="ExternalInput").ap()
         for name, a in arrays.items()}
    out = nc.dram_tensor("out_0_dram", (1, SEQ, D), F32, kind="ExternalOutput").ap()
    build_program(nc, t, out)
    r = run_bass_kernel_spmd(nc, [arrays], core_ids=[0])
    return r.results[0]["out_0_dram"]
```
